# Optimizing a Trainium2 kernel written in Bass

```python
import math
import jax, jax.numpy as jnp
from jax import lax
import numpy as np

D_MODEL = 2048
BATCH = 1
SEQ = 256
DEPTH = 2

GRID_W = 64
D_MIX = D_MODEL
N_MIXERS = 4
D_GROUP = D_MIX // N_MIXERS
HEAD_DIM = 64
N_NA_HEADS = D_GROUP // HEAD_DIM
N_RET_HEADS = D_GROUP // HEAD_DIM
N_FFT_GROUPS = 4
FFT_GROUP_DIM = D_GROUP // N_FFT_GROUPS
NA_KH_MAX = 8
NA_KW = 16
RET_CHUNK = 128
CONV_WIDTH = 31
ROPE_BASE = 10000.0
EPS = 1e-6
N_IN_PIECES = 13
D_IN = N_IN_PIECES * D_GROUP


def _rmsnorm(x, g):
    xf = x.astype(jnp.float32)
    ms = jnp.mean(xf * xf, axis=-1, keepdims=True)
    return (xf * lax.rsqrt(ms + EPS)).astype(x.dtype) * g

def _fourier_mix(u, w_fft):
    B, S, _ = u.shape
    uf = u.astype(jnp.float32).reshape(B, S, N_FFT_GROUPS, FFT_GROUP_DIM)
    y = jnp.real(jnp.fft.fft2(uf, axes=(1, 3), norm="ortho"))
    return y.reshape(B, S, D_GROUP).astype(u.dtype) @ w_fft

def _neighbourhood_attention(q, k, v, rel_bias):
    B, S, _ = q.shape
    rows = S // GRID_W
    kh = min(NA_KH_MAX, rows)

    def grid(t):
        return t.reshape(B, rows, GRID_W, N_NA_HEADS, HEAD_DIM)

    qg = grid(q) * (HEAD_DIM ** -0.5)
    kg, vg = grid(k), grid(v)
    r = jnp.arange(rows)
    row_start = jnp.clip(r - kh // 2, 0, rows - kh)
    key_rows = row_start[:, None] + jnp.arange(kh)[None, :]
    kb = kg[:, key_rows]
    vb = vg[:, key_rows]
    col = jnp.arange(GRID_W)
    col_start = jnp.clip(col - NA_KW // 2, 0, GRID_W - NA_KW)
    rel_c = col[None, :] - col_start[:, None]
    col_in = (rel_c >= 0) & (rel_c < NA_KW)
    dc = col[None, :] - col[:, None]
    dr = key_rows - r[:, None]
    bias = rel_bias[:, (dr + NA_KH_MAX - 1)[:, :, None, None],
                    jnp.clip(dc + NA_KW - 1, 0, 2 * NA_KW - 2)[None, None]]
    bias = bias.transpose(0, 1, 3, 2, 4)
    s = jnp.einsum('brqhd,brakhd->bhrqak', qg, kb).astype(jnp.float32)
    s = s + bias[None].astype(jnp.float32)
    s = jnp.where(col_in[:, None, :], s, -jnp.inf)
    p = jax.nn.softmax(s.reshape(B, N_NA_HEADS, rows, GRID_W, kh * GRID_W), axis=-1)
    p = p.reshape(B, N_NA_HEADS, rows, GRID_W, kh, GRID_W).astype(v.dtype)
    o = jnp.einsum('bhrqak,brakhd->brqhd', p, vb)
    return o.reshape(B, S, D_GROUP)

def _rotary(t):
    S = t.shape[2]
    half = HEAD_DIM // 2
    inv = ROPE_BASE ** (-jnp.arange(half, dtype=jnp.float32) / half)
    ang = jnp.arange(S, dtype=jnp.float32)[:, None] * inv[None, :]
    cos, sin = jnp.cos(ang), jnp.sin(ang)
    t1, t2 = t[..., :half], t[..., half:]
    return jnp.concatenate([t1 * cos - t2 * sin, t1 * sin + t2 * cos], axis=-1)

def _retention_direction(q, k, v, log_gamma, include_diag):
    B, H, S, Dh = q.shape
    C = RET_CHUNK
    n = S // C
    qc = q.reshape(B, H, n, C, Dh)
    kc = k.reshape(B, H, n, C, Dh)
    vc = v.reshape(B, H, n, C, Dh)
    idx = jnp.arange(C, dtype=jnp.float32)
    diff = idx[:, None] - idx[None, :]
    mask = (diff >= 0) if include_diag else (diff > 0)
    lg = log_gamma[:, None, None]
    d_intra = jnp.where(mask, jnp.exp(lg * jnp.where(mask, diff, 0.0)), 0.0)
    scores = jnp.einsum('bhnid,bhnjd->bhnij', qc, kc) * d_intra[None, :, None]
    o_intra = jnp.einsum('bhnij,bhnjd->bhnid', scores, vc)
    k_decay = jnp.exp(log_gamma[:, None] * (C - 1 - idx)[None, :])
    kv = jnp.einsum('bhnjd,bhnje->nbhde', kc * k_decay[None, :, None, :, None], vc)
    chunk_decay = jnp.exp(log_gamma * C)[None, :, None, None]

    def step(state, kv_n):
        return chunk_decay * state + kv_n, state

    _, prev = lax.scan(step, jnp.zeros((B, H, Dh, Dh), jnp.float32), kv)
    q_decay = jnp.exp(log_gamma[:, None] * (idx + 1.0)[None, :])
    o_cross = jnp.einsum('bhnid,nbhde->bhnie', qc * q_decay[None, :, None, :, None], prev)
    return (o_intra + o_cross).reshape(B, H, S, Dh)

def _retention(q, k, v, logit_fwd, logit_bwd):
    B, S, _ = q.shape

    def heads(t):
        return t.astype(jnp.float32).reshape(B, S, N_RET_HEADS, HEAD_DIM).transpose(0, 2, 1, 3)

    qh = _rotary(heads(q)) * (HEAD_DIM ** -0.5)
    kh = _rotary(heads(k))
    vh = heads(v)
    lf = jax.nn.log_sigmoid(logit_fwd.astype(jnp.float32))
    lb = jax.nn.log_sigmoid(logit_bwd.astype(jnp.float32))
    fwd = _retention_direction(qh, kh, vh, lf, True)
    bwd = _retention_direction(qh[:, :, ::-1], kh[:, :, ::-1], vh[:, :, ::-1], lb, False)[:, :, ::-1]
    o = fwd + bwd
    o = o * lax.rsqrt(jnp.mean(o * o, axis=-1, keepdims=True) + EPS)
    return o.transpose(0, 2, 1, 3).reshape(B, S, D_GROUP).astype(q.dtype)

def _conformer_conv(a, b, conv_w, conv_b, ln_g, ln_b, w_pw):
    u = a * jax.nn.sigmoid(b)
    y = lax.conv_general_dilated(
        u, conv_w[:, None, :].astype(u.dtype), window_strides=(1,),
        padding=[(CONV_WIDTH // 2, CONV_WIDTH // 2)],
        dimension_numbers=('NWC', 'WIO', 'NWC'), feature_group_count=D_GROUP) + conv_b
    yf = y.astype(jnp.float32)
    mu = jnp.mean(yf, axis=-1, keepdims=True)
    var = jnp.mean((yf - mu) ** 2, axis=-1, keepdims=True)
    y = ((yf - mu) * lax.rsqrt(var + EPS)).astype(u.dtype) * ln_g + ln_b
    return jax.nn.silu(y) @ w_pw

def first_inputs(seed: int = 0) -> dict:
    key = jax.random.key(seed)
    ks = jax.random.split(key, 17)
    f32 = jnp.float32
    nrm = lambda k, shape, s: jax.random.normal(k, shape, f32) * s
    gam = 1.0 - 2.0 ** (-5.0 - jnp.arange(N_RET_HEADS, dtype=f32))
    ret_logit0 = jnp.log(gam) - jnp.log1p(-gam)
    return {
        "x": nrm(ks[0], (BATCH, SEQ, D_MODEL), 1.0),
        "c": nrm(ks[1], (BATCH, D_MODEL), 1.0),
        "norm_g": 1.0 + nrm(ks[2], (DEPTH, D_MODEL), 0.01),
        "w_ada": nrm(ks[3], (DEPTH, D_MODEL, 3 * D_MODEL), 0.5 * D_MODEL ** -0.5),
        "b_ada": nrm(ks[4], (DEPTH, 3 * D_MODEL), 0.01),
        "w_in": nrm(ks[5], (DEPTH, D_MODEL, D_IN), D_MODEL ** -0.5),
        "w_fft": nrm(ks[6], (DEPTH, D_GROUP, D_GROUP), D_GROUP ** -0.5),
        "na_rel_bias": nrm(ks[7], (DEPTH, N_NA_HEADS, 2 * NA_KH_MAX - 1, 2 * NA_KW - 1), 0.02),
        "ret_logit_fwd": ret_logit0[None] + nrm(ks[8], (DEPTH, N_RET_HEADS), 0.01),
        "ret_logit_bwd": ret_logit0[None] + nrm(ks[9], (DEPTH, N_RET_HEADS), 0.01),
        "conv_w": nrm(ks[10], (DEPTH, CONV_WIDTH, D_GROUP), CONV_WIDTH ** -0.5),
        "conv_b": nrm(ks[11], (DEPTH, D_GROUP), 0.01),
        "conv_ln_g": 1.0 + nrm(ks[12], (DEPTH, D_GROUP), 0.01),
        "conv_ln_b": nrm(ks[13], (DEPTH, D_GROUP), 0.01),
        "conv_w_pw": nrm(ks[14], (DEPTH, D_GROUP, D_GROUP), D_GROUP ** -0.5),
        "w_out": nrm(ks[15], (DEPTH, D_MIX, D_MODEL), D_MIX ** -0.5),
        "final_g": 1.0 + nrm(ks[16], (D_MODEL,), 0.01),
    }

def first_block(x, c, norm_g, w_ada, b_ada, w_in, w_fft, na_rel_bias, ret_logit_fwd, ret_logit_bwd,
              conv_w, conv_b, conv_ln_g, conv_ln_b, conv_w_pw, w_out, final_g):
    c_act = jax.nn.silu(c)
    for l in range(DEPTH):
        mod = c_act @ w_ada[l] + b_ada[l]
        shift, scale, gate = jnp.split(mod, 3, axis=-1)
        h = _rmsnorm(x, norm_g[l]) * (1.0 + scale[:, None, :]) + shift[:, None, :]
        z = h @ w_in[l]
        (f_x, f_g, na_q, na_k, na_v, na_g, r_q, r_k, r_v, r_g,
         cv_a, cv_b, cv_g) = jnp.split(z, N_IN_PIECES, axis=-1)
        o_fft = _fourier_mix(f_x, w_fft[l]) * jax.nn.silu(f_g)
        o_na = _neighbourhood_attention(na_q, na_k, na_v, na_rel_bias[l]) * jax.nn.silu(na_g)
        o_ret = _retention(r_q, r_k, r_v, ret_logit_fwd[l], ret_logit_bwd[l]) * jax.nn.silu(r_g)
        o_cv = _conformer_conv(cv_a, cv_b, conv_w[l], conv_b[l], conv_ln_g[l], conv_ln_b[l],
                               conv_w_pw[l]) * jax.nn.silu(cv_g)
        y = jnp.concatenate([o_fft, o_na, o_ret, o_cv], axis=-1) @ w_out[l]
        x = x + gate[:, None, :] * y
    return _rmsnorm(x, final_g)


CTX_LEN = 256
N_MIXERS_2 = 2
N_POOL_LAYERS = (DEPTH + N_MIXERS_2 - 1) // N_MIXERS_2
N_MLA_LAYERS = DEPTH // N_MIXERS_2
POOL_WIDTH = D_MODEL
POOL_GROUPS = 4
POOL_GROUP_DIM = POOL_WIDTH // POOL_GROUPS
POOL_WINDOWS = (2, 4, 8, 16)
MLA_HEADS = 16
Q_LORA_RANK = 512
KV_LORA_RANK = 512
QK_NOPE_DIM = 128
QK_ROPE_DIM = 64
V_HEAD_DIM = 128
MLA_WIDTH = MLA_HEADS * V_HEAD_DIM
MLA_IN_WIDTH = Q_LORA_RANK + KV_LORA_RANK + QK_ROPE_DIM + MLA_WIDTH
MLA_SCALE = (QK_NOPE_DIM + QK_ROPE_DIM) ** -0.5
Q_BLOCK = 128
NORM_EPS = 1e-6


def rms_norm(x, g):
    xf = x.astype(jnp.float32)
    y = xf * lax.rsqrt(jnp.mean(xf * xf, axis=-1, keepdims=True) + NORM_EPS)
    return (y * g.astype(jnp.float32)).astype(x.dtype)

def centred_multiscale_pool(u):
    L = u.shape[1]
    uf = u.astype(jnp.float32)
    cs = jnp.concatenate([jnp.zeros_like(uf[:, :1]), jnp.cumsum(uf, axis=1)], axis=1)
    win = jnp.array(POOL_WINDOWS, dtype=jnp.int32)
    left = win // 2
    right = win - 1 - left
    t = jnp.arange(L, dtype=jnp.int32)[:, None]
    hi = jnp.minimum(t + right + 1, L)
    lo = jnp.maximum(t - left, 0)
    g = jnp.arange(POOL_GROUPS, dtype=jnp.int32)[None, :]
    s = cs[:, hi, g] - cs[:, lo, g]
    mean = s / (hi - lo).astype(jnp.float32)[None, :, :, None]
    return (mean - uf).astype(u.dtype)

def pool_branch(h, w_in, w_grp, b_grp, scale, w_out):
    B, L, _ = h.shape
    u, gate = jnp.split(h @ w_in, 2, axis=-1)
    p = centred_multiscale_pool(u.reshape(B, L, POOL_GROUPS, POOL_GROUP_DIM))
    p = jnp.einsum('blgc,gcd->blgd', p, w_grp) + b_grp
    y = p.reshape(B, L, POOL_WIDTH) * scale
    return (y * jax.nn.silu(gate)) @ w_out

def axial_rope_tables(L):
    rows = L // GRID_W
    row = jnp.repeat(jnp.arange(rows, dtype=jnp.float32), GRID_W)
    col = jnp.tile(jnp.arange(GRID_W, dtype=jnp.float32), rows)
    n = QK_ROPE_DIM // 4
    freqs = ROPE_BASE ** (-jnp.arange(n, dtype=jnp.float32) / n)
    ang = jnp.stack([row[:, None] * freqs, col[:, None] * freqs], axis=1)
    return jnp.cos(ang), jnp.sin(ang)

def apply_axial_rope(x, cos, sin):
    xs = x.reshape(x.shape[:-1] + (2, 2, QK_ROPE_DIM // 4))
    x1, x2 = xs[..., 0, :], xs[..., 1, :]
    cos = cos.astype(x.dtype)
    sin = sin.astype(x.dtype)
    out = jnp.stack([x1 * cos - x2 * sin, x1 * sin + x2 * cos], axis=-2)
    return out.reshape(x.shape)

def mla_project(h, w_in, q_norm, kv_norm, w_uq, w_ukv, rope):
    B, L, _ = h.shape
    proj = h @ w_in
    c_q, c_kv, k_r, gate = jnp.split(
        proj, [Q_LORA_RANK, Q_LORA_RANK + KV_LORA_RANK, Q_LORA_RANK + KV_LORA_RANK + QK_ROPE_DIM], axis=-1)
    q = (rms_norm(c_q, q_norm) @ w_uq).reshape(B, L, MLA_HEADS, QK_NOPE_DIM + QK_ROPE_DIM)
    q_nope, q_rope = q[..., :QK_NOPE_DIM], q[..., QK_NOPE_DIM:]
    kv = (rms_norm(c_kv, kv_norm) @ w_ukv).reshape(B, L, MLA_HEADS, QK_NOPE_DIM + V_HEAD_DIM)
    k_nope, v = kv[..., :QK_NOPE_DIM], kv[..., QK_NOPE_DIM:]
    if rope is not None:
        cos, sin = rope
        q_rope = apply_axial_rope(q_rope, cos[:, None], sin[:, None])
        k_r = apply_axial_rope(k_r, cos, sin)
    return q_nope, q_rope, k_nope, k_r, v, gate

def mla_attend(q_nope, q_rope, k_nope, k_rope, v):
    s = (jnp.einsum('bqhd,bkhd->bhqk', q_nope, k_nope)
         + jnp.einsum('bqhr,bkr->bhqk', q_rope, k_rope)).astype(jnp.float32) * MLA_SCALE
    p = jax.nn.softmax(s, axis=-1).astype(v.dtype)
    return jnp.einsum('bhqk,bkhd->bqhd', p, v)

def blocked_mla_attend(q_nope, q_rope, k_nope, k_rope, v):
    B, L, H, _ = q_nope.shape
    nb = L // Q_BLOCK
    qn = q_nope.reshape(B, nb, Q_BLOCK, H, QK_NOPE_DIM).transpose(1, 0, 2, 3, 4)
    qr = q_rope.reshape(B, nb, Q_BLOCK, H, QK_ROPE_DIM).transpose(1, 0, 2, 3, 4)
    out = lax.map(lambda qb: mla_attend(qb[0], qb[1], k_nope, k_rope, v), (qn, qr))
    return out.transpose(1, 0, 2, 3, 4).reshape(B, L, H * V_HEAD_DIM)

def mla_branch(h_lat, h_ctx, w_in, q_norm, kv_norm, w_uq, w_ukv, w_out, need_ctx_out):
    L = h_lat.shape[1]
    rope = axial_rope_tables(L)
    qn_l, qr_l, kn_l, kr_l, v_l, g_l = mla_project(h_lat, w_in, q_norm, kv_norm, w_uq, w_ukv, rope)
    qn_c, qr_c, kn_c, kr_c, v_c, g_c = mla_project(h_ctx, w_in, q_norm, kv_norm, w_uq, w_ukv, None)
    kn = jnp.concatenate([kn_c, kn_l], axis=1)
    kr = jnp.concatenate([kr_c, kr_l], axis=1)
    v = jnp.concatenate([v_c, v_l], axis=1)
    o_lat = blocked_mla_attend(qn_l, qr_l, kn, kr, v)
    y_lat = (o_lat * jax.nn.silu(g_l)) @ w_out
    if not need_ctx_out:
        return y_lat, None
    B, Lc = h_ctx.shape[:2]
    o_ctx = mla_attend(qn_c, qr_c, kn_c, kr_c, v_c).reshape(B, Lc, MLA_WIDTH)
    y_ctx = (o_ctx * jax.nn.silu(g_c)) @ w_out
    return y_lat, y_ctx

def second_inputs(seed: int = 0) -> dict:
    key = jax.random.key(seed)
    ks = jax.random.split(key, 20)
    nrm = jax.random.normal
    f32 = jnp.float32
    return {
        "x": nrm(ks[0], (BATCH, SEQ, D_MODEL), f32),
        "c": nrm(ks[1], (BATCH, D_MODEL), f32),
        "ctx": nrm(ks[2], (BATCH, CTX_LEN, D_MODEL), f32),
        "c_ctx": nrm(ks[3], (D_MODEL,), f32),
        "ada_w": nrm(ks[4], (DEPTH, D_MODEL, 3 * D_MODEL), f32) * D_MODEL ** -0.5,
        "ada_b": nrm(ks[5], (DEPTH, 3 * D_MODEL), f32) * 0.01,
        "pre_norm": 1.0 + 0.1 * nrm(ks[6], (DEPTH, D_MODEL), f32),
        "post_norm": 1.0 + 0.1 * nrm(ks[7], (DEPTH, D_MODEL), f32),
        "pool_w_in": nrm(ks[8], (N_POOL_LAYERS, D_MODEL, 2 * POOL_WIDTH), f32) * D_MODEL ** -0.5,
        "pool_w_grp": nrm(ks[9], (N_POOL_LAYERS, POOL_GROUPS, POOL_GROUP_DIM, POOL_GROUP_DIM), f32) * POOL_GROUP_DIM ** -0.5,
        "pool_b_grp": nrm(ks[10], (N_POOL_LAYERS, POOL_GROUPS, POOL_GROUP_DIM), f32) * 0.01,
        "pool_scale": 1.0 + 0.1 * nrm(ks[11], (N_POOL_LAYERS, POOL_WIDTH), f32),
        "pool_w_out": nrm(ks[12], (N_POOL_LAYERS, POOL_WIDTH, D_MODEL), f32) * POOL_WIDTH ** -0.5,
        "mla_w_in": nrm(ks[13], (N_MLA_LAYERS, D_MODEL, MLA_IN_WIDTH), f32) * D_MODEL ** -0.5,
        "mla_q_norm": 1.0 + 0.1 * nrm(ks[14], (N_MLA_LAYERS, Q_LORA_RANK), f32),
        "mla_kv_norm": 1.0 + 0.1 * nrm(ks[15], (N_MLA_LAYERS, KV_LORA_RANK), f32),
        "mla_w_uq": nrm(ks[16], (N_MLA_LAYERS, Q_LORA_RANK, MLA_HEADS * (QK_NOPE_DIM + QK_ROPE_DIM)), f32) * Q_LORA_RANK ** -0.5,
        "mla_w_ukv": nrm(ks[17], (N_MLA_LAYERS, KV_LORA_RANK, MLA_HEADS * (QK_NOPE_DIM + V_HEAD_DIM)), f32) * KV_LORA_RANK ** -0.5,
        "mla_w_out": nrm(ks[18], (N_MLA_LAYERS, MLA_WIDTH, D_MODEL), f32) * MLA_WIDTH ** -0.5,
    }

def second_block(x, c, ctx, c_ctx, ada_w, ada_b, pre_norm, post_norm,
              pool_w_in, pool_w_grp, pool_b_grp, pool_scale, pool_w_out,
              mla_w_in, mla_q_norm, mla_kv_norm, mla_w_uq, mla_w_ukv, mla_w_out):
    for i in range(DEPTH):
        last = i == DEPTH - 1
        j = i // N_MIXERS_2
        is_pool = (i % N_MIXERS_2) == 0
        need_ctx_out = not last
        need_ctx_in = need_ctx_out or not is_pool
        shift, scale, gate = jnp.split(jax.nn.silu(c) @ ada_w[i] + ada_b[i], 3, axis=-1)
        h_lat = rms_norm(x, pre_norm[i]) * (1 + scale[:, None]) + shift[:, None]
        h_ctx = None
        gate_c = None
        if need_ctx_in:
            shift_c, scale_c, gate_c = jnp.split(jax.nn.silu(c_ctx) @ ada_w[i] + ada_b[i], 3, axis=-1)
            h_ctx = rms_norm(ctx, pre_norm[i]) * (1 + scale_c) + shift_c
        if is_pool:
            y_lat = pool_branch(h_lat, pool_w_in[j], pool_w_grp[j], pool_b_grp[j], pool_scale[j], pool_w_out[j])
            y_ctx = (pool_branch(h_ctx, pool_w_in[j], pool_w_grp[j], pool_b_grp[j], pool_scale[j], pool_w_out[j])
                     if need_ctx_out else None)
        else:
            y_lat, y_ctx = mla_branch(h_lat, h_ctx, mla_w_in[j], mla_q_norm[j], mla_kv_norm[j],
                                      mla_w_uq[j], mla_w_ukv[j], mla_w_out[j], need_ctx_out)
        x = x + gate[:, None] * rms_norm(y_lat, post_norm[i])
        if need_ctx_out:
            ctx = ctx + gate_c * rms_norm(y_ctx, post_norm[i])
    return x


def setup_inputs(seed=0):
    out = dict(first_inputs(seed))
    for name, value in second_inputs(seed + 1).items():
        if name != "x":
            out[name + "_2"] = value
    return out


def reference(
    x, c, norm_g, w_ada, b_ada, w_in, w_fft, na_rel_bias, ret_logit_fwd, ret_logit_bwd, conv_w,
    conv_b, conv_ln_g, conv_ln_b, conv_w_pw, w_out, final_g, c_2, ctx_2, c_ctx_2, ada_w_2,
    ada_b_2, pre_norm_2, post_norm_2, pool_w_in_2, pool_w_grp_2, pool_b_grp_2, pool_scale_2,
    pool_w_out_2, mla_w_in_2, mla_q_norm_2, mla_kv_norm_2, mla_w_uq_2, mla_w_ukv_2, mla_w_out_2,
):
    x = first_block(
        x, c, norm_g, w_ada, b_ada, w_in, w_fft, na_rel_bias, ret_logit_fwd, ret_logit_bwd,
        conv_w, conv_b, conv_ln_g, conv_ln_b, conv_w_pw, w_out, final_g,
    )
    return second_block(
        x, c_2, ctx_2, c_ctx_2, ada_w_2, ada_b_2, pre_norm_2, post_norm_2, pool_w_in_2,
        pool_w_grp_2, pool_b_grp_2, pool_scale_2, pool_w_out_2, mla_w_in_2, mla_q_norm_2,
        mla_kv_norm_2, mla_w_uq_2, mla_w_ukv_2, mla_w_out_2,
    )


_drawn_inputs = setup_inputs


def setup_inputs(seed=0):
    import zlib

    import numpy as np

    out = dict(_drawn_inputs(seed))
    spreads = {}
    factors = {'norm_g': 8.0,
     'b_ada': 5.537,
     'na_rel_bias': 8.0,
     'conv_b': 8.0,
     'conv_ln_g': 8.0,
     'conv_ln_b': 8.0,
     'final_g': 29.602,
     'ada_b_2': 11.691,
     'pool_b_grp_2': 42.521,
     'mla_q_norm_2': 10.513,
     'post_norm_2': 3.232,
     'pool_scale_2': 4.172,
     'mla_kv_norm_2': 3.258}
    for name, (base, spread) in spreads.items():
        noise = np.random.default_rng([zlib.crc32(name.encode()), seed]).standard_normal(out[name].shape)
        drawn = base * np.exp(spread * noise) if base else spread * noise
        out[name] = __import__('jax').numpy.asarray(drawn.astype(out[name].dtype))
    for name, factor in factors.items():
        out[name] = (out[name] * factor).astype(out[name].dtype)
    return out
```

```python
import concourse.bass as bass
from concourse import mybir
from contextlib import ExitStack
import numpy as np

F = mybir.dt.float32
R = mybir.dt.float32r
ACT = mybir.ActivationFunctionType
ALU = mybir.AluOpType
AX = mybir.AxisListType

D = 2048
NKT = 16
EPS = 1e-6
MASKED = -1.0e30
MLA_SCALE = (128 + 64) ** -0.5
WINDOWS = (2, 4, 8, 16)
PIECES = ["f_x", "f_g", "na_q", "na_k", "na_v", "na_g", "r_q", "r_k", "r_v", "r_g",
          "cv_a", "cv_b", "cv_g"]
ORDER = ["cv_a", "cv_b", "r_q", "r_k", "r_v", "r_g", "na_q", "na_k", "na_v", "na_g",
         "f_x", "cv_g", "f_g"]
OUT_ORDER = ["ret", "na", "cv", "fft"]
CONCAT = ["fft", "na", "ret", "cv"]

CONST_COLS = {}


def _const_columns():
    at = 0
    for name, n in [("ident", 128), ("ones", 128), ("cc", 256), ("dist_f", 384), ("dist_b", 384),
                    ("sel", 4), ("hsel", 2), ("cosr", 64), ("sinr", 128), ("mask", 64),
                    ("eps", 1), ("edge", 64)]:
        CONST_COLS[name] = (at, at + n)
        at += n
    return at


NCONST = _const_columns()


def constants():
    k = np.zeros((128, NCONST), np.float64)

    def put(name, a):
        lo, hi = CONST_COLS[name]
        k[:, lo:hi] = np.asarray(a).reshape(128, hi - lo)

    p = np.arange(128)
    put("ident", np.eye(128))
    put("ones", np.ones((128, 128)))
    ang = 2 * np.pi * ((p[:, None] * p[None, :]) % 128) / 128
    norm = 1.0 / np.sqrt(256 * 128)
    put("cc", np.concatenate([np.cos(ang) * norm, -np.sin(ang) * norm], axis=1))
    m = np.arange(384)[None, :] - 128 - p[:, None]
    put("dist_f", np.maximum(m, 0))
    put("dist_b", np.maximum(-m, 0))
    sel = np.zeros((128, 4))
    for i, rows in enumerate([(0, 64), (1, 65), (32, 96), (33, 97)]):
        sel[list(rows), i] = 1
    put("sel", sel)
    put("hsel", np.stack([p < 64, p >= 64], axis=1))
    inv = 10000.0 ** (-np.arange(32, dtype=np.float32) / np.float32(32))
    tok = np.arange(2)[None, :, None] * 128 + p[:, None, None]
    a = (tok.astype(np.float32) * inv.astype(np.float32)[None, None, :]).astype(np.float64)
    put("cosr", np.cos(a))
    put("sinr", np.stack([-np.sin(a), np.sin(a)], axis=2))
    col = p % 64
    start = np.clip(col - 8, 0, 48)
    rel = np.arange(64)[None, :] - start[:, None]
    put("mask", np.where((rel >= 0) & (rel < 16), 0.0, MASKED))
    put("eps", np.full((128, 1), EPS))
    edge = np.ones((4, 2, 8))
    for g, w in enumerate(WINDOWS):
        left, right = w // 2, w - 1 - w // 2
        for side, t0 in enumerate((0, 248)):
            for i in range(8):
                t = t0 + i
                cnt = min(t + right + 1, 256) - max(t - left, 0)
                edge[g, side, i] = w / cnt
    put("edge", np.broadcast_to(edge.reshape(1, 64), (128, 64)))
    return k.astype(np.float32)


def dft_tokens():
    n = np.arange(256)
    ang = 2 * np.pi * ((n[:, None] * n[None, :]) % 256) / 256
    t = np.concatenate([np.cos(ang), np.sin(ang)], axis=1)
    return np.ascontiguousarray(t.reshape(2, 128, 512).transpose(1, 0, 2)).reshape(128, 1024).astype(np.float32)


def rope_tables():
    d = np.arange(128) % 64
    n = np.arange(256)
    freqs = (10000.0 ** (-np.arange(16, dtype=np.float32) / np.float32(16))).astype(np.float32)
    pos = np.where((d < 32)[:, None], (n // 64)[None, :], (n % 64)[None, :]).astype(np.float32)
    ang = (pos * freqs[d % 16][:, None]).astype(np.float32).astype(np.float64)
    sign = np.where(d % 32 < 16, -1.0, 1.0)[:, None]
    swap = np.zeros((128, 128))
    i = np.arange(128)
    swap[i ^ 16, i] = 1
    return np.concatenate([np.cos(ang), np.sin(ang) * sign, swap], axis=1).astype(np.float32)


def pack_a(w):
    k, n = w.shape
    t = w.reshape(k // 512, 4, 128, n // 512, 512).transpose(3, 0, 2, 1, 4)
    return np.ascontiguousarray(t).reshape(n // 512, k // 512, 128, 2048)


def pack_b(w):
    k, n = w.shape
    t = w.reshape(16, 128, n // 128, 128).transpose(2, 1, 0, 3)
    return np.ascontiguousarray(t).reshape(n // 128, 128, 2048)


def pack_b4(w):
    t = w.reshape(4, 128, w.shape[1] // 512, 4, 128).transpose(2, 1, 3, 0, 4)
    return np.ascontiguousarray(t).reshape(w.shape[1] // 512, 128, 2048)


def pack_ada(w):
    t = w.reshape(8, 2, 128, 3, 4, 512)
    mod = t[:, :, :, 0:2].transpose(4, 0, 2, 1, 3, 5)
    gate = t[:, :, :, 2].reshape(8, 2, 128, 2, 2, 512).transpose(3, 0, 2, 1, 4, 5)
    return np.concatenate([mod.reshape(4, 8, 128, 2048), gate.reshape(2, 8, 128, 2048)])


def pack_ada_bias(b):
    t = b.reshape(3, 4, 512)
    jobs = [(t[0, j], t[1, j]) for j in range(4)] + [(t[2, 0], t[2, 1]), (t[2, 2], t[2, 3])]
    return np.stack([np.stack([a, a, c, c]) for a, c in jobs])


def cols(v):
    return np.asarray(v).reshape(-1, 128).T


PARAM_COLS = {}


def _param_columns():
    at = 0
    for name, n in [("norm_g", 32), ("conv", 272), ("logit", 32), ("final_g", 16), ("pre", 32), ("post", 32),
                    ("b_grp", 16), ("p_scale", 16), ("q_norm", 4), ("kv_norm", 4), ("c", 48)]:
        PARAM_COLS[name] = (at, at + n)
        at += n
    return at


NPARAM = _param_columns()


def lay_out(i):
    o = {}
    o["x_in"] = i["x"][0]
    o["ctx_in"] = i["ctx_2"][0]
    out_rows = [CONCAT.index(n) for n in OUT_ORDER]
    o["w_ada"] = np.stack([pack_ada(w) for w in i["w_ada"]] + [pack_ada(w) for w in i["ada_w_2"]])
    o["b_ada"] = np.stack([pack_ada_bias(b) for b in i["b_ada"]] + [pack_ada_bias(b) for b in i["ada_b_2"]])
    o["w_in"] = np.stack([pack_a(w) for w in i["w_in"]])
    o["w_fft"] = np.stack([pack_a(w) for w in i["w_fft"]])
    o["w_pw"] = np.stack([pack_a(w) for w in i["conv_w_pw"]])
    o["w_out"] = np.stack([pack_a(w.reshape(4, 512, 2048)[out_rows].reshape(2048, 2048)) for w in i["w_out"]])
    conv = np.concatenate([i["conv_w"], i["conv_b"][:, None], i["conv_ln_g"][:, None], i["conv_ln_b"][:, None]], axis=1)
    conv = conv.reshape(2, 34, 4, 128).transpose(3, 0, 2, 1).reshape(128, 272)
    logit = np.stack([i["ret_logit_fwd"], i["ret_logit_bwd"]], axis=1).reshape(1, 32)
    c = np.stack([cols(i["c"][0]), cols(i["c_2"][0]), cols(i["c_ctx_2"])], axis=2).reshape(128, 48)
    parts = {"norm_g": cols(i["norm_g"]), "conv": conv, "logit": np.broadcast_to(logit, (128, 32)),
             "final_g": cols(i["final_g"]), "pre": cols(i["pre_norm_2"]), "post": cols(i["post_norm_2"]),
             "b_grp": cols(i["pool_b_grp_2"]), "p_scale": cols(i["pool_scale_2"]),
             "q_norm": cols(i["mla_q_norm_2"]), "kv_norm": cols(i["mla_kv_norm_2"]), "c": c}
    o["params"] = np.concatenate([parts[n] for n in PARAM_COLS], axis=1)
    t = np.pad(i["na_rel_bias"], ((0, 0), (0, 0), (0, 0), (48, 48)))
    half, cc = np.arange(128)[:, None, None] // 64, np.arange(128)[:, None, None] % 64
    m, c2 = np.arange(6)[None, :, None], np.arange(64)[None, None, :]
    o["na_bias"] = np.ascontiguousarray(t[:, :, m + 5 - half, c2 - cc + 63]).reshape(2, 8, 128, 384)
    o["pool_in"] = pack_b(i["pool_w_in_2"][0])
    o["pool_grp"] = np.concatenate([pack_b4(w) for w in i["pool_w_grp_2"][0]])
    o["pool_out"] = pack_a(i["pool_w_out_2"][0])
    w = i["mla_w_in_2"][0]
    o["mla_in"] = pack_a(np.concatenate([w[:, :1024], w[:, 1088:]], axis=1))
    o["mla_kr"] = pack_b(np.concatenate([w[:, 1024:1088]] * 2, axis=1))
    uq = i["mla_w_uq_2"][0].reshape(512, 16, 192)
    ukv = i["mla_w_ukv_2"][0].reshape(512, 16, 256)
    qk = np.stack([uq[:, :, :128], ukv[:, :, :128]], axis=2).reshape(4, 128, 8, 2, 2, 128)
    o["mla_qk"] = np.ascontiguousarray(qk.transpose(2, 1, 3, 4, 0, 5)).reshape(8, 128, 2048)
    o["mla_rope"] = pack_b4(np.ascontiguousarray(uq[:, :, 128:]).reshape(512, 1024))
    o["mla_v"] = pack_a(np.ascontiguousarray(ukv[:, :, 128:]).reshape(512, 2048))
    o["mla_out"] = pack_a(i["mla_w_out_2"][0])
    o["const"] = constants()
    o["dft"] = dft_tokens()
    o["rope"] = rope_tables()
    return {n: np.ascontiguousarray(a) for n, a in o.items()}


class Token:

    def __init__(self, sem, value=None):
        self.sem, self.value, self.hit = sem, value, False


def flat(after):
    for t in after:
        if t is None:
            continue
        if isinstance(t, (list, tuple)):
            yield from flat(t)
        else:
            yield t


class Queue:

    def __init__(self, sem):
        self.sem, self.ops, self.last = sem, [], None

    def do(self, fn, after=()):
        after = list(flat(after))
        for t in after:
            t.hit = True
        tok = Token(self.sem)
        self.ops.append((fn, after, tok))
        self.last = tok
        return tok

    def number(self):
        n = 0
        for _, _, tok in self.ops:
            if tok.value is None and tok.hit:
                n += 1
                tok.value = n

    def play(self, e):
        seen = {}
        for fn, after, tok in self.ops:
            need = {}
            for t in after:
                need[t.sem.name] = max(need.get(t.sem.name, (0, t.sem)), (t.value, t.sem), key=lambda p: p[0])
            for name, (v, sem) in need.items():
                if seen.get(name, 0) < v:
                    e.wait_ge(sem, v)
                    seen[name] = v
            ins = fn(e)
            if tok.hit and tok.sem is self.sem:
                ins.then_inc(self.sem, 1)


class Slots:

    def __init__(self, places):
        self.free = [(p, []) for p in places]

    def take(self):
        return self.free.pop(0)

    def put(self, place, toks):
        self.free.append((place, list(flat([toks]))))



def bcast(ap, *dims):
    return bass.AP(tensor=ap.tensor, offset=ap.offset, ap=[list(ap.ap[0])] + [list(d) for d in dims])


def three(ap, a):
    return ap.rearrange("p (a b) -> p a b", a=a)


def weave(main, ada, over):
    res, k = [], 0
    for n, u in enumerate(main):
        res.append(u)
        want = len(ada) if n + 1 >= over else len(ada) * (n + 1) // over
        res += ada[k:want]
        k = max(k, want)
    return res


def program(nc, io, out, upto=None):
    ctx = ExitStack()
    with ctx:
        def sb(name, shape, dt, c=ctx):
            return c.enter_context(nc.sbuf_tensor("s_" + name, shape, dt))

        def sem(name):
            return ctx.enter_context(nc.semaphore("m_" + name))

        NR, NH = 4, 3
        KC = sb("const", [128, NCONST], F)
        PR = sb("params", [128, NPARAM], F)
        raw = [sb(f"raw{i}", [128, 2048], F) for i in range(NR)]
        hi_s = [sb(f"hi{i}", [128, 1024], R) for i in range(NH)]
        lo_s = [sb(f"lo{i}", [128, 1024], R) for i in range(NH)]
        E = [sb(f"E{i}", [128, 544], F) for i in range(4)]
        OG = [sb(f"og{i}", [128, 2, 256], F) for i in range(2)]
        GB1 = sb("gb1", [128, 512], F)
        CS = sb("cs", [128, 16, 3], F)
        MOD = [sb(f"mod{i}", [128, 3, 16, 2], F) for i in range(2)]
        ROWS = sb("rows", [128, 512], F)
        BR = sb("br", [128, 512], F)
        SS = sb("ss", [128, 4, 4], F)
        ST = sb("stat", [128, 16], F)
        LG = sb("lg", [128, 6, 32], F)
        RN = sb("rn", [128, 2, 16], F)
        MX = sb("mx", [128, 2, 4], F)
        BN = sb("bn", [128, 2, 16], F)

        def overlay(*variants):
            made, size = {}, 0
            for n_var, names in enumerate(variants):
                c, n = ExitStack(), 0
                for name, shape, dt in names:
                    made[name] = sb(name or f"gap{n_var}_{variants[0][0][0]}_{n}", shape, dt, c)
                    n += 4 * int(np.prod(shape[1:]))
                c.close()
                size = max(size, n)
            return made, size

        W, size = overlay(
            [("W1", [128, 2, 2048], F), ("G", [128, 2, 2, 512], F), ("qT", [128, 4, 256], F),
             ("kT", [128, 4, 256], F), ("dec", [128, 2, 384], F), ("nb", [128, 2, 384], F),
             ("dft", [128, 2, 512], F)],
            [("YB", [128, 8192], F), ("CT", [128, 2048], F), ("GB0", [128, 512], F)],
            [("cqT_h", [128, 4, 256], R), ("cqT_l", [128, 4, 256], R), ("ckT_h", [128, 4, 512], R),
             ("ckT_l", [128, 4, 512], R), ("cq", [128, 2, 512], F), ("ckv", [128, 4, 512], F),
             ("kr_h", [128, 512], R), ("kr_l", [128, 512], R), ("rope", [128, 640], F)],
            [("Y2", [128, 2, 2048], F), ("", [128, 2048], F)] +
            [(f"{n}{i}", [128, k], R) for i in range(2)
             for n, k in (("qn_h", 256), ("qn_l", 256), ("kn_h", 512), ("kn_l", 512))])
        sb("room_w", [128, size // 4], F)
        XR, size = overlay([("X", [128, 2, 2048], F)], [("PH", [128, 4, 512], R), ("PL", [128, 4, 512], R)])
        sb("room_x", [128, size // 4], F)
        HU, _ = overlay(
            [("", [128, 6144], F), ("uT", [128, 4, 286], F)],
            [("", [128, 6144], F), ("PQ", [128, 4, 512], F), ("", [128, 6144], F), ("acc", [128, 4, 256], F),
             ("FX", [128, 2, 512], F)],
            [("", [128, 4096], F), ("V", [128, 2, 4, 512], F), ("", [128, 4096], F), ("qr_h", [128, 4, 256], R),
             ("qr_l", [128, 4, 256], R), ("Pm", [128, 2, 512], F), ("PT", [128, 4, 256], F)])
        Hh = sb("Hh", [128, 2, 16, 256], R)
        Hl = sb("Hl", [128, 2, 16, 256], R)
        ps = ctx.enter_context(nc.psum_tensor("ps", [128, 8, 512], F))

        pe, act, dve, pool, sp = (Queue(sem(n)) for n in ("pe", "act", "dve", "pool", "sp"))
        ring_sems = [sem(f"ring{i}") for i in range(NR)]
        loaded = {}

        def K(name, lo=0, hi=None):
            a, b = CONST_COLS[name]
            return KC[:, a + lo:(b if hi is None else a + hi)]

        def P(name, lo=0, hi=None):
            a, b = PARAM_COLS[name]
            return PR[:, a + lo:(b if hi is None else a + hi)]

        def load(q, dst, src, s, *after):
            loaded[s.name] = loaded.get(s.name, 0) + 16
            q.do(lambda e: e.dma_start(dst, src).then_inc(s, 16), after)
            return Token(s, loaded[s.name])

        def mm(o, l, r, first, last, *after):
            return pe.do(lambda e: e.matmul(o, l, r, start=first, stop=last, skip_group_check=True), after)

        def mm3(o, l, r, first, last, *after):
            mm(o, l[0], r[0], first, False, *after)
            mm(o, l[0], r[1], False, False)
            return mm(o, l[1], r[0], False, last)

        def tr(o, i, *after):
            ident = K("ident")
            return pe.do(lambda e: e.transpose(o, i, ident), after)

        def tt(q, o, a, b, op, *after):
            return q.do(lambda e: e.tensor_tensor(o, a, b, op), after)

        def ts(q, o, a, s1, s2, op0, op1, *after):
            if op1 is None:
                return q.do(lambda e: e.tensor_scalar(o, a, s1, None, op0), after)
            return q.do(lambda e: e.tensor_scalar(o, a, s1, s2, op0, op1), after)

        def stt(q, o, a, s1, b, op0, op1, *after):
            return q.do(lambda e: e.scalar_tensor_tensor(out=o, in0=a, scalar=s1, in1=b, op0=op0, op1=op1), after)

        def cp(q, o, a, *after):
            if q is act:
                return q.do(lambda e: e.activation(o, a, ACT.Copy), after)
            return q.do(lambda e: e.tensor_copy(o, a), after)

        def fn(f, o, a, *after, **kw):
            return act.do(lambda e: e.activation(o, a, f, **kw), after)

        def fill(q, o, v, *after):
            return q.do(lambda e: e.memset(o, v), after)

        def recip(o, a, *after):
            return dve.do(lambda e: e.reciprocal(o, a), after)

        def split(h, l, v, *after):
            t = cp(act, h, v, *after)
            return tt(dve, l, v, h, ALU.subtract, t)

        main = Slots([0, 1, 2, 3])
        side = Slots([4, 5, 6])
        scratch = Slots([0, 1, 2, 3])
        og = Slots([0, 1])

        def w_units(l):
            if l < 2:
                u = [("w", io["w_in"][l, PIECES.index(p), i]) for p in ORDER for i in range(4)]
                u += [("w", io["w_pw"][l, 0, 0]), ("w", io["w_fft"][l, 0, 0])]
                return u + [("w", io["w_out"][l, c, i]) for c in range(4) for i in range(4)]
            if l == 2:
                u = []
                for g in range(4):
                    u += [("w", io["pool_in"][4 * g + i]) for i in range(4)]
                    u += [("w", io["pool_in"][16 + 4 * g + i]) for i in range(4)]
                    u += [("w", io["pool_grp"][g])]
                return u + [("w", io["pool_out"][c, i]) for c in range(4) for i in range(4)]
            u = [("w", io["mla_in"][0, i]) for i in range(4)] + [("w", io["mla_in"][1, i]) for i in range(4)]
            u += [("w", io["mla_kr"][0])]
            u += [("w", io["mla_in"][2 + c, i]) for c in range(4) for i in range(4)]
            for g in range(4):
                u += [("w", io["mla_v"][g, 0])]
                if g % 2 == 0:
                    u += [("w", io["mla_rope"][g // 2])]
                u += [("w", io["mla_qk"][2 * g + i]) for i in range(2)]
            return u + [("w", io["mla_out"][c, i]) for c in range(4) for i in range(4)]

        def a_units(l, jobs):
            return [("ada", io["w_ada"][l, j, u], l, j, u) for j in jobs for u in range(8)]

        units = a_units(0, range(4))
        for l, over in enumerate((66, 54, 44, 16)):
            nxt = a_units(l + 1, range(4)) if l < 3 else []
            units += weave(w_units(l), a_units(l, (4, 5)) + nxt, over)

        st = dict(consumed_upto=0, dma=0, pos=0, half=0, split=0, loaded=[], raw_free=[[] for _ in range(NR)])
        halves = [(n, h) for n, u in enumerate(units) if u[0] == "w" for h in range(2)]
        hl = Slots(range(NH))
        ready = {}

        def more_loads():
            while st["dma"] < len(units) and st["dma"] - NR < st["consumed_upto"]:
                n = st["dma"]
                st["loaded"].append(load(sp, raw[n % NR][:, :], units[n][1], ring_sems[n % NR], st["raw_free"][n % NR]))
                st["dma"] += 1

        done_units = set()

        def unit_read(n, tok):
            st["raw_free"][n % NR] = [tok]
            done_units.add(n)
            while st["consumed_upto"] in done_units:
                st["consumed_upto"] += 1
            more_loads()

        def more_splits():
            while st["split"] < len(halves) and hl.free:
                n, h = halves[st["split"]]
                if n >= st["dma"]:
                    return
                i, free = hl.take()
                v = raw[n % NR][:, 1024 * h:1024 * (h + 1)]
                t = split(hi_s[i][:, :], lo_s[i][:, :], v, st["loaded"][n], free)
                ready[st["split"]] = (i, t)
                st["split"] += 1
                if h == 1:
                    unit_read(n, t)

        sides = []

        def pump(n=1, width=2):
            for _ in range(n):
                for s in list(sides)[:width]:
                    if s["wait"] > 0:
                        s["wait"] -= 1
                        continue
                    try:
                        s["wait"] = next(s["gen"]) or 0
                    except StopIteration:
                        sides.remove(s)

        def launch(name, gen, front=False, start=False):
            s = dict(name=name, gen=gen, wait=(next(gen) or 0) if start else 0)
            if front:
                sides.insert(0, s)
            else:
                sides.append(s)

        def finish(name):
            for s in list(sides):
                if s["name"] == name:
                    for _ in s["gen"]:
                        pass
                    sides.remove(s)

        def work_off_ada():
            while units[st["pos"]][0] == "ada":
                ada_unit(st["pos"])
                st["pos"] += 1
                pump()

        def pump_until(there):
            for _ in range(400):
                if there():
                    return
                pump()
            raise AssertionError("no side job leads there: " + str([s["name"] for s in sides]))

        def next_half():
            work_off_ada()
            more_splits()
            k = st["half"]
            st["half"] += 1
            if k % 2 == 1:
                st["pos"] += 1
            i, t = ready.pop(k)
            return (hi_s[i], lo_s[i]), t, i

        def give_back(i, tok):
            hl.put(i, tok)
            more_splits()

        ada = dict(bank=[], rows=[], br=[])
        mod_ready, mod_read = {}, {0: [], 1: []}
        br_sem = sem("br")

        def load_bias(l, j, *after):
            load(sp, BR[0:2, :], io["b_ada"][l, j, 0:2], br_sem, *after)
            return load(sp, BR[32:34, :], io["b_ada"][l, j, 2:4], br_sem, *after)

        def ada_unit(n):
            _, _, l, j, u = units[n]
            c0, m = (0, 1) if l < 2 else (1, 2)
            for s in range(4):
                o = ps[32 * s:32 * s + m, 7, :]
                last = mm(o, CS[:, 2 * u + s // 2, c0:c0 + m], raw[n % NR][:, 512 * s:512 * (s + 1)],
                          u == 0, u == 7, st["loaded"][n], cs_ready, ada["bank"] if u == 0 else None)
            unit_read(n, last)
            if u == 4:
                ada["br"] = load_bias(l, j, ada["bank"])
            if u == 7:
                ada["bank"] = [tt(dve, ROWS[:, :], ps[:, 7, :], BR[:, :], ALU.add, last, ada["br"], ada["rows"])]
                launch("ada", ada_cols(l, j, ada["bank"]), front=True)
                ada["rows"] = None

        def ada_cols(l, j, rows):
            yield
            b, free = side.take()
            for i in range(4):
                t = mm(ps[:, b, 4 * i:4 * i + 4], ROWS[:, 128 * i:128 * (i + 1)], K("sel"), True, True,
                       rows if i == 0 else None, free if i == 0 else None)
            ada["rows"] = [t]
            M, old = MOD[l % 2], mod_read[l % 2]
            v = ps[:, b, 0:16].rearrange("p (i c) -> p i c", i=4)
            nc_ = 1 if l < 2 else 2
            if j < 4:
                g = P("norm_g" if l < 2 else "pre", 16 * (l % 2) + 4 * j, 16 * (l % 2) + 4 * j + 4)
                cp(dve, M[:, 0, 4 * j:4 * j + 4, 0:nc_], v[:, :, 0:nc_], t, old)
                for c in range(nc_):
                    t = stt(dve, M[:, 1, 4 * j:4 * j + 4, c], v[:, :, 2 + c], 1.0, g, ALU.add, ALU.mult)
            else:
                for half in range(2):
                    k0 = 8 * (j - 4) + 4 * half
                    for c in range(nc_):
                        o, i = M[:, 2, k0:k0 + 4, c], v[:, :, 2 * half + c]
                        if l < 2:
                            t = cp(dve, o, i, t, old)
                        else:
                            t = tt(dve, o, i, P("post", 16 * (l - 2) + k0, 16 * (l - 2) + k0 + 4), ALU.mult, t, old)
            side.put(b, t)
            mod_ready[l, j] = t

        def chunk_a(stat, tiles, nk, need, evac, hooks={}, order=None):
            banks = [main.take() for _ in tiles]
            for h in range(nk // 2):
                w, w_tok, slot = next_half()
                last = []
                for j in range(2):
                    kt = 2 * h + j
                    for n, t in enumerate(tiles):
                        b, free = banks[n]
                        last_n = mm3(ps[:, b, :], stat(kt, t), [p[:, 512 * j:512 * (j + 1)] for p in w],
                                     kt == 0, kt == nk - 1, w_tok, need(kt), free if kt == 0 else None)
                        last.append(last_n)
                give_back(slot, last[-1])
                if h in hooks:
                    hooks[h](last[-1])
                if h < nk // 2 - 1:
                    pump()
            for n, t in enumerate(tiles):
                main.put(banks[n][0], evac(n, ps[:, banks[n][0], :], last[n - len(tiles)]))
            pump()

        def b_tile(rhs, shape, need, evac):
            b, free = main.take()
            for part in range(2):
                w, w_tok, slot = next_half()
                for j in range(8):
                    kt = 8 * part + j
                    last = mm3(shape(b), [p[:, 128 * j:128 * (j + 1)] for p in w], rhs(kt), kt == 0, kt == 15,
                               w_tok, need(kt), free if kt == 0 else None)
                give_back(slot, last)
                if part == 0:
                    pump()
            main.put(b, evac(shape(b), last))
            pump()

        def b_half(jobs):
            w, w_tok, slot = next_half()
            todo = []
            for m, (rhs, shape, need, evac) in enumerate(jobs):
                b, free = main.take()
                for kt in range(4):
                    c = 128 * (4 * m + kt)
                    last = mm3(shape(b), [p[:, c:c + 128] for p in w], rhs(kt), kt == 0, kt == 3,
                               w_tok, need(kt), free if kt == 0 else None)
                todo.append((b, evac, shape(b), last))
            give_back(slot, last)
            for b, evac, o, t in todo:
                main.put(b, evac(o, t))

        def sums(src, i, junk, *after):
            return fn(ACT.Square, junk, src, *after, accum_out=SS[:, i[0], i[1]:i[1] + 1])

        def inv_rms(tiles, parts, n, col, *after):
            k = len(tiles)
            t0, o = tiles[0], ST[:, col:col + k]
            if parts > 1:
                t = dve.do(lambda e: e.tensor_reduce(o, SS[:, t0:t0 + k, 0:parts], AX.X, ALU.add), after)
            else:
                t = cp(dve, o, SS[:, t0:t0 + k, 0], after)
            t = fn(ACT.Sqrt, o, o, t, bias=K("eps"), scale=1.0 / n)
            return recip(o, o, t)

        def feature_major(src, dst, mul, add, nk, when, got):
            for b2 in range(nk // 2):
                b, free = side.take()
                for j in range(2):
                    kt = 2 * b2 + j
                    for t2 in range(2):
                        t = tr(ps[:, b, 256 * j + 128 * t2:256 * j + 128 * (t2 + 1)],
                               src(t2)[:, 128 * kt:128 * (kt + 1)], when(kt), free)
                i, ofree = og.take()
                for j in range(2):
                    kt = 2 * b2 + j
                    v = ps[:, b, 256 * j:256 * (j + 1)]
                    if add is None:
                        e = ts(dve, OG[i][:, j, :], v, mul(kt), None, ALU.mult, None, t, ofree)
                    else:
                        e = ts(dve, OG[i][:, j, :], v, mul(kt), add(kt), ALU.mult, ALU.add, t, ofree)
                side.put(b, e)
                h, l = dst(2 * b2)
                t = split(h, l, OG[i][:, :, :], e)
                og.put(i, t)
                got(2 * b2, t)
                got(2 * b2 + 1, t)
                yield

        def row_broadcast(dst, col_ap, reads, *after):
            n, nfree = scratch.take()
            for i in range(4):
                t = ts(pool, E[n][:, 128 * i:128 * (i + 1)], K("ident"), col_ap[:, i:i + 1], None, ALU.mult, None,
                       nfree, after)
            b, free = side.take()
            t = mm(ps[:, b, :], K("ones"), E[n][:, 0:512], True, True, t, free)
            scratch.put(n, t)
            t = cp(act, dst, ps[:, b, :], t, reads)
            side.put(b, t)
            return t


        X = XR["X"]
        start_sem = sem("start")
        load(act, PR[:, :], io["params"], start_sem)
        params = load(act, KC[:, :], io["const"], start_sem)
        x_sem = sem("x")
        for t2 in range(2):
            x_tok = load(act, X[:, t2, :], io["x_in"][128 * t2:128 * (t2 + 1), :], x_sem)
        more_loads()
        t0 = fill(dve, ps[:, 7, :], 0.0)
        fill(dve, BR[:, :], 0.0)
        for i in range(4):
            t = fill(dve, E[i][:, :], 0.0)
        ada["bank"] = [t0, t]
        cs_ready = fn(ACT.Silu, CS[:, :, :], P("c").rearrange("p (k c) -> p k c", k=16), params)

        x = P("logit")
        a_, e_, s_, s2, p_, m_ = (LG[:, i, :] for i in range(6))
        t = ts(dve, a_, x, -1.0, None, ALU.mult, None, params)
        t = tt(dve, a_, a_, x, ALU.max, t)
        te = fn(ACT.Exp, e_, a_, t, scale=-1.0)
        t = ts(dve, s_, e_, 2.0, None, ALU.add, None, te)
        t = recip(s_, s_, t)
        t = tt(dve, s_, s_, e_, ALU.mult, t)
        t = tt(dve, s2, s_, s_, ALU.mult, t)
        t = ts(dve, p_, s2, 1.0 / 19, None, ALU.mult, None, t)
        for k in range(8, 0, -1):
            t = stt(dve, p_, p_, 1.0 / (2 * k + 1), s2, ALU.add, ALU.mult, t)
        t = stt(dve, p_, p_, 1.0, s_, ALU.add, ALU.mult, t)
        tm = ts(dve, m_, x, -1.0, 0.0, ALU.mult, ALU.max)
        t = stt(dve, p_, p_, 2.0, m_, ALU.mult, ALU.add, t, tm)
        lg_ready = ts(dve, LG[:, 0, :], p_, -1.0, None, ALU.mult, None, t)

        def lgam(l, back, h):
            c = 16 * l + 8 * back + h
            return LG[:, 0, c:c + 1]

        W1, G, qT, kT, dec, nb, dft = (W[n] for n in ("W1", "G", "qT", "kT", "dec", "nb", "dft"))
        uT, PQ, acc, FX = HU["uT"], HU["PQ"], HU["acc"], HU["FX"]
        TQ, TK = three(W1[:, 0, 0:1024], 2), three(W1[:, 0, 1024:2048], 2)
        V0, V1 = three(W1[:, 1, 0:1024], 2), three(W1[:, 1, 1024:2048], 2)
        G0, G1 = G[:, 0], G[:, 1]
        dec_slots, nb_slots = Slots([0, 1]), Slots([0, 1])
        dft_sem, nb_sems = sem("dft"), [sem("nb0"), sem("nb1")]
        places = {n: [] for n in ("TQ", "TK", "V0", "V1", "G0", "G1", "qk", "uT", "PQ", "acc", "FX", "dft",
                                  "H0", "H1", "rn0", "rn1", "rn2", "X")}

        def own(*names):
            toks = [places[n] for n in names]
            assert None not in toks, names
            for n in names:
                places[n] = None
            return toks

        def give(name, *toks):
            places[name] = list(flat(toks))

        def own_when(*names):
            pump_until(lambda: not (any(places[n] is None for n in names)))
            return own(*names)

        def keep(dst, free, f=ACT.Copy):
            done = []

            def ev(i, o, t):
                done.append(fn(f, dst[:, i, :], o, t, free))
                return done[-1]
            return ev, done

        def rotate(dst, free):
            done = []

            def ev(i, o, t):
                s, sfree = scratch.take()
                o4 = o.rearrange("p (h x d) -> p h x d", h=8, x=2)
                s4 = E[s][:, 0:512].rearrange("p (h x d) -> p h x d", h=8, x=2)
                d4 = dst[:, i, :].rearrange("p (h x d) -> p h x d", h=8, x=2)
                a = tt(dve, d4, o4, bcast(K("cosr", 32 * i), (0, 8), (0, 2), (1, 32)), ALU.mult, t, free)
                for x in range(2):
                    sin = bcast(K("sinr", 64 * i + 32 * x), (0, 8), (1, 32))
                    e = tt(dve, s4[:, :, x, :], o4[:, :, 1 - x, :], sin, ALU.mult, sfree)
                r = tt(dve, dst[:, i, :], dst[:, i, :], E[s][:, 0:512], ALU.add, a, e)
                scratch.put(s, r)
                done.append(r)
                return e
            return ev, done

        def pair_transposed(q_tok, k_tok):
            while places["qk"] is None:
                yield
            free, n, got = own("qk"), 0, []
            for src, dst, tok, name in ((TQ, qT, q_tok, "TQ"), (TK, kT, k_tok, "TK")):
                for i in range(2):
                    b, bfree = side.take()
                    for pr in range(4):
                        tp = tr(ps[:, b, 128 * pr:128 * (pr + 1)], src[:, i, 128 * pr:128 * (pr + 1)], tok, bfree)
                    got.append(cp((act, dve)[n % 2], dst[:, :, 128 * i:128 * (i + 1)], three(ps[:, b, :], 4), tp, free))
                    n += 1
                    side.put(b, got[-1])
                    yield
                give(name, tp)
            return got

        def gate_transposed(gate, rn, *after):
            s, free = scratch.take()
            v = three(E[s][:, 0:256], 2)
            for i in range(2):
                t = tt(dve, three(v[:, i], 2), three(gate[:, i], 2), bcast(rn(i), (1, 2), (0, 64)), ALU.mult, after, free)
            yield
            b, free = side.take()
            for i in range(2):
                tp = tr(ps[:, b, 128 * i:128 * (i + 1)], v[:, i], t, free)
            scratch.put(s, tp)
            return b, tp, t

        def token_to_parts(src, src_tok, free, s_out, k0, o_tok):
            for b2 in range(2):
                b, bfree = side.take()
                for j in range(2):
                    for i in range(2):
                        c = 128 * (2 * b2 + j)
                        tp = tr(ps[:, b, 256 * j + 128 * i:256 * j + 128 * (i + 1)], src[:, i, c:c + 128],
                                src_tok, bfree)
                k = k0 + 2 * b2
                h, l = (p[:, s_out, k:k + 2, :] for p in (Hh, Hl))
                t = split(h, l, three(ps[:, b, :], 2), tp, free)
                side.put(b, t)
                o_tok[k] = o_tok[k + 1] = t
                yield
            return tp

        def layer1(l, x_ready):
            M = MOD[l % 2]
            hT, oT = 0, 1
            h_tok, o_tok, made = {}, {}, {}
            t = inv_rms([0, 1], 4, D, 0, x_ready)
            free = own("TQ", "TK", "V0", "V1")
            xn = [ts(dve, W1[:, i, :], X[:, i, :], ST[:, i:i + 1], None, ALU.mult, None, t, free) for i in range(2)]
            pump_until(lambda: not ((l, 3) not in mod_ready))
            hfree = own("H0")
            prep = feature_major(
                lambda i: W1[:, i, :], lambda k: (Hh[:, hT, k:k + 2, :], Hl[:, hT, k:k + 2, :]),
                lambda k: M[:, 1, k, 0:1], lambda k: M[:, 0, k, 0:1], NKT,
                lambda k: [xn, hfree, mod_ready[l, k // 4]], lambda k, t: h_tok.__setitem__(k, t))

            def need_h(k):
                while k not in h_tok or (k + 2 < NKT and k + 2 not in h_tok):
                    next(prep)
                return h_tok[k]

            def stat(s):
                return lambda k, i: [p[:, s, k, 128 * i:128 * (i + 1)] for p in (Hh, Hl)]

            def piece(ev, hooks={}):
                chunk_a(stat(hT), [0, 1], NKT, need_h, ev, hooks)

            def cw(ct, k):
                return P("conv", 136 * l + 34 * ct + k, 136 * l + 34 * ct + k + 1)

            ev, a_tok = keep(TQ, xn)
            piece(ev)
            u_tok = []

            def ev_b(i, o, t):
                t = fn(ACT.Sigmoid, TK[:, i, :], o, t)
                u_tok.append(tt(dve, TQ[:, i, :], TQ[:, i, :], TK[:, i, :], ALU.mult, t, a_tok[i]))
                return t

            piece(ev_b)
            give("V0")
            give("V1")

            def conv():
                free_u, free_a = own("uT", "PQ"), own("acc")
                t = fill(pool, uT[:, :, 0:15], 0.0, free_u)
                t = [t, fill(pool, uT[:, :, 271:286], 0.0)]
                for i in range(2):
                    b, free = side.take()
                    for ct in range(4):
                        tp = tr(ps[:, b, 128 * ct:128 * (ct + 1)], TQ[:, i, 128 * ct:128 * (ct + 1)], u_tok, free)
                    e = cp(dve, uT[:, :, 15 + 128 * i:15 + 128 * (i + 1)], three(ps[:, b, :], 4), tp, free_u)
                    side.put(b, e)
                    t.append(e)
                give("TQ", tp)
                give("TK", u_tok)
                last = [None] * 4
                for k in range(31):
                    for ct in range(4):
                        u, a = uT[:, ct, k:k + 256], acc[:, ct, :]
                        if k == 0:
                            last[ct] = ts(dve, a, u, cw(ct, 0), cw(ct, 31), ALU.mult, ALU.add, t, free_a)
                        else:
                            last[ct] = stt(dve, a, u, cw(ct, k), a, ALU.mult, ALU.add, last[ct])
                    yield
                yn = bcast(uT[:, 0, :], (512, 2), (1, 512))
                y_tok = []
                for i in range(2):
                    b, free = side.take()
                    for ct in range(4):
                        tp = tr(ps[:, b, 128 * ct:128 * (ct + 1)], acc[:, ct, 128 * i:128 * (i + 1)], last, free)
                    S, A, V, o = BN[:, i, 0:6], BN[:, i, 6:8], BN[:, i, 8:9], ps[:, b, :]
                    t = dve.do(lambda e, S=S, o=o: e.bn_stats(S, o), [tp])
                    t = dve.do(lambda e, S=S, A=A: e.bn_aggr(A, S), [t])
                    t = fn(ACT.Sqrt, V, BN[:, i, 7:8], t, bias=K("eps"))
                    t = recip(V, V, t)
                    t = ts(dve, yn[:, i, :], o, BN[:, i, 6:7], V, ALU.subtract, ALU.mult, t, last)
                    side.put(b, t)
                    y_tok.append(t)
                yield 1
                for b2 in range(2):
                    b, free = side.take()
                    for j in range(2):
                        c = 128 * (2 * b2 + j)
                        for i in range(2):
                            tp = tr(ps[:, b, 256 * j + 128 * i:256 * j + 128 * (i + 1)], yn[:, i, c:c + 128], y_tok, free)
                    for j in range(2):
                        ct = 2 * b2 + j
                        t = fn(ACT.Silu, acc[:, ct, :], ps[:, b, 256 * j:256 * (j + 1)], tp,
                               bias=cw(ct, 33), scale=cw(ct, 32))
                    side.put(b, t)
                    yield
                give("uT", tp)
                give("PQ", tp)
                made["s"] = t

            launch("conv", conv(), start=True)

            ev, rq = rotate(TQ, own("TQ"))
            piece(ev)
            ev, rk = rotate(TK, own("TK"))
            piece(ev)
            ev, rv = keep(V0, own("V0"))
            piece(ev)
            ev, rg = keep(G0, own("G0"), ACT.Silu)
            piece(ev)

            def retention():
                qk = yield from pair_transposed(rq, rk)
                ofree, rfree = own("FX", "rn0")
                oraw = bcast(FX[:, 0, :], (256, 4), (1, 256))
                oraw_tok, ss_tok, decs = [], [], {}

                def decay(h):
                    d, free = dec_slots.take()
                    c = dec[:, d, :]
                    t = ts(pool, c, K("dist_b"), lgam(l, 1, h), None, ALU.mult, None, lg_ready, free)
                    t = stt(dve, c, K("dist_f"), lgam(l, 0, h), c, ALU.mult, ALU.add, t)
                    decs[h] = (d, fn(ACT.Exp, c, c, t))

                decay(0)
                for pr in range(4):
                    ob, obfree = side.take()
                    for hh in range(2):
                        h, o = 2 * pr + hh, 64 * hh
                        if h < 7:
                            decay(h + 1)
                        b, free = side.take()
                        for jt in range(2):
                            t = mm(ps[:, b, 256 * (1 - jt):256 * (2 - jt)], kT[o:o + 64, pr, 128 * jt:128 * (jt + 1)],
                                   qT[o:o + 64, pr, :], True, True, qk, free)
                        s, sfree = scratch.take()
                        d, d_tok = decs.pop(h)
                        t = stt(dve, three(E[s][:, 0:512], 2), three(ps[:, b, :], 2), 0.125,
                                bcast(dec[:, d, :], (128, 2), (1, 256)), ALU.mult, ALU.mult, t, d_tok, sfree)
                        side.put(b, t)
                        dec_slots.put(d, t)
                        yield
                        for jt in range(2):
                            tp = mm(ps[o:o + 64, ob, 0:256], V0[:, jt, 64 * h:64 * (h + 1)],
                                    E[s][:, 256 * (1 - jt):256 * (2 - jt)], jt == 0, jt == 1, t, rv, obfree)
                        scratch.put(s, tp)
                    oraw_tok.append(cp(act, oraw[:, pr, :], ps[:, ob, 0:256], tp, ofree))
                    s, sfree = scratch.take()
                    t = fn(ACT.Square, E[s][:, 0:256], ps[:, ob, 0:256], sfree)
                    side.put(ob, t)
                    yield
                    b, free = side.take()
                    for i in range(2):
                        tp = mm(ps[:, b, 2 * i:2 * i + 2], E[s][:, 128 * i:128 * (i + 1)], K("hsel"), True, True, t, free)
                    scratch.put(s, tp)
                    ss_tok.append(cp(dve, bcast(RN[:, 0, 2 * pr:2 * pr + 1], (8, 2), (1, 2)), three(ps[:, b, 0:4], 2),
                                     tp, rfree))
                    side.put(b, ss_tok[-1])
                give("qk", tp)
                give("V0", tp)
                t = fn(ACT.Sqrt, RN[:, 0, :], RN[:, 0, :], ss_tok, bias=K("eps"), scale=1.0 / 64)
                rn_tok = recip(RN[:, 0, :], RN[:, 0, :], t)
                yield
                ofree = places["H1"]
                for pr in range(4):
                    b, tp, g = yield from gate_transposed(
                        G0[:, :, 128 * pr:128 * (pr + 1)], lambda i: RN[:, 0, 8 * i + 2 * pr:8 * i + 2 * pr + 2],
                        rn_tok, rg)
                    n, free = og.take()
                    t = tt(dve, OG[n][:, 0, :], ps[:, b, 0:256], oraw[:, pr, :], ALU.mult, tp, oraw_tok, free)
                    side.put(b, t)
                    fx = t
                    t = split(Hh[:, oT, pr, :], Hl[:, oT, pr, :], OG[n][:, 0, :], t, ofree)
                    og.put(n, t)
                    o_tok[pr] = t
                    yield
                give("G0", g)
                give("FX", fx)
                give("rn0", g)

            launch("ret", retention())

            ev, nq = keep(TQ, own_when("TQ"))
            piece(ev)
            ev, nk = keep(TK, own_when("TK"))
            piece(ev)
            ev, nv = keep(V1, own("V1"))
            piece(ev)
            ev, ng = keep(G1, own("G1"), ACT.Silu)
            piece(ev)

            def neighbours():
                qk = yield from pair_transposed(nq, nk)
                hfree = places["H1"]
                biases, mx_read = {}, {0: [], 1: []}

                def bias(h):
                    d, free = nb_slots.take()
                    t = load(sp, nb[:, d, :], io["na_bias"][l, h], nb_sems[d], free)
                    v = nb[:, d, :].rearrange("p (m c) -> p m c", m=6)
                    biases[h] = (d, tt(pool, v, v, bcast(K("mask"), (0, 6), (1, 64)), ALU.add, t))

                bias(0)
                for pr in range(4):
                    rn = f"rn{1 + pr % 2}"
                    rfree = own(rn)
                    ob, obfree = side.take()
                    c0, exps = 8 * (pr % 2), []
                    for hh in range(2):
                        h, o = 2 * pr + hh, 64 * hh
                        if h < 7:
                            bias(h + 1)
                        b, free = side.take()
                        for i in range(2):
                            t = mm(ps[:, b, 256 * (1 - i):256 * (2 - i)], qT[o:o + 64, pr, 128 * i:128 * (i + 1)],
                                   kT[o:o + 64, pr, :], True, True, qk, free)
                        s, sfree = scratch.take()
                        d, d_tok = biases.pop(h)
                        pm, mx = three(E[s][:, 0:512], 2), MX[:, hh, 0:2]
                        t = stt(dve, pm, three(ps[:, b, :], 2), 0.125, bcast(nb[:, d, :], (128, 2), (1, 256)),
                                ALU.mult, ALU.add, t, d_tok, sfree)
                        side.put(b, t)
                        nb_slots.put(d, t)
                        t = dve.do(lambda e, mx=mx, pm=pm: e.tensor_reduce(mx, pm, AX.X, ALU.max, negate=True),
                                   [t] + mx_read[hh])
                        for x in range(2):
                            c = c0 + 2 * (1 - x) + hh
                            t2 = fn(ACT.Exp, pm[:, x, :], pm[:, x, :], t, rfree, bias=mx[:, x:x + 1],
                                    accum_out=RN[:, 1, c:c + 1])
                        mx_read[hh] = [t2]
                        exps.append(t2)
                        yield
                        b, free = side.take()
                        for kt in range(2):
                            for i in range(2):
                                tp = tr(ps[:, b, 256 * kt + 128 * i:256 * kt + 128 * (i + 1)],
                                        pm[:, 1 - i, 128 * kt:128 * (kt + 1)], t2, free)
                        scratch.put(s, tp)
                        s, sfree = scratch.take()
                        t = cp((act, dve)[hh], E[s][:, 0:512], ps[:, b, :], tp, sfree)
                        side.put(b, t)
                        yield
                        for kt in range(2):
                            tp = mm(ps[o:o + 64, ob, 0:256], V1[:, kt, 64 * h:64 * (h + 1)],
                                    E[s][:, 256 * kt:256 * (kt + 1)], kt == 0, kt == 1, t, nv, obfree)
                        scratch.put(s, tp)
                    o_done = tp
                    r = RN[:, 1, c0:c0 + 4]
                    t = recip(r, r, exps)
                    b, tp, g = yield from gate_transposed(
                        G1[:, :, 128 * pr:128 * (pr + 1)], lambda i: RN[:, 1, c0 + 2 * i:c0 + 2 * i + 2], t, ng)
                    give(rn, g)
                    n, free = og.take()
                    t = cp(act, OG[n][:, 1, :], ps[:, b, 0:256], tp, free)
                    side.put(b, t)
                    t = tt(dve, OG[n][:, 0, :], ps[:, ob, 0:256], OG[n][:, 1, :], ALU.mult, t, o_done)
                    side.put(ob, t)
                    t = split(Hh[:, oT, 4 + pr, :], Hl[:, oT, 4 + pr, :], OG[n][:, 0, :], t, hfree)
                    og.put(n, t)
                    o_tok[4 + pr] = t
                    yield
                give("qk", pe.last)
                give("V1", o_done)
                give("G1", g)

            launch("na", neighbours())

            ev, fx = keep(FX, own_when("FX"))
            dft_tok = load(sp, dft[:, :, :], three(io["dft"], 2), dft_sem, places["dft"])
            piece(ev)

            def fourier():
                free = own_when("PQ")
                pq = []
                for g in range(4):
                    b, bfree = side.take()
                    for i in range(2):
                        tp = mm(ps[:, b, :], FX[:, i, 128 * g:128 * (g + 1)], dft[:, i, :], i == 0, i == 1,
                                fx, dft_tok, bfree)
                    pq.append(cp((act, dve)[g % 2], PQ[:, g, :], ps[:, b, :], tp, free))
                    side.put(b, pq[-1])
                    yield
                give("dft", tp)
                yf = bcast(FX[:, 0, :], (256, 4), (1, 256))
                for g2 in range(2):
                    b, bfree = side.take()
                    for g in (2 * g2, 2 * g2 + 1):
                        for x in range(2):
                            tq = mm(ps[:, b, 256 * (g % 2):256 * (g % 2 + 1)], K("cc", 128 * x, 128 * (x + 1)),
                                    PQ[:, g, 256 * x:256 * (x + 1)], x == 0, x == 1, pq, bfree)
                    t = cp(act, yf[:, 2 * g2:2 * g2 + 2, :], three(ps[:, b, :], 2), tq, tp)
                    side.put(b, t)
                    made["f", g2] = t
                    yield
                made["pq"] = tq
                made["y"] = t

            launch("fft", fourier())
            ev, cg = keep(G0, own_when("G0"), ACT.Silu)
            piece(ev)
            ev, fg = keep(V0, own_when("V0"), ACT.Silu)

            def parts_of(src, k0, name):
                def hook(tok):
                    pump_until(lambda: not (name not in made))
                    for j in (0, 2):
                        made[name, "parts", j] = split(Hh[:, hT, k0 + j:k0 + j + 2, :], Hl[:, hT, k0 + j:k0 + j + 2, :],
                                                       src[:, j:j + 2, :], made[name], tok)
                return hook

            yf = bcast(FX[:, 0, :], (256, 4), (1, 256))
            piece(ev, {1: parts_of(acc, 0, "s"), 3: parts_of(yf, 4, "y")})

            def gated_chunk(k0, name, dst, gate, gate_tok, free):
                o_done = []

                def ev(i, o, t):
                    o_done.append(tt(dve, dst[:, i, :], o, gate[:, i, :], ALU.mult, t, gate_tok, free))
                    return o_done[-1]
                chunk_a(lambda k, i: [p[:, hT, k0 + k, 128 * i:128 * (i + 1)] for p in (Hh, Hl)], [0, 1], 4,
                        lambda k: made[name, "parts", k // 2 * 2], ev)
                return o_done

            o_cv = gated_chunk(0, "s", TQ, G0, cg, own_when("TQ"))
            give("G0", o_cv)
            hfree = places["H1"]

            def cv_out():
                tp = yield from token_to_parts(TQ, o_cv, [hfree, made["pq"]], oT, 8, o_tok)
                give("TQ", tp)

            launch("cvo", cv_out())
            o_ff = gated_chunk(4, "y", TK, V0, fg, own_when("TK"))
            give("V0", o_ff)
            give("H0", pe.last)

            def ff_out():
                tp = yield from token_to_parts(TK, o_ff, hfree, oT, 12, o_tok)
                give("TK", tp)
                made["ffo"] = tp

            launch("ffo", ff_out())
            if l == 1:
                launch("ctx", context_prep())
                launch("fg", final_gain())

            def need_o(k):
                pump_until(lambda: not (k not in o_tok))
                return o_tok[k]

            pump_until(lambda: not ((l, 5) not in mod_ready))
            gb_read = [dve.last]
            x_tok = []
            for c in range(4):
                gb = {}

                def make_gate(_, c=c, gb=gb):
                    gb["t"] = row_broadcast(GB1[:, :], M[:, 2, 4 * c:4 * c + 4, 0], list(gb_read), mod_ready[l, 4 + c // 2])

                def ev(i, o, t, c=c, gb=gb):
                    s, free = scratch.take()
                    xs = X[:, i, 512 * c:512 * (c + 1)]
                    t = tt(dve, E[s][:, 0:512], o, GB1[:, :], ALU.mult, t, gb["t"], free)
                    gb_read[:] = [t]
                    a = tt(dve if c == 3 else pool, xs, xs, E[s][:, 0:512], ALU.add, t)
                    a = sums(xs, (i, c), E[s][:, 0:512], a)
                    scratch.put(s, a)
                    x_tok.append(a)
                    return t

                chunk_a(stat(oT), [0, 1], NKT, need_o, ev, {4: make_gate})
            mod_read[l % 2] = [dve.last, pool.last]
            for n in ("conv", "ret", "na", "fft", "cvo", "ffo"):
                assert all(s["name"] != n for s in sides), n
            give("H1", pe.last)
            for n in ("uT", "acc", "FX", "PQ"):
                give(n, pe.last)
            return x_tok

        YB, CT = W["YB"], W["CT"]
        h2 = {0: {}, 1: {}}
        ctx_sem, spill_sem, reload_sem, ct_sem = sem("ctx"), sem("spill"), sem("reload"), sem("ct")
        fg_made = {}

        def context_prep():
            names = ("TQ", "TK", "V0", "V1")
            while any(places[n] is None for n in names) or places["H0"] is None or (2, 0) not in mod_ready:
                yield
            free, hfree = own(*names), own("H0")
            for i in range(2):
                t = load(sp, W1[:, i, :], io["ctx_in"][128 * i:128 * (i + 1), :], ctx_sem, free)
            yield 3
            sq = []
            for i in range(2):
                for c in range(4):
                    n, nfree = scratch.take()
                    sq.append(sums(W1[:, i, 512 * c:512 * (c + 1)], (2 + i, c), E[n][:, 0:512], t, nfree))
                    scratch.put(n, sq[-1])
                yield
            t = inv_rms([2, 3], 4, D, 2, sq)
            xn = [ts(dve, W1[:, i, :], W1[:, i, :], ST[:, 2 + i:3 + i], None, ALU.mult, None, t) for i in range(2)]
            yield
            M = MOD[0]
            gen = feature_major(
                lambda i: W1[:, i, :], lambda k: (Hh[:, 0, k:k + 2, :], Hl[:, 0, k:k + 2, :]),
                lambda k: M[:, 1, k, 1:2], lambda k: M[:, 0, k, 1:2], NKT,
                lambda k: [xn, hfree, mod_ready[2, k // 4]], lambda k, t: h2[0].__setitem__(k, t))
            for b2 in range(8):
                while (2, b2 // 2) not in mod_ready:
                    yield
                next(gen)
                yield
            made = pe.last
            for n in names:
                give(n, made)

        def final_gain():
            while places["G0"] is None or places["G1"] is None:
                yield
            free = own("G0", "G1")
            for c in range(4):
                g = P("final_g", 4 * c, 4 * c + 4)
                fg_made[c] = row_broadcast(G[:, c // 2, c % 2, :], g, free)
                yield

        def latent_prep(s, src, src_tok, l, k_after):
            M = MOD[l % 2]
            c = 1 - s
            return feature_major(
                src, lambda k: (Hh[:, s, k:k + 2, :], Hl[:, s, k:k + 2, :]),
                lambda k: M[:, 1, k, c:c + 1], lambda k: M[:, 0, k, c:c + 1], NKT,
                lambda k: [src_tok, k_after, mod_ready[l, k // 4]], lambda k, t: h2[s].__setitem__(k, t))

        def layer2(x_tok):
            finish("ctx")
            finish("fg")
            t = inv_rms([0, 1], 4, D, 0, x_tok)
            xs, xn = [], []
            for i in range(2):
                FG = G[:, :, :, :].rearrange("p a b c -> p (a b c)")
                a = stt(dve, X[:, i, :], X[:, i, :], ST[:, i:i + 1], FG, ALU.mult, ALU.mult, t, list(fg_made.values()))
                xs.append(a)
                sq = []
                for c in range(4):
                    n, nfree = scratch.take()
                    sq.append(sums(X[:, i, 512 * c:512 * (c + 1)], (i, c), E[n][:, 0:512], a, nfree))
                    scratch.put(n, sq[-1])
                r = inv_rms([i], 4, D, 4 + i, sq)
                xn.append(ts(dve, YB[:, 2048 * i:2048 * (i + 1)], X[:, i, :], ST[:, 4 + i:5 + i], None, ALU.mult, None,
                             r, places["TQ"]))
            for i in range(2):
                spill = load(sp, out[128 * i:128 * (i + 1), :], X[:, i, :], spill_sem, xs[i])
            prep = latent_prep(1, lambda i: YB[:, 2048 * i:2048 * (i + 1)], xn, 2, places["H1"])

            def need_h(k):
                while k not in h2[1] or (k + 2 < NKT and k + 2 not in h2[1]):
                    next(prep)
                return [h2[0][k], h2[1][k]]

            PH, PL = XR["PH"], XR["PL"]
            for _ in range(4):
                scratch.take()
            z = [fill(dve, E[i][:, :], 0.0, act.last, pe.last) for i in range(2)]
            U = [three(E[i][:, :], 2) for i in range(4)]
            u_free = [[z[0]], [z[1]]]
            pt, y_tok, yt_tok = {}, {}, {}
            grp_read = [xn, xs]
            Yk = YB[:, :].rearrange("p (k s n) -> p k s n", k=16, s=2)

            def pooled(g, i):
                w, slot = WINDOWS[g], i % 2

                def ev(o, t):
                    A, B, u = U[2], U[3], U[slot]
                    t = cp(act, u[:, :, 8:264], o, t, u_free[slot])
                    ev_tok = t
                    a, b = 8 - 7, 8 + 263
                    if w == 2:
                        a, b = 8, 264
                    t = tt(dve, A[:, :, a:b], u[:, :, a - 1:b - 1], u[:, :, a:b], ALU.add, t, scr_free)
                    cur, other, shift, width = A, B, 1, 2
                    while width < w:
                        width *= 2
                        shift = width // 4
                        a, b = (8, 264) if width == w else (a + shift, b - shift)
                        t = tt(dve, other[:, :, a:b], cur[:, :, a - shift:b - shift], cur[:, :, a + shift:b + shift],
                               ALU.add, t)
                        cur, other = other, cur
                    ed = bcast(cur[:, 0, 8:9], (272, 2), (248, 2), (1, 8))
                    t = tt(dve, ed, ed, bcast(K("edge", 16 * g), (0, 2), (8, 2), (1, 8)), ALU.mult, t)
                    n, nfree = og.take()
                    t = stt(dve, OG[n][:, :, :], cur[:, :, 8:264], 1.0 / w, u[:, :, 8:264], ALU.mult, ALU.subtract,
                            t, nfree)
                    u_free[slot] = [t]
                    scr_free[:] = [t]
                    t = split(three(PH[:, i, :], 2), three(PL[:, i, :], 2), OG[n][:, :, :], t, list(grp_read), spill)
                    og.put(n, t)
                    pt[i] = t
                    return ev_tok
                return ev

            scr_free = []

            def gate_ev(k):
                def ev(o, t):
                    t = fn(ACT.Silu, Yk[:, k], o, t, xn_read)
                    y_tok[k] = ts(pool, Yk[:, k], Yk[:, k], P("p_scale", k, k + 1), None, ALU.mult, None, t)
                    return t
                return ev

            def grp_ev(k):
                def ev(o, t):
                    yt_tok[k] = stt(dve, Yk[:, k], o, P("b_grp", k, k + 1), Yk[:, k], ALU.add, ALU.mult, t, y_tok[k])
                    return yt_tok[k]
                return ev

            def bank(b):
                return three(ps[:, b, :], 2)

            def rhs(k):
                return [p[:, :, k, :] for p in (Hh, Hl)]

            xn_read = None
            for g in range(4):
                for i in range(4):
                    b_tile(rhs, bank, need_h, pooled(g, i))
                    if xn_read is None:
                        xn_read = [pe.last]
                for i in range(4):
                    b_tile(rhs, bank, need_h, gate_ev(4 * g + i))
                h_read = pe.last
                for half in range(2):
                    jobs = []
                    for i in (2 * half, 2 * half + 1):
                        jobs.append((lambda k: [three(PH[:, k, :], 2), three(PL[:, k, :], 2)], bank,
                                     lambda k: pt[k], grp_ev(4 * g + i)))
                    b_half(jobs)
                    if g == 3 and half == 0:
                        early = y_parts(range(12), yt_tok, h_read, Yk)
                    pump()
                grp_read[:] = [pe.last]
            rest = y_parts(range(12, 16), yt_tok, h_read, Yk)
            parts = {**early, **rest}
            for i in range(4):
                scratch.put(i, [dve.last, act.last])

            for b in (4, 5):
                pair = [f for f in side.free if f[0] == b]
                assert pair
                side.free.remove(pair[0])
                main.free.append(pair[0])
            Y = YB[:, :].rearrange("p (t n) -> p t n", t=4)
            M = MOD[0]
            tiles = [(1, 0), (1, 1), (0, 0), (0, 1)]
            pump_until(lambda: not ((2, 5) not in mod_ready))
            for i in range(2):
                reload = load(sp, X[:, i, :], out[128 * i:128 * (i + 1), :], reload_sem, grp_read, spill)
            ct0 = load(sp, CT[:, :], io["ctx_in"][0:128, :], ct_sem, pe.last)
            GB2 = [W["GB0"], GB1]
            gb_read = {0: [pe.last], 1: [dve.last]}
            sq, yg = {}, {}
            for c in range(4):
                gb = {}

                def make_gate(_, s, c=c, gb=gb):
                    gb[s] = row_broadcast(GB2[s][:, :], M[:, 2, 4 * c:4 * c + 4, 1 - s], list(gb_read[s]),
                                          mod_ready[2, 4 + c // 2])

                def ev(n, o, t, c=c, gb=gb):
                    s, i = tiles[n]
                    j = 2 * s + i
                    e, efree = scratch.take()
                    t = sums(o, (j, c), E[e][:, 0:512], t, efree)
                    scratch.put(e, t)
                    sq[j, c] = t
                    t = tt(dve, Y[:, j, 512 * c:512 * (c + 1)], o, GB2[s][:, :], ALU.mult, t, gb[s])
                    gb_read[s] = [t]
                    yg[j, c] = t
                    return t

                chunk_a(lambda k, t: [p[:, t[0], k, 128 * t[1]:128 * (t[1] + 1)] for p in (Hh, Hl)], tiles, NKT,
                        lambda k: parts[k], ev,
                        {4: lambda _: make_gate(_, 1), 5: lambda _: make_gate(_, 0)})
            mod_read[0] = [dve.last, pool.last]
            for b in (4, 5):
                pair = [f for f in main.free if f[0] == b]
                assert pair
                main.free.remove(pair[0])
                side.free.append(pair[0])
            y_read = pe.last

            prep = {}
            spilled = []
            xn3 = {0: [], 1: []}
            ct_tok = ct0
            for s, i in tiles:
                j = 2 * s + i
                r = inv_rms([j], 4, D, 8 + j, [sq[j, c] for c in range(4)])
                dst = X[:, i, :] if s == 1 else CT[:, :]
                t = stt(dve, dst, Y[:, j, :], ST[:, 8 + j:9 + j], dst, ALU.mult, ALU.add, r, yg[j, 3],
                        reload if s == 1 else ct_tok)
                if s == 1:
                    spilled.append(t)
                q = []
                for c in range(4):
                    e, efree = scratch.take()
                    q.append(sums(dst[:, 512 * c:512 * (c + 1)], (j, c), E[e][:, 0:512], t, efree))
                    scratch.put(e, q[-1])
                r = inv_rms([j], 4, D, 12 + j, q)
                t = ts(dve, Y[:, j, :], dst, ST[:, 12 + j:13 + j], None, ALU.mult, None, r)
                xn3[s].append(t)
                if s == 0 and i == 0:
                    ct_tok = load(sp, CT[:, :], io["ctx_in"][128:256, :], ct_sem, t, q)
            for i in range(2):
                sp3 = load(sp, out[128 * i:128 * (i + 1), :], X[:, i, :], spill_sem, spilled[i], reload)
            for s in (0, 1):
                h2[s].clear()
                prep[s] = latent_prep(s, lambda i, s=s: Y[:, 2 * s + i, :], xn3[s], 3, y_read)
            return prep, sp3, xn3

        def y_parts(ks, yt_tok, h_read, Yk):
            return {k: split(Hh[:, :, k, :], Hl[:, :, k, :], Yk[:, k], yt_tok[k], h_read) for k in ks}

        def layer3(prep, spill, xn3):
            cqT, ckT = [W["cqT_h"], W["cqT_l"]], [W["ckT_h"], W["ckT_l"]]
            kr = [W["kr_h"], W["kr_l"]]
            cq, ckv, RT = W["cq"], W["ckv"], W["rope"]
            V, Pm, PT = HU["V"], HU["Pm"], HU["PT"]
            qr = [HU["qr_h"], HU["qr_l"]]
            rope_sem = sem("rope")
            rope_tok = load(sp, RT[:, :], io["rope"], rope_sem, pe.last)

            def need(s):
                def f(k):
                    while k not in h2[s] or (k + 2 < NKT and k + 2 not in h2[s]):
                        next(prep[s])
                    return h2[s][k]
                return f

            def stat(k, t):
                return [p[:, t[0], k, 128 * t[1]:128 * (t[1] + 1)] for p in (Hh, Hl)]

            def low_rank(dst, sq, done, row):
                def ev(n, o, t):
                    done.append(fn(ACT.Copy, dst[:, n, :], o, t))
                    e, efree = scratch.take()
                    t = sums(o, (n, row), E[e][:, 0:512], t, efree)
                    scratch.put(e, t)
                    sq.append(t)
                    return t
                return ev

            cq_tok, cq_sq, ck_tok, ck_sq = [], [], [], []
            lat = [(1, 0), (1, 1)]
            keys = [(0, 0), (0, 1), (1, 0), (1, 1)]
            chunk_a(stat, lat, NKT, need(1), low_rank(cq, cq_sq, cq_tok, 0))

            def normed(name, src, tok, sq, tiles, col, mul, dst, width, row):
                o = ST[:, col:col + tiles]
                t = cp(dve, o, SS[:, 0:tiles, row], sq)
                t = fn(ACT.Sqrt, o, o, t, bias=K("eps"), scale=1.0 / 512)
                t = recip(o, o, t)
                nt = [ts(dve, src[:, i, :], src[:, i, :], ST[:, col + i:col + i + 1], None, ALU.mult, None, t, tok)
                      for i in range(tiles)]
                yield
                per = 512 // width
                for b2 in range(4 // per):
                    b, free = side.take()
                    for j in range(per):
                        k = per * b2 + j
                        for i in range(tiles):
                            tp = tr(ps[:, b, width * j + 128 * i:width * j + 128 * (i + 1)],
                                    src[:, i, 128 * k:128 * (k + 1)], nt, free)
                    n, nfree = og.take()
                    flat_og = OG[n][:, :, :].rearrange("p a b -> p (a b)")
                    for j in range(per):
                        k = per * b2 + j
                        e = ts(dve, flat_og[:, width * j:width * (j + 1)], ps[:, b, width * j:width * (j + 1)],
                               mul(k), None, ALU.mult, None, tp, nfree)
                    side.put(b, e)
                    k = per * b2
                    v = flat_og if per == 1 else OG[n][:, :, :]
                    h, l = (p[:, k, :] if per == 1 else p[:, k:k + 2, :] for p in dst)
                    t = split(h, l, v, e, xn3[0], pe.last)
                    og.put(n, t)
                    for j in range(per):
                        done[name, k + j] = t
                    yield

            done = {}
            for k in range(0, NKT, 2):
                need(0)(k)
            launch("cq", normed("cq", cq, cq_tok, cq_sq, 2, 0, lambda k: P("q_norm", k, k + 1), cqT, 256, 0))
            chunk_a(stat, keys, NKT, lambda k: [need(0)(k), need(1)(k)], low_rank(ckv, ck_sq, ck_tok, 1))
            launch("ckv", normed("ck", ckv, ck_tok, ck_sq, 4, 4, lambda k: P("kv_norm", k, k + 1), ckT, 512, 1))

            def turned(o, t, dst, free):
                s, sfree = scratch.take()
                v = E[s]
                t = cp(act, v[:, 0:256], o, t, sfree)
                bank_free = t
                yield bank_free
                b, bfree = side.take()
                tp = mm(ps[:, b, 0:256], RT[:, 512:640], v[:, 0:256], True, True, t, bfree, rope_tok)
                a = tt(dve, v[:, 256:512], ps[:, b, 0:256], RT[:, 256:512], ALU.mult, tp)
                side.put(b, a)
                c = tt(dve, v[:, 0:256], v[:, 0:256], RT[:, 0:256], ALU.mult, a)
                c = tt(dve, v[:, 0:256], v[:, 0:256], v[:, 256:512], ALU.add, c)
                t = split(dst[0], dst[1], v[:, 0:256], c, free)
                scratch.put(s, t)
                yield t

            kr_tok = {}

            def kr_ev(o, t):
                t1 = split(kr[0][:, 0:256], kr[1][:, 0:256], o[:, 0, :], t)
                kr_tok[0] = t1
                g = turned(o[:, 1, :], t1, [p[:, 256:512] for p in kr], None)
                t2 = next(g)

                def rest():
                    kr_tok[1] = next(g)
                    yield
                launch("kr", rest())
                return [t1, t2]

            b_tile(lambda k: [p[:, :, k, :] for p in (Hh, Hl)], lambda b: three(ps[:, b, :], 2),
                   lambda k: [h2[0][k], h2[1][k]], kr_ev)
            GX = X
            g_tok = {}
            for c in range(4):
                def ev(n, o, t, c=c):
                    t = fn(ACT.Silu, GX[:, n, 512 * c:512 * (c + 1)], o, t, spill)
                    g_tok[c, n] = t
                    return t
                chunk_a(stat, lat, NKT, need(1), ev)
            for n in ("cq", "ckv", "kr"):
                finish(n)
            h_read = pe.last

            qn = [[W[f"qn_h{i}"], W[f"qn_l{i}"]] for i in range(2)]
            kn = [[W[f"kn_h{i}"], W[f"kn_l{i}"]] for i in range(2)]
            scores_read = {i: [pe.last, dve.last, act.last] for i in range(2)}
            qr_read, v_read = [h_read], {0: [h_read], 1: [h_read]}
            qr_tok, v_tok, qk_tok, o_tok = {}, {}, {}, {}
            pm_free, pt_free = [h_read], [h_read]
            pending = {}

            def scores(h):
                r, o = h % 2, 64 * (h % 2)
                pr = h // 2 % 4
                rn = RN[:, r, 0:2]
                exps = []
                for i in range(2):
                    b, free = side.take()
                    q, k = [p[:, 128 * i:128 * (i + 1)] for p in qn[r]], [p[:, :] for p in kn[r]]
                    mm3(ps[:, b, :], q, k, True, False, qk_tok[h], free)
                    q, k = [p[o:o + 64, pr, 128 * i:128 * (i + 1)] for p in qr], [p[o:o + 64, :] for p in kr]
                    t = mm3(ps[:, b, :], q, k, False, True, qr_tok[h // 2], list(kr_tok.values()))
                    last = t
                    mx, o_ = MX[:, r, 2 * i:2 * i + 1], ps[:, b, :]
                    t = dve.do(lambda e, mx=mx, o_=o_: e.tensor_reduce(mx, o_, AX.X, ALU.max), [t, mx_free[r]])
                    mn = MX[:, r, 2 * i + 1:2 * i + 2]
                    t = ts(dve, mn, mx, -MLA_SCALE, None, ALU.mult, None, t)
                    t = fn(ACT.Exp, Pm[:, i, :], o_, t, pm_free, rn_free[r], bias=mn, scale=MLA_SCALE,
                           accum_out=RN[:, r, i:i + 1])
                    side.put(b, t)
                    exps.append(t)
                mx_free[r] = exps[-1]
                scores_read[r] = [last]
                pending[h] = exps
                pending[h, "rn"] = recip(rn, rn, exps)

            def transposes(h):
                r = h % 2
                t = pending[h]
                g = []
                for i in range(2):
                    b, free = side.take()
                    for kt in range(4):
                        tp = tr(ps[:, b, 128 * kt:128 * (kt + 1)], Pm[:, i, 128 * kt:128 * (kt + 1)], t, free)
                    g.append(cp((act, dve)[i], PT[:, :, 128 * i:128 * (i + 1)], three(ps[:, b, :], 4), tp, pt_free))
                    side.put(b, g[-1])
                pm_free[:] = [tp]
                pending[h] = g
                s, free = scratch.take()
                v = three(E[s][:, 0:256], 2)
                for i in range(2):
                    t = ts(dve, v[:, i], GX[:, i, 128 * h:128 * (h + 1)], RN[:, r, i:i + 1], None, ALU.mult, None,
                           pending[h, "rn"], [g_tok[h // 4, i]], free)
                rn_free[r] = [t]
                pending[h, "gate"] = (s, t)

            def values(h):
                s, t = pending[h, "gate"]
                b, free = side.take()
                v = three(E[s][:, 0:256], 2)
                for i in range(2):
                    tp = tr(ps[:, b, 128 * i:128 * (i + 1)], v[:, i], t, free)
                n, nfree = og.take()
                g = cp(act, OG[n][:, 1, :], ps[:, b, 0:256], tp, nfree)
                scratch.put(s, tp)
                side.put(b, g)
                b, free = side.take()
                for kt in range(4):
                    tp = mm(ps[:, b, 0:256], V[:, h // 4 % 2, kt, 128 * (h % 4):128 * (h % 4 + 1)], PT[:, kt, :],
                            kt == 0, kt == 3, pending[h], v_tok[h // 4], free)
                pt_free[:] = [tp]
                v_read[h // 4 % 2] = [tp]
                t = tt(dve, OG[n][:, 0, :], ps[:, b, 0:256], OG[n][:, 1, :], ALU.mult, tp, g)
                side.put(b, t)
                t = split(Hh[:, 0, h, :], Hl[:, 0, h, :], OG[n][:, 0, :], t, h_read)
                og.put(n, t)
                o_tok[h] = t

            mx_free, rn_free = {0: None, 1: None}, {0: None, 1: None}
            assert (3, 5) in mod_ready
            side.put(7, ada["bank"])
            def attend(h):
                if h in attended:
                    return
                attended.add(h)
                if h >= 2:
                    transposes(h - 2)
                if 1 <= h <= 16:
                    scores(h - 1)
                if h >= 2:
                    values(h - 2)

            def q_bank(b):
                return ps[:, b, 0:256]

            def q_stat(k):
                return [p[:, k, :] for p in cqT]

            def q_need(k):
                return done["cq", k]

            def k_stat(k):
                return [p[:, k, :] for p in ckT]

            def k_need(k):
                return done["ck", k]

            attended = set()
            for g in range(4):
                def v_ev(n, o, t, g=g):
                    t = fn(ACT.Copy, V[:, g % 2, n, :], o, t, v_read[g % 2])
                    v_tok.setdefault(g, []).append(t)
                    return t

                chunk_a(lambda k, t: [p[:, k, 256 * t[0] + 128 * t[1]:256 * t[0] + 128 * (t[1] + 1)] for p in ckT],
                        keys, 4, k_need, v_ev)
                if g > 0:
                    attend(4 * g)
                if g % 2 == 0:
                    qr_read = [pe.last]
                    for half in range(2):
                        jobs, gens = [], []
                        for i in (2 * half, 2 * half + 1):
                            def ev(o, t, i=i):
                                gen = turned(o, t, [p[:, i, :] for p in qr], qr_read)
                                gens.append((i, gen))
                                return next(gen)
                            jobs.append((q_stat, q_bank, q_need, ev))
                        b_half(jobs)
                        for i, gen in gens:
                            qr_tok[2 * g + i] = next(gen)
                for j in range(4):
                    h = 4 * g + j

                    def part_ev(dst, h=h):
                        def ev(o, t):
                            t = split(dst[0][:, :], dst[1][:, :], o, t, scores_read[h % 2])
                            qk_tok.setdefault(h, []).append(t)
                            return t
                        return ev
                    b_half([(q_stat, q_bank, q_need, part_ev(qn[h % 2])),
                            (k_stat, lambda b: ps[:, b, :], k_need, part_ev(kn[h % 2]))])
                    attend(h)
            attend(16)
            attend(17)

            Y = W["Y2"]
            M = MOD[1]
            for i in range(2):
                reload = load(sp, X[:, i, :], out[128 * i:128 * (i + 1), :], reload_sem, dve.last, spill)
            gb_read, sq, yg = [dve.last], {}, {}
            for c in range(4):
                gb = {}

                def make_gate(_, c=c, gb=gb):
                    gb["t"] = row_broadcast(GB1[:, :], M[:, 2, 4 * c:4 * c + 4, 0], list(gb_read),
                                            mod_ready[3, 4 + c // 2])

                def ev(n, o, t, c=c, gb=gb):
                    e, efree = scratch.take()
                    t = sums(o, (n, c), E[e][:, 0:512], t, efree)
                    scratch.put(e, t)
                    sq[n, c] = t
                    t = tt(dve, Y[:, n, 512 * c:512 * (c + 1)], o, GB1[:, :], ALU.mult, t, gb["t"])
                    gb_read[:] = [t]
                    yg[n, c] = t
                    return t

                chunk_a(lambda k, t: [p[:, 0, k, 128 * t[1]:128 * (t[1] + 1)] for p in (Hh, Hl)], lat, NKT,
                        lambda k: o_tok[k], ev, {4: make_gate})
            for i in range(2):
                r = inv_rms([i], 4, D, 8 + i, [sq[i, c] for c in range(4)])
                t = stt(dve, X[:, i, :], Y[:, i, :], ST[:, 8 + i:9 + i], X[:, i, :], ALU.mult, ALU.add, r, yg[i, 3], reload)
                o_done = load(sp, out[128 * i:128 * (i + 1), :], X[:, i, :], spill_sem, t)
            sp.do(lambda e: None, [o_done])

        x_sums = []
        for i in range(2):
            for c in range(4):
                n, free = scratch.take()
                x_sums.append(sums(X[:, i, 512 * c:512 * (c + 1)], (i, c), E[n][:, 0:512], x_tok, free))
                scratch.put(n, x_sums[-1])
        x_tok = x_sums
        work_off_ada()
        if upto is None or upto > 0:
            x_tok = layer1(0, x_tok)
        if upto is None or upto > 1:
            x_tok = layer1(1, x_tok)
        if upto is None or upto > 2:
            prep, sp3, xn3 = layer2(x_tok)
        if upto is None:
            layer3(prep, sp3, xn3)
        if upto is not None:
            sp.do(lambda e: None, st["loaded"][-NR:] + ([sp3] if upto > 2 else []))
        for q in (pe, act, dve, pool, sp):
            q.number()
        block = ctx.enter_context(nc.Block())

        @block.sync
        def _(e):
            sp.play(e)

        @block.scalar
        def _(e):
            act.play(e)

        @block.tensor
        def _(e):
            pe.play(e)

        @block.vector
        def _(e):
            dve.play(e)

        @block.gpsimd
        def _(e):
            pool.play(e)


def kernel(**inputs):
    import concourse.bacc as _bacc
    from concourse.bass_utils import run_bass_kernel_spmd as _run

    arrays = lay_out({n: np.asarray(a) for n, a in inputs.items()})
    nc = _bacc.Bacc("TRN2", target_bir_lowering=False, num_devices=1)
    io = {n: nc.dram_tensor("in_" + n, a.shape, mybir.dt.from_np(a.dtype), kind="ExternalInput").ap()
          for n, a in arrays.items()}
    out = nc.dram_tensor("out_x", (256, 2048), F, kind="ExternalOutput").ap()
    program(nc, io, out)
    r = _run(nc, [{"in_" + n: a for n, a in arrays.items()}], core_ids=[0])
    return r.results[0]["out_x"].reshape(1, 256, 2048)
```

```python
import concourse.bass as bass
from concourse import mybir
from contextlib import ExitStack
import numpy as np

F = mybir.dt.float32
R = mybir.dt.float32r
ACT = mybir.ActivationFunctionType
ALU = mybir.AluOpType
AX = mybir.AxisListType

D = 2048
NKT = 16
EPS = 1e-6
MASKED = -1.0e30
MLA_SCALE = (128 + 64) ** -0.5
WINDOWS = (2, 4, 8, 16)
PIECES = ["f_x", "f_g", "na_q", "na_k", "na_v", "na_g", "r_q", "r_k", "r_v", "r_g",
          "cv_a", "cv_b", "cv_g"]
ORDER = ["cv_a", "cv_b", "na_v", "na_q", "na_k", "na_g", "r_v", "r_q", "r_k", "r_g",
         "f_x", "cv_g", "f_g"]
OUT_ORDER = ["na", "ret", "cv", "fft"]
CONCAT = ["fft", "na", "ret", "cv"]

CONST_COLS = {}


def _const_columns():
    at = 0
    for name, n in [("ident", 128), ("ones", 128), ("cc", 256), ("dist_f", 384), ("dist_b", 384),
                    ("sel", 4), ("hsel", 2), ("cosr", 64), ("sinr", 128), ("mask", 64),
                    ("eps", 1), ("edge", 64)]:
        CONST_COLS[name] = (at, at + n)
        at += n
    return at


NCONST = _const_columns()


def constants():
    k = np.zeros((128, NCONST), np.float64)

    def put(name, a):
        lo, hi = CONST_COLS[name]
        k[:, lo:hi] = np.asarray(a).reshape(128, hi - lo)

    p = np.arange(128)
    put("ident", np.eye(128))
    put("ones", np.ones((128, 128)))
    ang = 2 * np.pi * ((p[:, None] * p[None, :]) % 128) / 128
    norm = 1.0 / np.sqrt(256 * 128)
    put("cc", np.concatenate([np.cos(ang) * norm, -np.sin(ang) * norm], axis=1))
    m = np.arange(384)[None, :] - 128 - p[:, None]
    put("dist_f", np.maximum(m, 0))
    put("dist_b", np.maximum(-m, 0))
    sel = np.zeros((128, 4))
    for i, rows in enumerate([(0, 64), (1, 65), (32, 96), (33, 97)]):
        sel[list(rows), i] = 1
    put("sel", sel)
    put("hsel", np.stack([p < 64, p >= 64], axis=1))
    inv = 10000.0 ** (-np.arange(32, dtype=np.float32) / np.float32(32))
    tok = np.arange(2)[None, :, None] * 128 + p[:, None, None]
    a = (tok.astype(np.float32) * inv.astype(np.float32)[None, None, :]).astype(np.float64)
    put("cosr", np.cos(a))
    put("sinr", np.stack([-np.sin(a), np.sin(a)], axis=2))
    col = p % 64
    start = np.clip(col - 8, 0, 48)
    rel = np.arange(64)[None, :] - start[:, None]
    put("mask", np.where((rel >= 0) & (rel < 16), 0.0, MASKED))
    put("eps", np.full((128, 1), EPS))
    edge = np.ones((4, 2, 8))
    for g, w in enumerate(WINDOWS):
        left, right = w // 2, w - 1 - w // 2
        for side, t0 in enumerate((0, 248)):
            for i in range(8):
                t = t0 + i
                cnt = min(t + right + 1, 256) - max(t - left, 0)
                edge[g, side, i] = w / cnt
    put("edge", np.broadcast_to(edge.reshape(1, 64), (128, 64)))
    return k.astype(np.float32)


def dft_tokens():
    n = np.arange(256)
    ang = 2 * np.pi * ((n[:, None] * n[None, :]) % 256) / 256
    t = np.concatenate([np.cos(ang), np.sin(ang)], axis=1)
    return np.ascontiguousarray(t.reshape(2, 128, 512).transpose(1, 0, 2)).reshape(128, 1024).astype(np.float32)


def rope_tables():
    d = np.arange(128) % 64
    n = np.arange(256)
    freqs = (10000.0 ** (-np.arange(16, dtype=np.float32) / np.float32(16))).astype(np.float32)
    pos = np.where((d < 32)[:, None], (n // 64)[None, :], (n % 64)[None, :]).astype(np.float32)
    ang = (pos * freqs[d % 16][:, None]).astype(np.float32).astype(np.float64)
    sign = np.where(d % 32 < 16, -1.0, 1.0)[:, None]
    swap = np.zeros((128, 128))
    i = np.arange(128)
    swap[i ^ 16, i] = 1
    return np.concatenate([np.cos(ang), np.sin(ang) * sign, swap], axis=1).astype(np.float32)


def pack_a(w):
    k, n = w.shape
    t = w.reshape(k // 512, 4, 128, n // 512, 512).transpose(3, 0, 2, 1, 4)
    return np.ascontiguousarray(t).reshape(n // 512, k // 512, 128, 2048)


def pack_b(w):
    k, n = w.shape
    t = w.reshape(16, 128, n // 128, 128).transpose(2, 1, 0, 3)
    return np.ascontiguousarray(t).reshape(n // 128, 128, 2048)


def pack_b4(w):
    t = w.reshape(4, 128, w.shape[1] // 512, 4, 128).transpose(2, 1, 3, 0, 4)
    return np.ascontiguousarray(t).reshape(w.shape[1] // 512, 128, 2048)


def pack_ada(w):
    t = w.reshape(8, 2, 128, 3, 4, 512)
    mod = t[:, :, :, 0:2].transpose(4, 0, 2, 1, 3, 5)
    gate = t[:, :, :, 2].reshape(8, 2, 128, 2, 2, 512).transpose(3, 0, 2, 1, 4, 5)
    return np.concatenate([mod.reshape(4, 8, 128, 2048), gate.reshape(2, 8, 128, 2048)])


def pack_ada_bias(b):
    t = b.reshape(3, 4, 512)
    jobs = [(t[0, j], t[1, j]) for j in range(4)] + [(t[2, 0], t[2, 1]), (t[2, 2], t[2, 3])]
    return np.stack([np.stack([a, a, c, c]) for a, c in jobs])


def cols(v):
    return np.asarray(v).reshape(-1, 128).T


PARAM_COLS = {}


def _param_columns():
    at = 0
    for name, n in [("norm_g", 32), ("conv", 272), ("logit", 32), ("final_g", 16), ("pre", 32), ("post", 32),
                    ("b_grp", 16), ("p_scale", 16), ("q_norm", 4), ("kv_norm", 4), ("c", 48)]:
        PARAM_COLS[name] = (at, at + n)
        at += n
    return at


NPARAM = _param_columns()


def lay_out(i):
    o = {}
    o["x_in"] = i["x"][0]
    o["ctx_in"] = i["ctx_2"][0]
    out_rows = [CONCAT.index(n) for n in OUT_ORDER]
    o["w_ada"] = np.stack([pack_ada(w) for w in i["w_ada"]] + [pack_ada(w) for w in i["ada_w_2"]])
    o["b_ada"] = np.stack([pack_ada_bias(b) for b in i["b_ada"]] + [pack_ada_bias(b) for b in i["ada_b_2"]])
    o["w_in"] = np.stack([pack_a(w) for w in i["w_in"]])
    o["w_fft"] = np.stack([pack_a(w) for w in i["w_fft"]])
    o["w_pw"] = np.stack([pack_a(w) for w in i["conv_w_pw"]])
    o["w_out"] = np.stack([pack_a(w.reshape(4, 512, 2048)[out_rows].reshape(2048, 2048)) for w in i["w_out"]])
    conv = np.concatenate([i["conv_w"], i["conv_b"][:, None], i["conv_ln_g"][:, None], i["conv_ln_b"][:, None]], axis=1)
    conv = conv.reshape(2, 34, 4, 128).transpose(3, 0, 2, 1).reshape(128, 272)
    logit = np.stack([i["ret_logit_fwd"], i["ret_logit_bwd"]], axis=1).reshape(1, 32)
    c = np.stack([cols(i["c"][0]), cols(i["c_2"][0]), cols(i["c_ctx_2"])], axis=2).reshape(128, 48)
    parts = {"norm_g": cols(i["norm_g"]), "conv": conv, "logit": np.broadcast_to(logit, (128, 32)),
             "final_g": cols(i["final_g"]), "pre": cols(i["pre_norm_2"]), "post": cols(i["post_norm_2"]),
             "b_grp": cols(i["pool_b_grp_2"]), "p_scale": cols(i["pool_scale_2"]),
             "q_norm": cols(i["mla_q_norm_2"]), "kv_norm": cols(i["mla_kv_norm_2"]), "c": c}
    o["params"] = np.concatenate([parts[n] for n in PARAM_COLS], axis=1)
    t = np.pad(i["na_rel_bias"], ((0, 0), (0, 0), (0, 0), (48, 48)))
    half, cc = np.arange(128)[:, None, None] // 64, np.arange(128)[:, None, None] % 64
    m, c2 = np.arange(6)[None, :, None], np.arange(64)[None, None, :]
    o["na_bias"] = np.ascontiguousarray(t[:, :, m + 5 - half, c2 - cc + 63]).reshape(2, 8, 128, 384)
    o["pool_in"] = pack_b(i["pool_w_in_2"][0])
    o["pool_grp"] = np.concatenate([pack_b4(w) for w in i["pool_w_grp_2"][0]])
    o["pool_out"] = pack_a(i["pool_w_out_2"][0])
    w = i["mla_w_in_2"][0]
    o["mla_in"] = pack_a(np.concatenate([w[:, :1024], w[:, 1088:]], axis=1))
    o["mla_kr"] = pack_b(np.concatenate([w[:, 1024:1088]] * 2, axis=1))
    uq = i["mla_w_uq_2"][0].reshape(512, 16, 192)
    ukv = i["mla_w_ukv_2"][0].reshape(512, 16, 256)
    qk = np.stack([uq[:, :, :128], ukv[:, :, :128]], axis=2).reshape(4, 128, 8, 2, 2, 128)
    o["mla_qk"] = np.ascontiguousarray(qk.transpose(2, 1, 3, 4, 0, 5)).reshape(8, 128, 2048)
    o["mla_rope"] = pack_b4(np.ascontiguousarray(uq[:, :, 128:]).reshape(512, 1024))
    o["mla_v"] = pack_a(np.ascontiguousarray(ukv[:, :, 128:]).reshape(512, 2048))
    o["mla_out"] = pack_a(i["mla_w_out_2"][0])
    o["const"] = constants()
    o["dft"] = dft_tokens()
    o["rope"] = rope_tables()
    return {n: np.ascontiguousarray(a) for n, a in o.items()}


class Token:

    def __init__(self, sem, value=None, due=0.0):
        self.sem, self.value, self.hit, self.due = sem, value, False, due


def flat(after):
    for t in after:
        if t is None:
            continue
        if isinstance(t, (list, tuple)):
            yield from flat(t)
        else:
            yield t


class Queue:

    def __init__(self, sem):
        self.sem, self.ops, self.last, self.t = sem, [], None, 0.0

    def do(self, fn, after=(), cost=0.1):
        after = list(flat(after))
        for t in after:
            t.hit = True
            self.t = max(self.t, t.due + 0.06)
        self.t += cost
        tok = Token(self.sem, None, self.t)
        self.ops.append((fn, after, tok))
        self.last = tok
        return tok

    def number(self):
        n = 0
        for _, _, tok in self.ops:
            if tok.value is None and tok.hit:
                n += 1
                tok.value = n

    def play(self, e):
        seen = {}
        for fn, after, tok in self.ops:
            need = {}
            for t in after:
                need[t.sem.name] = max(need.get(t.sem.name, (0, t.sem)), (t.value, t.sem), key=lambda p: p[0])
            for name, (v, sem) in need.items():
                if seen.get(name, 0) < v:
                    e.wait_ge(sem, v)
                    seen[name] = v
            ins = fn(e)
            if tok.hit and tok.sem is self.sem:
                ins.then_inc(self.sem, 1)


class Slots:

    def __init__(self, places):
        self.free = [(p, []) for p in places]

    def take(self):
        return self.free.pop(0)

    def put(self, place, toks):
        self.free.append((place, list(flat([toks]))))



def bcast(ap, *dims):
    return bass.AP(tensor=ap.tensor, offset=ap.offset, ap=[list(ap.ap[0])] + [list(d) for d in dims])


def three(ap, a):
    return ap.rearrange("p (a b) -> p a b", a=a)


def weave(main, ada, over):
    res, k = [], 0
    for n, u in enumerate(main):
        res.append(u)
        want = len(ada) if n + 1 >= over else len(ada) * (n + 1) // over
        res += ada[k:want]
        k = max(k, want)
    return res


def program(nc, io, out, upto=None):
    ctx = ExitStack()
    with ctx:
        def sb(name, shape, dt, c=ctx):
            return c.enter_context(nc.sbuf_tensor("s_" + name, shape, dt))

        def sem(name):
            return ctx.enter_context(nc.semaphore("m_" + name))

        NR, NH = 4, 3
        KC = sb("const", [128, NCONST], F)
        PR = sb("params", [128, NPARAM], F)
        raw = [sb(f"raw{i}", [128, 2048], F) for i in range(NR)]
        hi_s = [sb(f"hi{i}", [128, 1024], R) for i in range(NH)]
        lo_s = [sb(f"lo{i}", [128, 1024], R) for i in range(NH)]
        E = [sb(f"E{i}", [128, 544], F) for i in range(4)]
        OG = [sb(f"og{i}", [128, 2, 256], F) for i in range(2)]
        GB1 = sb("gb1", [128, 512], F)
        CS = sb("cs", [128, 16, 3], F)
        MOD = [sb(f"mod{i}", [128, 3, 16, 2], F) for i in range(2)]
        ROWS = sb("rows", [128, 512], F)
        BR = sb("br", [128, 512], F)
        SS = sb("ss", [128, 6, 6], F)
        ST = sb("stat", [128, 16], F)
        LG = sb("lg", [128, 6, 32], F)
        RN = sb("rn", [128, 2, 16], F)
        MX = sb("mx", [128, 2, 4], F)
        BN = sb("bn", [128, 2, 16], F)

        def overlay(*variants):
            made, size = {}, 0
            for n_var, names in enumerate(variants):
                c, n = ExitStack(), 0
                for name, shape, dt in names:
                    made[name] = sb(name or f"gap{n_var}_{variants[0][0][0]}_{n}", shape, dt, c)
                    n += 4 * int(np.prod(shape[1:]))
                c.close()
                size = max(size, n)
            return made, size

        W, size = overlay(
            [("W1", [128, 2, 2048], F), ("G", [128, 2, 2, 512], F), ("qT", [128, 4, 256], F),
             ("kT", [128, 4, 256], F), ("dec", [128, 2, 384], F), ("nb", [128, 2, 384], F),
             ("dft", [128, 2, 512], F)],
            [("YB", [128, 8192], F), ("CT", [128, 2048], F), ("GB0", [128, 512], F)],
            [("cqT_h", [128, 4, 256], R), ("cqT_l", [128, 4, 256], R), ("ckT_h", [128, 4, 512], R),
             ("ckT_l", [128, 4, 512], R), ("cq", [128, 2, 512], F), ("ckv", [128, 4, 512], F),
             ("kr_h", [128, 512], R), ("kr_l", [128, 512], R), ("rope", [128, 640], F)],
            [("Y2", [128, 2, 2048], F), ("", [128, 2048], F)] +
            [(f"{n}{i}", [128, k], R) for i in range(2)
             for n, k in (("qn_h", 256), ("qn_l", 256), ("kn_h", 512), ("kn_l", 512))])
        sb("room_w", [128, size // 4], F)
        XR, size = overlay([("X", [128, 2, 2048], F)], [("PH", [128, 4, 512], R), ("PL", [128, 4, 512], R)])
        sb("room_x", [128, size // 4], F)
        HU, _ = overlay(
            [("", [128, 6144], F), ("uT", [128, 4, 286], F)],
            [("", [128, 6144], F), ("PQ", [128, 4, 512], F), ("", [128, 6144], F), ("acc", [128, 4, 256], F),
             ("FX", [128, 2, 512], F)],
            [("", [128, 4096], F), ("V", [128, 2, 4, 512], F), ("", [128, 4096], F), ("qr_h", [128, 4, 256], R),
             ("qr_l", [128, 4, 256], R), ("Pm", [128, 2, 512], F), ("PT", [128, 4, 256], F)])
        Hh = sb("Hh", [128, 2, 16, 256], R)
        Hl = sb("Hl", [128, 2, 16, 256], R)
        ps = ctx.enter_context(nc.psum_tensor("ps", [128, 8, 512], F))

        pe, act, dve, pool, sp = (Queue(sem(n)) for n in ("pe", "act", "dve", "pool", "sp"))
        ring_sems = [sem(f"ring{i}") for i in range(NR)]
        loaded, bus, table = {}, [0.0], [None]

        def K(name, lo=0, hi=None):
            a, b = CONST_COLS[name]
            return KC[:, a + lo:(b if hi is None else a + hi)]

        def P(name, lo=0, hi=None):
            a, b = PARAM_COLS[name]
            return PR[:, a + lo:(b if hi is None else a + hi)]

        def size(ap):
            return int(np.prod(ap.shape[1:]))

        def load(q, dst, src, s, *after):
            loaded[s.name] = loaded.get(s.name, 0) + 16
            t = q.do(lambda e: e.dma_start(dst, src).then_inc(s, 16), after, 0.05)
            bus[0] = max(bus[0], t.due) + 128 * 4 * size(dst) / 360e3
            return Token(s, loaded[s.name], bus[0] + 2.0)

        def mm(o, l, r, first, last, *after):
            passes = 1 if l.dtype == R else 4
            return pe.do(lambda e: e.matmul(o, l, r, start=first, stop=last, skip_group_check=True), after,
                         max(0.02, passes * size(r) * 0.00042 * (0.27 if size(l) < 4 else 1)))

        def mm3(o, l, r, first, last, *after):
            mm(o, l[0], r[0], first, False, *after)
            mm(o, l[0], r[1], False, False)
            return mm(o, l[1], r[0], False, last)

        def tr(o, i, *after):
            ident = K("ident")
            return pe.do(lambda e: e.transpose(o, i, ident), after, 0.055)

        def vcost(q, o, rate=0.00104):
            return 0.1 + 0.0023 * size(o) if q is pool else 0.065 + rate * size(o)

        def tt(q, o, a, b, op, *after):
            return q.do(lambda e: e.tensor_tensor(o, a, b, op), after, vcost(q, o))

        def ts(q, o, a, s1, s2, op0, op1, *after):
            if op1 is None:
                return q.do(lambda e: e.tensor_scalar(o, a, s1, None, op0), after, vcost(q, o, 0.0007))
            return q.do(lambda e: e.tensor_scalar(o, a, s1, s2, op0, op1), after, vcost(q, o, 0.0007))

        def stt(q, o, a, s1, b, op0, op1, *after):
            return q.do(lambda e: e.scalar_tensor_tensor(out=o, in0=a, scalar=s1, in1=b, op0=op0, op1=op1), after,
                        vcost(q, o))

        def cp(q, o, a, *after):
            if q is act:
                return q.do(lambda e: e.activation(o, a, ACT.Copy), after, 0.1 + 0.00084 * size(o))
            return q.do(lambda e: e.tensor_copy(o, a), after, vcost(q, o))

        def fn(f, o, a, *after, **kw):
            cost = 0.1 + 0.00084 * size(o)
            if f not in (ACT.Copy, ACT.Square, ACT.Identity, table[0]):
                cost += 1.3
                table[0] = f
            return act.do(lambda e: e.activation(o, a, f, **kw), after, cost)

        def fill(q, o, v, *after):
            return q.do(lambda e: e.memset(o, v), after)

        def recip(o, a, *after):
            return dve.do(lambda e: e.reciprocal(o, a), after)

        def split(h, l, v, *after):
            t = cp(act, h, v, *after)
            return tt(dve, l, v, h, ALU.subtract, t)

        main = Slots([0, 1, 2, 3])
        side = Slots([4, 5, 6])
        scratch = Slots([0, 1, 2, 3])
        og = Slots([0, 1])

        def pair(name, l=None):
            v = io[name] if l is None else io[name][l]
            order = [(c, i) for i in range(4) for c in range(2)] + [(c, i) for c in (2, 3) for i in range(4)]
            return [("w", v[c, i]) for c, i in order]

        def w_units(l):
            if l < 2:
                u = [("w", io["w_in"][l, PIECES.index(p), i]) for p in ORDER for i in range(4)]
                if l == 0:
                    u[:12] = [("w", io["w_in"][l, PIECES.index(p), i]) for i in range(4) for p in ORDER[:3]]
                return u + [("w", io["w_pw"][l, 0, 0]), ("w", io["w_fft"][l, 0, 0])] + pair("w_out", l)
            if l == 2:
                u = []
                for g in range(4):
                    u += [("w", io["pool_in"][4 * g + i]) for i in range(4)]
                    u += [("w", io["pool_in"][16 + 4 * g + i]) for i in range(4)]
                    u += [("w", io["pool_grp"][g])]
                return u + [("w", io["pool_out"][c, i]) for c in range(4) for i in range(4)]
            chunk = [[("w", io["mla_in"][c, i]) for i in range(4)] for c in range(6)]
            u = chunk[0] + chunk[2] + chunk[3] + chunk[1] + [("w", io["mla_kr"][0])] + chunk[4] + chunk[5]
            for g in range(4):
                u += [("w", io["mla_v"][g, 0])]
                if g % 2 == 0:
                    u += [("w", io["mla_rope"][g // 2])]
                u += [("w", io["mla_qk"][2 * g + i]) for i in range(2)]
            return u + pair("mla_out")

        def a_units(l, jobs):
            return [("ada", io["w_ada"][l, j, u], l, j, u) for j in jobs for u in range(8)]

        first, m0 = [a_units(0, [j]) for j in range(4)], w_units(0)
        units = first[0]
        for j in range(1, 4):
            units += first[j][:4] + m0[3 * j - 3:3 * j - 1] + first[j][4:6] + m0[3 * j - 1:3 * j] + first[j][6:]
        units += weave(m0[9:], a_units(0, (4, 5)) + a_units(1, range(4)), 54) + a_units(1, (4,))[:3]
        units += weave(w_units(1), a_units(1, (4,))[3:] + a_units(1, (5,)) + a_units(2, range(4)), 54)
        units += a_units(2, (4,))[:3]
        units += weave(w_units(2), a_units(2, (4,))[3:] + a_units(2, (5,)) + a_units(3, range(4)), 44)
        units += a_units(3, (4,))[:3]
        units += weave(w_units(3), a_units(3, (4,))[3:] + a_units(3, (5,)), 16)

        st = dict(consumed_upto=0, dma=0, pos=0, half=0, split=0, loaded=[], raw_free=[[] for _ in range(NR)])
        halves = [(n, h) for n, u in enumerate(units) if u[0] == "w" for h in range(2)]
        hl = Slots(range(NH))
        ready = {}

        def more_loads():
            while st["dma"] < len(units) and st["dma"] - NR < st["consumed_upto"]:
                n = st["dma"]
                st["loaded"].append(load(sp, raw[n % NR][:, :], units[n][1], ring_sems[n % NR], st["raw_free"][n % NR]))
                st["dma"] += 1

        done_units = set()

        def unit_read(n, tok):
            st["raw_free"][n % NR] = [tok]
            done_units.add(n)
            while st["consumed_upto"] in done_units:
                st["consumed_upto"] += 1
            more_loads()

        def more_splits():
            while st["split"] < len(halves) and hl.free:
                n, h = halves[st["split"]]
                if n >= st["dma"]:
                    return
                i, free = hl.take()
                v = raw[n % NR][:, 1024 * h:1024 * (h + 1)]
                t = split(hi_s[i][:, :], lo_s[i][:, :], v, st["loaded"][n], free)
                ready[st["split"]] = (i, t)
                st["split"] += 1
                if h == 1:
                    unit_read(n, t)

        sides = []

        SLACK, CALM, AHEAD = 6.0, 3.0, 4

        def is_due(s):
            w = s["wait"]
            if isinstance(w, int):
                s["wait"] = w - 1
                return w <= 0
            if dve.t > pe.t + SLACK or act.t > pe.t + SLACK:
                return False
            if w == "dve":
                return dve.t <= pe.t + CALM
            if not side.free:
                return False
            return all(t.due <= pe.t + 0.1 for t in flat([w, side.free[0][1]]))

        def need_time(s):
            return max([pe.t] + [t.due for t in flat([s["wait"]])]) if s["wait"] != "dve" else dve.t

        def step(s):
            try:
                s["wait"] = next(s["gen"])
                s["wait"] = 0 if s["wait"] is None else s["wait"]
            except StopIteration:
                sides.remove(s)

        def pump(budget=2.2):
            begin, went = pe.t, True
            while went and pe.t < begin + budget:
                went = False
                for s in [s for s in sides if not s["last"]]:
                    if is_due(s):
                        step(s)
                        went = went or s["wait"] != 0
                for s in [s for s in sides if s["last"]][:1]:
                    if is_due(s):
                        step(s)

        def lend(n):
            a, b = (side, main) if n > 0 else (main, side)
            for bank in (4, 5)[:abs(n)]:
                at = [f for f in a.free if f[0] == bank]
                assert at
                a.free.remove(at[0])
                b.free.append(at[0])

        def launch(name, gen, front=False, start=False, last=False):
            s = dict(name=name, gen=gen, wait=0, last=last)
            if front:
                sides.insert(0, s)
            else:
                sides.append(s)
            if start:
                step(s)

        def finish(name):
            for s in list(sides):
                if s["name"] == name:
                    for _ in s["gen"]:
                        pass
                    sides.remove(s)

        def work_off_ada():
            while units[st["pos"]][0] == "ada":
                ada_unit(st["pos"])
                st["pos"] += 1
                pump()

        def pump_until(there):
            for _ in range(2000):
                if there():
                    return
                waiting = []
                for s in list(sides):
                    if isinstance(s["wait"], int):
                        if is_due(s):
                            step(s)
                    else:
                        waiting.append(s)
                if there() or not waiting:
                    continue
                now = [s for s in waiting if is_due(s)]
                step(now[0] if now else min(waiting, key=need_time))
            raise AssertionError("no side job leads there: " + str([s["name"] for s in sides]))

        def prepared(h, k, can=lambda k: True):
            for j in range(k, min(k + AHEAD, NKT - 1) + 1, 2):
                if j == k or can(j):
                    pump_until(lambda: j in h)
            return h[k]

        def next_half():
            work_off_ada()
            more_splits()
            k = st["half"]
            st["half"] += 1
            if k % 2 == 1:
                st["pos"] += 1
            i, t = ready.pop(k)
            return (hi_s[i], lo_s[i]), t, i

        def give_back(i, tok):
            hl.put(i, tok)
            more_splits()

        ada = dict(bank=[], rows=[], br=[])
        mod_ready, mod_read = {}, {0: [], 1: []}
        br_sem = sem("br")

        def load_bias(l, j, *after):
            load(sp, BR[0:2, :], io["b_ada"][l, j, 0:2], br_sem, *after)
            return load(sp, BR[32:34, :], io["b_ada"][l, j, 2:4], br_sem, *after)

        def ada_unit(n):
            _, _, l, j, u = units[n]
            c0, m = (0, 1) if l < 2 else (1, 2)
            for s in range(4):
                o = ps[32 * s:32 * s + m, 7, :]
                last = mm(o, CS[:, 2 * u + s // 2, c0:c0 + m], raw[n % NR][:, 512 * s:512 * (s + 1)],
                          u == 0, u == 7, st["loaded"][n], cs_ready, ada["bank"] if u == 0 else None)
            unit_read(n, last)
            if u == 4:
                ada["br"] = load_bias(l, j, ada["bank"])
            if u == 7:
                ada["bank"] = [tt(dve, ROWS[:, :], ps[:, 7, :], BR[:, :], ALU.add, last, ada["br"], ada["rows"])]
                launch("ada", ada_cols(l, j, ada["bank"]), front=True)
                ada["rows"] = None

        def ada_cols(l, j, rows):
            yield rows
            b, free = side.take()
            for i in range(4):
                t = mm(ps[:, b, 4 * i:4 * i + 4], ROWS[:, 128 * i:128 * (i + 1)], K("sel"), True, True,
                       rows if i == 0 else None, free if i == 0 else None)
            ada["rows"] = [t]
            M, old = MOD[l % 2], mod_read[l % 2]
            v = ps[:, b, 0:16].rearrange("p (i c) -> p i c", i=4)
            nc_ = 1 if l < 2 else 2
            if j < 4:
                g = P("norm_g" if l < 2 else "pre", 16 * (l % 2) + 4 * j, 16 * (l % 2) + 4 * j + 4)
                cp(dve, M[:, 0, 4 * j:4 * j + 4, 0:nc_], v[:, :, 0:nc_], t, old)
                for c in range(nc_):
                    t = stt(dve, M[:, 1, 4 * j:4 * j + 4, c], v[:, :, 2 + c], 1.0, g, ALU.add, ALU.mult)
            else:
                for half in range(2):
                    k0 = 8 * (j - 4) + 4 * half
                    for c in range(nc_):
                        o, i = M[:, 2, k0:k0 + 4, c], v[:, :, 2 * half + c]
                        if l < 2:
                            t = cp(dve, o, i, t, old)
                        else:
                            t = tt(dve, o, i, P("post", 16 * (l - 2) + k0, 16 * (l - 2) + k0 + 4), ALU.mult, t, old)
            side.put(b, t)
            mod_ready[l, j] = t

        def chunk_a(stat, tiles, nk, need, evacs, hooks={}):
            banks = [[main.take() for _ in tiles] for _ in evacs]
            for u in range(nk // 4):
                for c, evac in enumerate(evacs):
                    for h in (2 * u, 2 * u + 1):
                        w, w_tok, slot = next_half()
                        last = []
                        for kt in (2 * h, 2 * h + 1):
                            for n, t in enumerate(tiles):
                                b, free = banks[c][n]
                                o = 512 * (kt % 2)
                                last.append(mm3(ps[:, b, :], stat(kt, t), [p[:, o:o + 512] for p in w], kt == 0,
                                                kt == nk - 1, w_tok, need(kt), free if kt == 0 else None))
                        give_back(slot, last[-1])
                        if (c, h) in hooks:
                            hooks[c, h](last[-1])
                        if h == nk // 2 - 1:
                            for n, t in enumerate(tiles):
                                main.put(banks[c][n][0], evac(n, ps[:, banks[c][n][0], :], last[n - len(tiles)]))
                        pump()

        def b_tile(rhs, shape, need, evac):
            b, free = main.take()
            for part in range(2):
                w, w_tok, slot = next_half()
                for j in range(8):
                    kt = 8 * part + j
                    last = mm3(shape(b), [p[:, 128 * j:128 * (j + 1)] for p in w], rhs(kt), kt == 0, kt == 15,
                               w_tok, need(kt), free if kt == 0 else None)
                give_back(slot, last)
                if part == 0:
                    pump()
            main.put(b, evac(shape(b), last))
            pump()

        def b_half(jobs):
            w, w_tok, slot = next_half()
            todo = []
            for m, (rhs, shape, need, evac) in enumerate(jobs):
                b, free = main.take()
                for kt in range(4):
                    c = 128 * (4 * m + kt)
                    last = mm3(shape(b), [p[:, c:c + 128] for p in w], rhs(kt), kt == 0, kt == 3,
                               w_tok, need(kt), free if kt == 0 else None)
                todo.append((b, evac, shape(b), last))
            give_back(slot, last)
            for b, evac, o, t in todo:
                main.put(b, evac(o, t))

        def sums(src, i, junk, *after):
            return fn(ACT.Square, junk, src, *after, accum_out=SS[:, i[0], i[1]:i[1] + 1])

        def inv_rms(tiles, parts, n, col, *after):
            k = len(tiles)
            t0, o = tiles[0], ST[:, col:col + k]
            if parts > 1:
                t = dve.do(lambda e: e.tensor_reduce(o, SS[:, t0:t0 + k, 0:parts], AX.X, ALU.add), after)
            else:
                t = cp(dve, o, SS[:, t0:t0 + k, 0], after)
            t = fn(ACT.Sqrt, o, o, t, bias=K("eps"), scale=1.0 / n)
            return recip(o, o, t)

        def feature_major(src, dst, mul, add, when, got):
            for k in range(0, NKT, 2):
                while when(k) is None:
                    yield 1
                yield when(k)
                b, free = side.take()
                for j in range(2):
                    for i in range(2):
                        c = 128 * (k + j)
                        t = tr(ps[:, b, 256 * j + 128 * i:256 * j + 128 * (i + 1)], src(i)[:, c:c + 128], when(k), free)
                n, nfree = og.take()
                for j in range(2):
                    e = fn(ACT.Identity, OG[n][:, j, :], ps[:, b, 256 * j:256 * (j + 1)], t, nfree,
                           scale=mul(k + j), bias=add(k + j))
                side.put(b, e)
                h, l = dst(k)
                t = cp(dve, h, OG[n][:, :, :], e)
                t = tt(dve, l, OG[n][:, :, :], h, ALU.subtract, t)
                og.put(n, t)
                got(k, t)
                got(k + 1, t)

        def row_broadcast(dst, col_ap, reads, after, res, name):
            n, nfree = scratch.take()
            for i in range(4):
                t = ts(pool, E[n][:, 128 * i:128 * (i + 1)], K("ident"), col_ap[:, i:i + 1], None, ALU.mult, None,
                       nfree, after)
            yield t
            b, free = side.take()
            t = mm(ps[:, b, :], K("ones"), E[n][:, 0:512], True, True, t, free)
            scratch.put(n, t)
            t = cp(act, dst, ps[:, b, :], t, reads)
            side.put(b, t)
            res[name] = t

        X = XR["X"]
        start_sem = sem("start")
        load(act, PR[:, :], io["params"], start_sem)
        params = load(act, KC[:, :], io["const"], start_sem)
        x_sem = sem("x")
        for t2 in range(2):
            x_tok = load(act, X[:, t2, :], io["x_in"][128 * t2:128 * (t2 + 1), :], x_sem)
        more_loads()
        t0 = fill(dve, ps[:, 7, :], 0.0)
        fill(dve, BR[:, :], 0.0)
        for i in range(4):
            t = fill(dve, E[i][:, :], 0.0)
        ada["bank"] = [t0, t]
        cs_ready = fn(ACT.Silu, CS[:, :, :], P("c").rearrange("p (k c) -> p k c", k=16), params)

        x = P("logit")
        a_, e_, s_, s2, p_, m_ = (LG[:, i, :] for i in range(6))
        t = ts(dve, a_, x, -1.0, None, ALU.mult, None, params)
        t = tt(dve, a_, a_, x, ALU.max, t)
        te = fn(ACT.Exp, e_, a_, t, scale=-1.0)
        t = ts(dve, s_, e_, 2.0, None, ALU.add, None, te)
        t = recip(s_, s_, t)
        t = tt(dve, s_, s_, e_, ALU.mult, t)
        t = tt(dve, s2, s_, s_, ALU.mult, t)
        t = ts(dve, p_, s2, 1.0 / 19, None, ALU.mult, None, t)
        for k in range(8, 0, -1):
            t = stt(dve, p_, p_, 1.0 / (2 * k + 1), s2, ALU.add, ALU.mult, t)
        t = stt(dve, p_, p_, 1.0, s_, ALU.add, ALU.mult, t)
        tm = ts(dve, m_, x, -1.0, 0.0, ALU.mult, ALU.max)
        t = stt(dve, p_, p_, 2.0, m_, ALU.mult, ALU.add, t, tm)
        lg_ready = ts(dve, LG[:, 0, :], p_, -1.0, None, ALU.mult, None, t)

        def lgam(l, back, h):
            c = 16 * l + 8 * back + h
            return LG[:, 0, c:c + 1]

        YB, CT = W["YB"], W["CT"]
        W1, G, qT, kT, dec, nb, dft = (W[n] for n in ("W1", "G", "qT", "kT", "dec", "nb", "dft"))
        uT, PQ, acc, FX = HU["uT"], HU["PQ"], HU["acc"], HU["FX"]
        TQ, TK = three(W1[:, 0, 0:1024], 2), three(W1[:, 0, 1024:2048], 2)
        V0, V1 = three(W1[:, 1, 0:1024], 2), three(W1[:, 1, 1024:2048], 2)
        G0, G1 = G[:, 0], G[:, 1]
        dec_slots, nb_slots = Slots([0, 1]), Slots([0, 1])
        dft_sem, nb_sems = sem("dft"), [sem("nb0"), sem("nb1")]
        places = {n: [] for n in ("TQ", "TK", "V0", "V1", "G0", "G1", "qk", "uT", "PQ", "acc", "FX", "dft",
                                  "H0", "H1", "rn0", "rn1", "rn2", "X")}

        def own(*names):
            toks = [places[n] for n in names]
            assert None not in toks, names
            for n in names:
                places[n] = None
            return toks

        def give(name, *toks):
            places[name] = list(flat(toks))

        def own_when(*names):
            pump_until(lambda: not (any(places[n] is None for n in names)))
            return own(*names)

        def keep(dst, name, f=ACT.Copy):
            done, free = [], []

            def ev(i, o, t):
                if i == 0:
                    free[:] = own_when(name)
                done.append(fn(f, dst[:, i, :], o, t, free))
                return done[-1]
            return ev, done

        def rotate(dst, name):
            done, free = [], []

            def ev(i, o, t):
                if i == 0:
                    free[:] = own_when(name)
                s, sfree = scratch.take()
                o4 = o.rearrange("p (h x d) -> p h x d", h=8, x=2)
                s4 = E[s][:, 0:512].rearrange("p (h x d) -> p h x d", h=8, x=2)
                d4 = dst[:, i, :].rearrange("p (h x d) -> p h x d", h=8, x=2)
                a = tt(dve, d4, o4, bcast(K("cosr", 32 * i), (0, 8), (0, 2), (1, 32)), ALU.mult, t, free)
                for x in range(2):
                    sin = bcast(K("sinr", 64 * i + 32 * x), (0, 8), (1, 32))
                    e = tt(dve, s4[:, :, x, :], o4[:, :, 1 - x, :], sin, ALU.mult, sfree)
                r = tt(dve, dst[:, i, :], dst[:, i, :], E[s][:, 0:512], ALU.add, a, e)
                scratch.put(s, r)
                done.append(r)
                return e
            return ev, done

        def pair_transposed(q_tok, k_tok):
            while places["qk"] is None:
                yield 1
            free, n, got = own("qk"), 0, []
            for src, dst, tok, name in ((TQ, qT, q_tok, "TQ"), (TK, kT, k_tok, "TK")):
                for i in range(2):
                    b, bfree = side.take()
                    for pr in range(4):
                        tp = tr(ps[:, b, 128 * pr:128 * (pr + 1)], src[:, i, 128 * pr:128 * (pr + 1)], tok, bfree)
                    got.append(cp((act, dve)[n % 2], dst[:, :, 128 * i:128 * (i + 1)], three(ps[:, b, :], 4), tp, free))
                    n += 1
                    side.put(b, got[-1])
                    yield (tok if i == 0 else k_tok) if dst is qT else got
                give(name, tp)
            return got

        def gate_transposed(gate, rn, *after):
            s, free = scratch.take()
            v = three(E[s][:, 0:256], 2)
            for i in range(2):
                t = tt(dve, three(v[:, i], 2), three(gate[:, i], 2), bcast(rn(i), (1, 2), (0, 64)), ALU.mult, after, free)
            yield t
            b, free = side.take()
            for i in range(2):
                tp = tr(ps[:, b, 128 * i:128 * (i + 1)], v[:, i], t, free)
            scratch.put(s, tp)
            return b, tp, t

        def token_to_parts(src, src_tok, free, s_out, k0, o_tok):
            yield src_tok
            for b2 in range(2):
                b, bfree = side.take()
                for j in range(2):
                    for i in range(2):
                        c = 128 * (2 * b2 + j)
                        tp = tr(ps[:, b, 256 * j + 128 * i:256 * j + 128 * (i + 1)], src[:, i, c:c + 128],
                                src_tok, bfree)
                k = k0 + 2 * b2
                h, l = (p[:, s_out, k:k + 2, :] for p in (Hh, Hl))
                t = split(h, l, three(ps[:, b, :], 2), tp, free)
                side.put(b, t)
                o_tok[k] = o_tok[k + 1] = t
                yield src_tok
            return tp

        def layer1(l, x_ready):
            M = MOD[l % 2]
            hT, oT = 0, 1
            h_tok, o_tok, made = {}, {}, {}
            t = inv_rms([0, 1], 4, D, 0, x_ready)
            free = own("TQ", "TK", "V0", "V1")
            xn = [ts(dve, W1[:, i, :], X[:, i, :], ST[:, i:i + 1], None, ALU.mult, None, t, free) for i in range(2)]
            hfree = own("H0")
            launch("prep", feature_major(
                lambda i: W1[:, i, :], lambda k: (Hh[:, hT, k:k + 2, :], Hl[:, hT, k:k + 2, :]),
                lambda k: M[:, 1, k, 0:1], lambda k: M[:, 0, k, 0:1],
                lambda k: [xn, hfree, mod_ready[l, k // 4]] if (l, k // 4) in mod_ready else None,
                h_tok.__setitem__), front=True)

            def need_h(k):
                return prepared(h_tok, k, lambda j: (l, j // 4) in mod_ready)

            def stat(s):
                return lambda k, i: [p[:, s, k, 128 * i:128 * (i + 1)] for p in (Hh, Hl)]

            def piece(ev, hooks={}):
                chunk_a(stat(hT), [0, 1], NKT, need_h, [ev], hooks)

            def cw(ct, k):
                return P("conv", 136 * l + 34 * ct + k, 136 * l + 34 * ct + k + 1)

            for n in ("TQ", "V0", "V1"):
                give(n, xn)
            ev_a, a_tok = keep(TQ, "TQ")
            u_tok = []

            def ev_b(i, o, t):
                t = fn(ACT.Sigmoid, TK[:, i, :], o, t)
                u_tok.append(tt(dve, TQ[:, i, :], TQ[:, i, :], TK[:, i, :], ALU.mult, t, a_tok[i]))
                if i == 1:
                    launch("conv", conv(), last=True)
                return t

            def conv():
                yield u_tok
                free_u, free_a = own("uT", "PQ"), own("acc")
                t = fill(pool, uT[:, :, 0:15], 0.0, free_u)
                t = [t, fill(pool, uT[:, :, 271:286], 0.0)]
                for i in range(2):
                    b, free = side.take()
                    for ct in range(4):
                        tp = tr(ps[:, b, 128 * ct:128 * (ct + 1)], TQ[:, i, 128 * ct:128 * (ct + 1)], u_tok, free)
                    e = cp(dve, uT[:, :, 15 + 128 * i:15 + 128 * (i + 1)], three(ps[:, b, :], 4), tp, free_u)
                    side.put(b, e)
                    t.append(e)
                give("TQ", tp)
                give("TK", u_tok)
                last = [None] * 4
                for k in range(31):
                    for ct in range(4):
                        u, a = uT[:, ct, k:k + 256], acc[:, ct, :]
                        if k == 0:
                            last[ct] = ts(dve, a, u, cw(ct, 0), cw(ct, 31), ALU.mult, ALU.add, t, free_a)
                        else:
                            last[ct] = stt(dve, a, u, cw(ct, k), a, ALU.mult, ALU.add, last[ct])
                    yield "dve" if k < 30 else last
                yn = bcast(uT[:, 0, :], (512, 2), (1, 512))
                y_tok = []
                for i in range(2):
                    b, free = side.take()
                    for ct in range(4):
                        tp = tr(ps[:, b, 128 * ct:128 * (ct + 1)], acc[:, ct, 128 * i:128 * (i + 1)], last, free)
                    S, A, V, o = BN[:, i, 0:6], BN[:, i, 6:8], BN[:, i, 8:9], ps[:, b, :]
                    t = dve.do(lambda e, S=S, o=o: e.bn_stats(S, o), [tp])
                    t = dve.do(lambda e, S=S, A=A: e.bn_aggr(A, S), [t])
                    t = fn(ACT.Sqrt, V, BN[:, i, 7:8], t, bias=K("eps"))
                    t = recip(V, V, t)
                    t = ts(dve, yn[:, i, :], o, BN[:, i, 6:7], V, ALU.subtract, ALU.mult, t, last)
                    side.put(b, t)
                    y_tok.append(t)
                yield y_tok
                for b2 in range(2):
                    b, free = side.take()
                    for j in range(2):
                        c = 128 * (2 * b2 + j)
                        for i in range(2):
                            tp = tr(ps[:, b, 256 * j + 128 * i:256 * j + 128 * (i + 1)], yn[:, i, c:c + 128], y_tok, free)
                    for j in range(2):
                        ct = 2 * b2 + j
                        t = fn(ACT.Silu, acc[:, ct, :], ps[:, b, 256 * j:256 * (j + 1)], tp,
                               bias=cw(ct, 33), scale=cw(ct, 32))
                    side.put(b, t)
                    yield y_tok
                give("uT", tp)
                give("PQ", tp)
                made["s"] = t

            ev_v, nv = keep(V0, "V0")
            if l == 0:
                lend(2)
                chunk_a(stat(hT), [0, 1], NKT, need_h, [ev_a, ev_b, ev_v])
                lend(-2)
            else:
                piece(ev_a)
                piece(ev_b)
                piece(ev_v)

            ev, nq = keep(TQ, "TQ")
            piece(ev)
            ev, nk = keep(TK, "TK")
            piece(ev)
            ev, ng = keep(G0, "G0", ACT.Silu)
            piece(ev)

            def neighbours():
                qk = yield from pair_transposed(nq, nk)
                hfree = places["H1"]
                biases, mx_read = {}, {0: [], 1: []}

                def bias(h):
                    d, free = nb_slots.take()
                    t = load(sp, nb[:, d, :], io["na_bias"][l, h], nb_sems[d], free)
                    v = nb[:, d, :].rearrange("p (m c) -> p m c", m=6)
                    biases[h] = (d, tt(pool, v, v, bcast(K("mask"), (0, 6), (1, 64)), ALU.add, t))

                bias(0)
                for pr in range(4):
                    rn = f"rn{1 + pr % 2}"
                    rfree = own(rn)
                    ob, obfree = side.take()
                    c0, exps = 8 * (pr % 2), []
                    for hh in range(2):
                        h, o = 2 * pr + hh, 64 * hh
                        if h < 7:
                            bias(h + 1)
                        b, free = side.take()
                        for i in range(2):
                            t = mm(ps[:, b, 256 * (1 - i):256 * (2 - i)], qT[o:o + 64, pr, 128 * i:128 * (i + 1)],
                                   kT[o:o + 64, pr, :], True, True, qk, free)
                        s, sfree = scratch.take()
                        d, d_tok = biases.pop(h)
                        pm, mx = three(E[s][:, 0:512], 2), MX[:, hh, 0:2]
                        t = stt(dve, pm, three(ps[:, b, :], 2), 0.125, bcast(nb[:, d, :], (128, 2), (1, 256)),
                                ALU.mult, ALU.add, t, d_tok, sfree)
                        side.put(b, t)
                        nb_slots.put(d, t)
                        t = dve.do(lambda e, mx=mx, pm=pm: e.tensor_reduce(mx, pm, AX.X, ALU.max, negate=True),
                                   [t] + mx_read[hh])
                        for x in range(2):
                            c = c0 + 2 * (1 - x) + hh
                            t2 = fn(ACT.Exp, pm[:, x, :], pm[:, x, :], t, rfree, bias=mx[:, x:x + 1],
                                    accum_out=RN[:, 1, c:c + 1])
                        mx_read[hh] = [t2]
                        exps.append(t2)
                        yield t2
                        b, free = side.take()
                        for kt in range(2):
                            for i in range(2):
                                tp = tr(ps[:, b, 256 * kt + 128 * i:256 * kt + 128 * (i + 1)],
                                        pm[:, 1 - i, 128 * kt:128 * (kt + 1)], t2, free)
                        scratch.put(s, tp)
                        s, sfree = scratch.take()
                        t = cp((act, dve)[hh], E[s][:, 0:512], ps[:, b, :], tp, sfree)
                        side.put(b, t)
                        yield t
                        for kt in range(2):
                            tp = mm(ps[o:o + 64, ob, 0:256], V0[:, kt, 64 * h:64 * (h + 1)],
                                    E[s][:, 256 * kt:256 * (kt + 1)], kt == 0, kt == 1, t, nv, obfree)
                        scratch.put(s, tp)
                    o_done = tp
                    r = RN[:, 1, c0:c0 + 4]
                    t = recip(r, r, exps)
                    b, tp, g = yield from gate_transposed(
                        G0[:, :, 128 * pr:128 * (pr + 1)], lambda i: RN[:, 1, c0 + 2 * i:c0 + 2 * i + 2], t, ng)
                    give(rn, g)
                    n, free = og.take()
                    t = cp(act, OG[n][:, 1, :], ps[:, b, 0:256], tp, free)
                    side.put(b, t)
                    t = tt(dve, OG[n][:, 0, :], ps[:, ob, 0:256], OG[n][:, 1, :], ALU.mult, t, o_done)
                    side.put(ob, t)
                    t = split(Hh[:, oT, pr, :], Hl[:, oT, pr, :], OG[n][:, 0, :], t, hfree)
                    og.put(n, t)
                    o_tok[pr] = t
                    yield t
                give("qk", pe.last)
                give("V0", o_done)
                give("G0", g)

            launch("na", neighbours())

            ev, rv = keep(V1, "V1")
            piece(ev)
            ev, rq = rotate(TQ, "TQ")
            piece(ev)
            ev, rk = rotate(TK, "TK")
            piece(ev)
            ev, rg = keep(G1, "G1", ACT.Silu)
            piece(ev)

            def retention():
                qk = yield from pair_transposed(rq, rk)
                ofree, rfree = own("TK", "rn0")
                oraw = bcast(TK[:, 0, :], (256, 4), (1, 256))
                oraw_tok, ss_tok, decs = [], [], {}

                def decay(h):
                    d, free = dec_slots.take()
                    c = dec[:, d, :]
                    t = ts(pool, c, K("dist_b"), lgam(l, 1, h), None, ALU.mult, None, lg_ready, free)
                    t = stt(dve, c, K("dist_f"), lgam(l, 0, h), c, ALU.mult, ALU.add, t)
                    decs[h] = (d, fn(ACT.Exp, c, c, t))

                decay(0)
                for pr in range(4):
                    ob, obfree = side.take()
                    for hh in range(2):
                        h, o = 2 * pr + hh, 64 * hh
                        if h < 7:
                            decay(h + 1)
                        b, free = side.take()
                        for jt in range(2):
                            t = mm(ps[:, b, 256 * (1 - jt):256 * (2 - jt)], kT[o:o + 64, pr, 128 * jt:128 * (jt + 1)],
                                   qT[o:o + 64, pr, :], True, True, qk, free)
                        s, sfree = scratch.take()
                        d, d_tok = decs.pop(h)
                        t = stt(dve, three(E[s][:, 0:512], 2), three(ps[:, b, :], 2), 0.125,
                                bcast(dec[:, d, :], (128, 2), (1, 256)), ALU.mult, ALU.mult, t, d_tok, sfree)
                        side.put(b, t)
                        dec_slots.put(d, t)
                        yield t
                        for jt in range(2):
                            tp = mm(ps[o:o + 64, ob, 0:256], V1[:, jt, 64 * h:64 * (h + 1)],
                                    E[s][:, 256 * (1 - jt):256 * (2 - jt)], jt == 0, jt == 1, t, rv, obfree)
                        scratch.put(s, tp)
                    oraw_tok.append(cp(act, oraw[:, pr, :], ps[:, ob, 0:256], tp, ofree))
                    s, sfree = scratch.take()
                    t = fn(ACT.Square, E[s][:, 0:256], ps[:, ob, 0:256], sfree)
                    side.put(ob, t)
                    yield t
                    b, free = side.take()
                    for i in range(2):
                        tp = mm(ps[:, b, 2 * i:2 * i + 2], E[s][:, 128 * i:128 * (i + 1)], K("hsel"), True, True, t, free)
                    scratch.put(s, tp)
                    ss_tok.append(cp(dve, bcast(RN[:, 0, 2 * pr:2 * pr + 1], (8, 2), (1, 2)), three(ps[:, b, 0:4], 2),
                                     tp, rfree))
                    side.put(b, ss_tok[-1])
                give("qk", tp)
                give("V1", tp)
                t = fn(ACT.Sqrt, RN[:, 0, :], RN[:, 0, :], ss_tok, bias=K("eps"), scale=1.0 / 64)
                rn_tok = recip(RN[:, 0, :], RN[:, 0, :], t)
                ofree = places["H1"]
                for pr in range(4):
                    b, tp, g = yield from gate_transposed(
                        G1[:, :, 128 * pr:128 * (pr + 1)], lambda i: RN[:, 0, 8 * i + 2 * pr:8 * i + 2 * pr + 2],
                        rn_tok, rg)
                    n, free = og.take()
                    t = tt(dve, OG[n][:, 0, :], ps[:, b, 0:256], oraw[:, pr, :], ALU.mult, tp, oraw_tok, free)
                    side.put(b, t)
                    fx = t
                    t = split(Hh[:, oT, 4 + pr, :], Hl[:, oT, 4 + pr, :], OG[n][:, 0, :], t, ofree)
                    og.put(n, t)
                    o_tok[4 + pr] = t
                give("G1", g)
                give("TK", fx)
                give("rn0", g)

            launch("ret", retention())

            ev, fx = keep(FX, "FX")
            dft_tok = load(sp, dft[:, :, :], three(io["dft"], 2), dft_sem, places["dft"])
            piece(ev)

            def fourier():
                while places["PQ"] is None:
                    yield 1
                free, pq = own("PQ"), []
                for g in range(4):
                    b, bfree = side.take()
                    for i in range(2):
                        tp = mm(ps[:, b, :], FX[:, i, 128 * g:128 * (g + 1)], dft[:, i, :], i == 0, i == 1,
                                fx, dft_tok, bfree)
                    pq.append(cp((act, dve)[g % 2], PQ[:, g, :], ps[:, b, :], tp, free))
                    side.put(b, pq[-1])
                    yield pq[-1] if g == 3 else fx
                give("dft", tp)
                yf = bcast(FX[:, 0, :], (256, 4), (1, 256))
                for g2 in range(2):
                    b, bfree = side.take()
                    for g in (2 * g2, 2 * g2 + 1):
                        for x in range(2):
                            tq = mm(ps[:, b, 256 * (g % 2):256 * (g % 2 + 1)], K("cc", 128 * x, 128 * (x + 1)),
                                    PQ[:, g, 256 * x:256 * (x + 1)], x == 0, x == 1, pq, bfree)
                    t = cp(act, yf[:, 2 * g2:2 * g2 + 2, :], three(ps[:, b, :], 2), tq, tp)
                    side.put(b, t)
                    made["f", g2] = t
                    yield pq
                made["pq"] = tq
                made["y"] = t

            launch("fft", fourier())
            ev, cg = keep(G0, "G0", ACT.Silu)
            piece(ev)
            ev, fg = keep(V0, "V0", ACT.Silu)

            def parts_of(src, k0, name):
                def hook(tok):
                    pump_until(lambda: not (name not in made))
                    for j in (0, 2):
                        made[name, "parts", j] = split(Hh[:, hT, k0 + j:k0 + j + 2, :], Hl[:, hT, k0 + j:k0 + j + 2, :],
                                                       src[:, j:j + 2, :], made[name], tok)
                return hook

            yf = bcast(FX[:, 0, :], (256, 4), (1, 256))
            piece(ev, {(0, 1): parts_of(acc, 0, "s"), (0, 3): parts_of(yf, 4, "y")})

            def gated_chunk(k0, name, dst, gate, gate_tok, free):
                o_done = []

                def ev(i, o, t):
                    o_done.append(tt(dve, dst[:, i, :], o, gate[:, i, :], ALU.mult, t, gate_tok, free))
                    return o_done[-1]
                chunk_a(lambda k, i: [p[:, hT, k0 + k, 128 * i:128 * (i + 1)] for p in (Hh, Hl)], [0, 1], 4,
                        lambda k: made[name, "parts", k // 2 * 2], [ev])
                return o_done

            o_cv = gated_chunk(0, "s", TQ, G0, cg, own_when("TQ"))
            give("G0", o_cv)
            hfree = places["H1"]

            def cv_out():
                tp = yield from token_to_parts(TQ, o_cv, [hfree, made["pq"]], oT, 8, o_tok)
                give("TQ", tp)

            launch("cvo", cv_out())
            o_ff = gated_chunk(4, "y", TK, V0, fg, own_when("TK"))
            give("V0", o_ff)
            give("H0", pe.last)

            def ff_out():
                tp = yield from token_to_parts(TK, o_ff, hfree, oT, 12, o_tok)
                give("TK", tp)
                made["ffo"] = tp

            launch("ffo", ff_out())
            if l == 1:
                launch("ctx", context_prep())

            def need_o(k):
                pump_until(lambda: not (k not in o_tok))
                return o_tok[k]

            GBs = [GB1, W["GB0"]]
            gb_read = {0: [dve.last], 1: places["dft"]}
            fg_read = {0: [], 1: []}
            x_tok = []

            def out_chunk(c):
                gb, b, late = {}, c % 2, c == 3

                def hook(_):
                    pump_until(lambda: (l, 4 + c // 2) in mod_ready)
                    launch("gate", row_broadcast(GBs[b][:, :], M[:, 2, 4 * c:4 * c + 4, 0], gb_read[b],
                                                 mod_ready[l, 4 + c // 2], gb, "g"))
                    if l == 1:
                        launch("fg", row_broadcast(CT[:, 512 * b:512 * (b + 1)], P("final_g", 4 * c, 4 * c + 4),
                                                   [fg_read[b], dve.last], None, gb, "f"))

                def ev(i, o, t):
                    pump_until(lambda: "g" in gb and (l == 0 or "f" in gb))
                    s, free = scratch.take()
                    xs = X[:, i, 512 * c:512 * (c + 1)]
                    t = tt(dve, E[s][:, 0:512], o, GBs[b][:, :], ALU.mult, t, gb["g"], free)
                    gb_read[b] = [t]
                    a = tt(dve if late else pool, xs, xs, E[s][:, 0:512], ALU.add, t)
                    x_tok.append(sums(xs, (i, c), E[s][:, 0:512], a))
                    if l == 1:
                        xf = YB[:, 4096 + 2048 * i + 512 * c:4096 + 2048 * i + 512 * (c + 1)]
                        a = tt(dve if late else pool, xf, xs, CT[:, 512 * b:512 * (b + 1)], ALU.mult, a, gb["f"], t)
                        fg_read[b] = [a]
                        x_tok.append(sums(xf, (4 + i, c), E[s][:, 0:512], a, x_tok[-1]))
                    scratch.put(s, x_tok[-1])
                    return t
                return ev, hook

            (ev0, hook0), (ev1, hook1) = out_chunk(0), out_chunk(1)
            chunk_a(stat(oT), [0, 1], NKT, need_o, [ev0, ev1], {(0, 4): hook0, (1, 4): hook1})
            for c in (2, 3):
                ev, hook = out_chunk(c)
                chunk_a(stat(oT), [0, 1], NKT, need_o, [ev], {(0, 2): hook})
            give("dft", gb_read[1])
            mod_read[l % 2] = [dve.last, pool.last]
            for n in ("conv", "ret", "na", "fft", "cvo", "ffo"):
                assert all(s["name"] != n for s in sides), n
            give("H1", pe.last)
            for n in ("uT", "acc", "FX", "PQ"):
                give(n, pe.last)
            return x_tok

        h2 = {0: {}, 1: {}}
        ctx_sem, spill_sem, reload_sem, ct_sem = sem("ctx"), sem("spill"), sem("reload"), sem("ct")

        def context_prep():
            names = ("TQ", "TK", "V0", "V1")
            while any(places[n] is None for n in names) or places["H0"] is None or (2, 0) not in mod_ready:
                yield 1
            free, hfree = own(*names), own("H0")
            for i in range(2):
                t = load(sp, W1[:, i, :], io["ctx_in"][128 * i:128 * (i + 1), :], ctx_sem, free)
            yield t
            sq = []
            for i in range(2):
                for c in range(4):
                    n, nfree = scratch.take()
                    sq.append(sums(W1[:, i, 512 * c:512 * (c + 1)], (2 + i, c), E[n][:, 0:512], t, nfree))
                    scratch.put(n, sq[-1])
                yield "dve"
            t = inv_rms([2, 3], 4, D, 2, sq)
            xn = [ts(dve, W1[:, i, :], W1[:, i, :], ST[:, 2 + i:3 + i], None, ALU.mult, None, t) for i in range(2)]
            yield xn
            M = MOD[0]
            yield from feature_major(
                lambda i: W1[:, i, :], lambda k: (Hh[:, 0, k:k + 2, :], Hl[:, 0, k:k + 2, :]),
                lambda k: M[:, 1, k, 1:2], lambda k: M[:, 0, k, 1:2],
                lambda k: [xn, hfree, mod_ready[2, k // 4]] if (2, k // 4) in mod_ready else None, h2[0].__setitem__)
            made = pe.last
            for n in names:
                give(n, made)

        def latent_prep(s, src, src_tok, l, k_after):
            M = MOD[l % 2]
            c = 1 - s
            return feature_major(
                src, lambda k: (Hh[:, s, k:k + 2, :], Hl[:, s, k:k + 2, :]),
                lambda k: M[:, 1, k, c:c + 1], lambda k: M[:, 0, k, c:c + 1],
                lambda k: [src_tok, k_after, mod_ready[l, k // 4]], h2[s].__setitem__)

        def layer2(x_tok):
            finish("ctx")
            r = inv_rms([0, 1], 4, D, 0, x_tok)
            S2 = ST[:, 4:6]
            t = dve.do(lambda e: e.tensor_reduce(S2, SS[:, 4:6, 0:4], AX.X, ALU.add), x_tok)
            t = tt(dve, S2, S2, ST[:, 0:2], ALU.mult, t, r)
            t = tt(dve, S2, S2, ST[:, 0:2], ALU.mult, t)
            t = fn(ACT.Sqrt, S2, S2, t, bias=K("eps"), scale=1.0 / D)
            t = recip(S2, S2, t)
            t = tt(dve, S2, S2, ST[:, 0:2], ALU.mult, t)
            xn = [ts(dve, YB[:, 2048 * i:2048 * (i + 1)], YB[:, 4096 + 2048 * i:6144 + 2048 * i], ST[:, 4 + i:5 + i],
                     None, ALU.mult, None, t, places["TQ"]) for i in range(2)]
            xs = [fn(ACT.Copy, X[:, i, :], YB[:, 4096 + 2048 * i:6144 + 2048 * i], r, scale=ST[:, i:i + 1])
                  for i in range(2)]
            for i in range(2):
                spill = load(sp, out[128 * i:128 * (i + 1), :], X[:, i, :], spill_sem, xs[i])
            launch("prep", latent_prep(1, lambda i: YB[:, 2048 * i:2048 * (i + 1)], xn, 2, places["H1"]), front=True)

            def need_h(k):
                prepared(h2[1], k)
                return [h2[0][k], h2[1][k]]

            PH, PL = XR["PH"], XR["PL"]
            for _ in range(4):
                scratch.take()
            z = [fill(dve, E[i][:, :], 0.0, act.last, pe.last) for i in range(2)]
            U = [three(E[i][:, :], 2) for i in range(4)]
            u_free = [[z[0]], [z[1]]]
            pt, y_tok, yt_tok = {}, {}, {}
            grp_read = [xn, xs]
            Yk = YB[:, :].rearrange("p (k s n) -> p k s n", k=16, s=2)

            def pooled(g, i):
                w, slot = WINDOWS[g], i % 2

                def ev(o, t):
                    A, B, u = U[2], U[3], U[slot]
                    t = cp(act, u[:, :, 8:264], o, t, u_free[slot])
                    ev_tok = t
                    a, b = 8 - 7, 8 + 263
                    if w == 2:
                        a, b = 8, 264
                    t = tt(dve, A[:, :, a:b], u[:, :, a - 1:b - 1], u[:, :, a:b], ALU.add, t, scr_free)
                    cur, other, shift, width = A, B, 1, 2
                    while width < w:
                        width *= 2
                        shift = width // 4
                        a, b = (8, 264) if width == w else (a + shift, b - shift)
                        t = tt(dve, other[:, :, a:b], cur[:, :, a - shift:b - shift], cur[:, :, a + shift:b + shift],
                               ALU.add, t)
                        cur, other = other, cur
                    ed = bcast(cur[:, 0, 8:9], (272, 2), (248, 2), (1, 8))
                    t = tt(dve, ed, ed, bcast(K("edge", 16 * g), (0, 2), (8, 2), (1, 8)), ALU.mult, t)
                    n, nfree = og.take()
                    t = stt(dve, OG[n][:, :, :], cur[:, :, 8:264], 1.0 / w, u[:, :, 8:264], ALU.mult, ALU.subtract,
                            t, nfree)
                    u_free[slot] = [t]
                    scr_free[:] = [t]
                    t = split(three(PH[:, i, :], 2), three(PL[:, i, :], 2), OG[n][:, :, :], t, list(grp_read), spill)
                    og.put(n, t)
                    pt[i] = t
                    return ev_tok
                return ev

            scr_free = []

            def gate_ev(k):
                def ev(o, t):
                    t = fn(ACT.Silu, Yk[:, k], o, t, xn_read)
                    y_tok[k] = ts(pool, Yk[:, k], Yk[:, k], P("p_scale", k, k + 1), None, ALU.mult, None, t)
                    return t
                return ev

            def grp_ev(k):
                def ev(o, t):
                    yt_tok[k] = stt(dve, Yk[:, k], o, P("b_grp", k, k + 1), Yk[:, k], ALU.add, ALU.mult, t, y_tok[k])
                    return yt_tok[k]
                return ev

            def bank(b):
                return three(ps[:, b, :], 2)

            def rhs(k):
                return [p[:, :, k, :] for p in (Hh, Hl)]

            xn_read = None
            for g in range(4):
                for i in range(4):
                    b_tile(rhs, bank, need_h, pooled(g, i))
                    if xn_read is None:
                        xn_read = [pe.last]
                for i in range(4):
                    b_tile(rhs, bank, need_h, gate_ev(4 * g + i))
                h_read = pe.last
                for half in range(2):
                    jobs = []
                    for i in (2 * half, 2 * half + 1):
                        jobs.append((lambda k: [three(PH[:, k, :], 2), three(PL[:, k, :], 2)], bank,
                                     lambda k: pt[k], grp_ev(4 * g + i)))
                    b_half(jobs)
                    if g == 3 and half == 0:
                        early = y_parts(range(12), yt_tok, h_read, Yk)
                    pump()
                grp_read[:] = [pe.last]
            rest = y_parts(range(12, 16), yt_tok, h_read, Yk)
            parts = {**early, **rest}
            for i in range(4):
                scratch.put(i, [dve.last, act.last])

            lend(2)
            Y = YB[:, :].rearrange("p (t n) -> p t n", t=4)
            M = MOD[0]
            tiles = [(1, 0), (1, 1), (0, 0), (0, 1)]
            pump_until(lambda: (2, 5) in mod_ready)
            for i in range(2):
                reload = load(sp, X[:, i, :], out[128 * i:128 * (i + 1), :], reload_sem, grp_read, spill)
            ct0 = load(sp, CT[:, :], io["ctx_in"][0:128, :], ct_sem, pe.last)
            GB2 = [W["GB0"], GB1]
            gb_read = {0: [pe.last], 1: [dve.last]}
            sq, yg = {}, {}
            for c in range(4):
                gb = {}

                def make_gate(_, s, c=c, gb=gb):
                    launch("gate", row_broadcast(GB2[s][:, :], M[:, 2, 4 * c:4 * c + 4, 1 - s], list(gb_read[s]),
                                                 mod_ready[2, 4 + c // 2], gb, s))

                def ev(n, o, t, c=c, gb=gb):
                    s, i = tiles[n]
                    pump_until(lambda: s in gb)
                    j = 2 * s + i
                    e, efree = scratch.take()
                    t = sums(o, (j, c), E[e][:, 0:512], t, efree)
                    scratch.put(e, t)
                    sq[j, c] = t
                    t = tt(dve, Y[:, j, 512 * c:512 * (c + 1)], o, GB2[s][:, :], ALU.mult, t, gb[s])
                    gb_read[s] = [t]
                    yg[j, c] = t
                    return t

                chunk_a(lambda k, t: [p[:, t[0], k, 128 * t[1]:128 * (t[1] + 1)] for p in (Hh, Hl)], tiles, NKT,
                        lambda k: parts[k], [ev],
                        {(0, 3): lambda _: make_gate(_, 1), (0, 4): lambda _: make_gate(_, 0)})
            mod_read[0] = [dve.last, pool.last]
            lend(-2)
            y_read = pe.last

            ry = [inv_rms([2 + i], 4, D, 10 + i, [sq[2 + i, c] for c in range(4)]) for i in range(2)]
            xs, xn = [], []
            for i in range(2):
                q = []
                for c in range(4):
                    v = slice(512 * c, 512 * (c + 1))
                    t = stt(dve, X[:, i, v], Y[:, 2 + i, v], ST[:, 10 + i:11 + i], X[:, i, v], ALU.mult, ALU.add,
                            ry[i], yg[2 + i, 3], reload)
                    e, efree = scratch.take()
                    q.append(sums(X[:, i, v], (2 + i, c), E[e][:, 0:512], t, efree))
                    scratch.put(e, q[-1])
                xs.append(t)
                rx = inv_rms([2 + i], 4, D, 14 + i, q)
                xn.append(ts(dve, Y[:, 2 + i, :], X[:, i, :], ST[:, 14 + i:15 + i], None, ALU.mult, None, rx))
            for i in range(2):
                sp3 = load(sp, out[128 * i:128 * (i + 1), :], X[:, i, :], spill_sem, xs[i], reload)
            for s in (0, 1):
                h2[s].clear()
            lat = latent_prep(1, lambda i: Y[:, 2 + i, :], xn, 3, y_read)

            def context():
                yield "dve"
                ct_tok, xn = ct0, []
                for i in range(2):
                    r = inv_rms([i], 4, D, 8 + i, [sq[i, c] for c in range(4)])
                    q = []
                    for c in range(4):
                        v = slice(512 * c, 512 * (c + 1))
                        t = stt(dve, CT[:, v], Y[:, i, v], ST[:, 8 + i:9 + i], CT[:, v], ALU.mult, ALU.add,
                                r, yg[i, 3], ct_tok)
                        e, efree = scratch.take()
                        q.append(sums(CT[:, v], (i, c), E[e][:, 0:512], t, efree))
                        scratch.put(e, q[-1])
                        yield "dve"
                    r = inv_rms([i], 4, D, 12 + i, q)
                    t = ts(dve, Y[:, i, :], CT[:, :], ST[:, 12 + i:13 + i], None, ALU.mult, None, r)
                    xn.append(t)
                    if i == 0:
                        ct_tok = load(sp, CT[:, :], io["ctx_in"][128:256, :], ct_sem, t, q)
                    yield ct_tok if i == 0 else xn
                yield from latent_prep(0, lambda i: Y[:, i, :], xn, 3, y_read)

            return lat, context, sp3

        def y_parts(ks, yt_tok, h_read, Yk):
            return {k: split(Hh[:, :, k, :], Hl[:, :, k, :], Yk[:, k], yt_tok[k], h_read) for k in ks}

        def layer3(lat_prep, context, spill):
            cqT, ckT = [W["cqT_h"], W["cqT_l"]], [W["ckT_h"], W["ckT_l"]]
            kr = [W["kr_h"], W["kr_l"]]
            cq, ckv, RT = W["cq"], W["ckv"], W["rope"]
            V, Pm, PT = HU["V"], HU["Pm"], HU["PT"]
            qr = [HU["qr_h"], HU["qr_l"]]
            rope_sem = sem("rope")
            rope_tok = load(sp, RT[:, :], io["rope"], rope_sem, pe.last)

            def need_lat(k):
                prepared(h2[1], k)
                return h2[1][k]

            def need_ctx(k):
                prepared(h2[0], k)
                return h2[0][k]

            launch("prep", lat_prep, front=True)
            launch("ctx", context())

            def stat(k, t):
                return [p[:, t[0], k, 128 * t[1]:128 * (t[1] + 1)] for p in (Hh, Hl)]

            def low_rank(dst, sq, done, row):
                def ev(n, o, t):
                    done.append(fn(ACT.Copy, dst[:, n, :], o, t))
                    e, efree = scratch.take()
                    t = sums(o, (n, row), E[e][:, 0:512], t, efree)
                    scratch.put(e, t)
                    sq.append(t)
                    return t
                return ev

            cq_tok, cq_sq, ck_tok, ck_sq = [], [], [], []
            lat = [(1, 0), (1, 1)]
            keys = [(0, 0), (0, 1), (1, 0), (1, 1)]
            chunk_a(stat, lat, NKT, need_lat, [low_rank(cq, cq_sq, cq_tok, 4)])

            def normed(name, src, tok, sq, tiles, col, mul, dst, width, row):
                o = ST[:, col:col + tiles]
                t = cp(dve, o, SS[:, 0:tiles, row], sq)
                t = fn(ACT.Sqrt, o, o, t, bias=K("eps"), scale=1.0 / 512)
                t = recip(o, o, t)
                nt = [ts(dve, src[:, i, :], src[:, i, :], ST[:, col + i:col + i + 1], None, ALU.mult, None, t, tok)
                      for i in range(tiles)]
                yield nt
                per = 512 // width
                for b2 in range(4 // per):
                    b, free = side.take()
                    for j in range(per):
                        k = per * b2 + j
                        for i in range(tiles):
                            tp = tr(ps[:, b, width * j + 128 * i:width * j + 128 * (i + 1)],
                                    src[:, i, 128 * k:128 * (k + 1)], nt, free)
                    n, nfree = og.take()
                    flat_og = OG[n][:, :, :].rearrange("p a b -> p (a b)")
                    for j in range(per):
                        k = per * b2 + j
                        e = fn(ACT.Copy, flat_og[:, width * j:width * (j + 1)], ps[:, b, width * j:width * (j + 1)],
                               tp, nfree, scale=mul(k))
                    side.put(b, e)
                    k = per * b2
                    v = flat_og if per == 1 else OG[n][:, :, :]
                    h, l = (p[:, k, :] if per == 1 else p[:, k:k + 2, :] for p in dst)
                    t = cp(dve, h, v, e, pe.last)
                    t = tt(dve, l, v, h, ALU.subtract, t)
                    og.put(n, t)
                    for j in range(per):
                        done[name, k + j] = t
                    yield nt

            done = {}
            GX = X
            g_tok = {}

            def gate_chunk(c):
                def ev(n, o, t):
                    t = fn(ACT.Silu, GX[:, n, 512 * c:512 * (c + 1)], o, t, spill)
                    g_tok[c, n] = t
                    return t
                chunk_a(stat, lat, NKT, need_lat, [ev])

            gate_chunk(0)
            gate_chunk(1)
            pump_until(lambda: 15 in h2[0])
            launch("cq", normed("cq", cq, cq_tok, cq_sq, 2, 0, lambda k: P("q_norm", k, k + 1), cqT, 256, 4))
            chunk_a(stat, keys, NKT, lambda k: [need_ctx(k), need_lat(k)], [low_rank(ckv, ck_sq, ck_tok, 5)])
            launch("ckv", normed("ck", ckv, ck_tok, ck_sq, 4, 4, lambda k: P("kv_norm", k, k + 1), ckT, 512, 5))

            def turned(o, t, dst, free):
                s, sfree = scratch.take()
                v = E[s]
                t = cp(act, v[:, 0:256], o, t, sfree)
                bank_free = t
                yield bank_free
                b, bfree = side.take()
                tp = mm(ps[:, b, 0:256], RT[:, 512:640], v[:, 0:256], True, True, t, bfree, rope_tok)
                a = tt(dve, v[:, 256:512], ps[:, b, 0:256], RT[:, 256:512], ALU.mult, tp)
                side.put(b, a)
                c = tt(dve, v[:, 0:256], v[:, 0:256], RT[:, 0:256], ALU.mult, a)
                c = tt(dve, v[:, 0:256], v[:, 0:256], v[:, 256:512], ALU.add, c)
                t = split(dst[0], dst[1], v[:, 0:256], c, free)
                scratch.put(s, t)
                yield t

            kr_tok = {}

            def kr_ev(o, t):
                t1 = split(kr[0][:, 0:256], kr[1][:, 0:256], o[:, 0, :], t)
                kr_tok[0] = t1
                g = turned(o[:, 1, :], t1, [p[:, 256:512] for p in kr], None)
                t2 = next(g)

                def rest():
                    yield t2
                    kr_tok[1] = next(g)
                launch("kr", rest())
                return [t1, t2]

            b_tile(lambda k: [p[:, :, k, :] for p in (Hh, Hl)], lambda b: three(ps[:, b, :], 2),
                   lambda k: [h2[0][k], h2[1][k]], kr_ev)
            gate_chunk(2)
            gate_chunk(3)
            for n in ("cq", "ckv", "kr"):
                finish(n)
            h_read = pe.last

            qn = [[W[f"qn_h{i}"], W[f"qn_l{i}"]] for i in range(2)]
            kn = [[W[f"kn_h{i}"], W[f"kn_l{i}"]] for i in range(2)]
            scores_read = {i: [pe.last, dve.last, act.last] for i in range(2)}
            v_read = {0: [h_read], 1: [h_read]}
            qr_tok, v_tok, qk_tok, o_tok = {}, {}, {}, {}
            def attention(h):
                while p_free[h % 2] is None or not og.free or any(k not in qk_done for k in [h, ("r", h // 2)]):
                    yield 1
                r, o, pr = h % 2, 64 * (h % 2), h // 2 % 4
                P_, pfree, (n, nfree) = PP[r], p_free[r], og.take()
                p_free[r] = None
                yield qk_tok[h], qr_tok[h // 2]
                exps = []
                for i in range(2):
                    b, free = side.take()
                    q, k = [p[:, 128 * i:128 * (i + 1)] for p in qn[r]], [p[:, :] for p in kn[r]]
                    mm3(ps[:, b, :], q, k, True, False, qk_tok[h], free)
                    q, k = [p[o:o + 64, pr, 128 * i:128 * (i + 1)] for p in qr], [p[o:o + 64, :] for p in kr]
                    last = mm3(ps[:, b, :], q, k, False, True, qr_tok[h // 2], list(kr_tok.values()))
                    mx, o_, mn = MX[:, r, 2 * i:2 * i + 1], ps[:, b, :], MX[:, r, 2 * i + 1:2 * i + 2]
                    t = dve.do(lambda e, mx=mx, o_=o_: e.tensor_reduce(mx, o_, AX.X, ALU.max), [last, mx_free[r]], 0.6)
                    t = ts(dve, mn, mx, -MLA_SCALE, None, ALU.mult, None, t)
                    t = fn(ACT.Exp, P_[i], o_, t, pfree, rn_free[r], bias=mn, scale=MLA_SCALE,
                           accum_out=RN[:, r, i:i + 1])
                    side.put(b, t)
                    exps.append(t)
                scores_done.add(h)
                mx_free[r], scores_read[r] = exps[-1], [last]
                rn = recip(RN[:, r, 0:2], RN[:, r, 0:2], exps)
                for i in range(2):
                    g = ts(dve, OG[n][:, 0, 128 * i:128 * (i + 1)], GX[:, i, 128 * h:128 * (h + 1)],
                           RN[:, r, i:i + 1], None, ALU.mult, None, rn, g_tok[h // 4, i], nfree)
                rn_free[r] = [g]
                yield exps
                while places["PT"] is None:
                    yield 1
                pt_free, cps = own("PT"), []
                for i in range(2):
                    b, free = side.take()
                    for kt in range(4):
                        tp = tr(ps[:, b, 128 * kt:128 * (kt + 1)], P_[i][:, 128 * kt:128 * (kt + 1)], exps, free)
                    cps.append(cp((act, dve)[i], PT[:, :, 128 * i:128 * (i + 1)], three(ps[:, b, :], 4), tp, pt_free))
                    side.put(b, cps[-1])
                p_free[r] = [tp]
                b, free = side.take()
                for i in range(2):
                    tp = tr(ps[:, b, 128 * i:128 * (i + 1)], OG[n][:, 0, 128 * i:128 * (i + 1)], g, free)
                g = cp(act, OG[n][:, 1, :], ps[:, b, 0:256], tp)
                side.put(b, g)
                yield cps, v_tok[h // 4]
                b, free = side.take()
                for kt in range(4):
                    tp = mm(ps[:, b, 0:256], V[:, h // 4 % 2, kt, 128 * (h % 4):128 * (h % 4 + 1)], PT[:, kt, :],
                            kt == 0, kt == 3, cps, v_tok[h // 4], free)
                give("PT", tp)
                v_read[h // 4 % 2] = [tp]
                values_done.add(h)
                t = tt(dve, OG[n][:, 0, :], ps[:, b, 0:256], OG[n][:, 1, :], ALU.mult, tp, g)
                side.put(b, t)
                t = split(Hh[:, 0, h, :], Hl[:, 0, h, :], OG[n][:, 0, :], t, h_read)
                og.put(n, t)
                o_tok[h] = t

            mx_free, rn_free = {0: None, 1: None}, {0: None, 1: None}
            scores_done, values_done, qk_done = set(), set(), set()
            e2, e3 = [p for p in scratch.free if p[0] >= 2]
            scratch.free = [p for p in scratch.free if p[0] < 2]
            PP = [[Pm[:, 0, :], Pm[:, 1, :]], [E[2][:, 0:512], E[3][:, 0:512]]]
            p_free = [[h_read], [e2[1], e3[1]]]
            places["PT"] = [h_read]
            assert (3, 5) in mod_ready
            side.put(7, ada["bank"])

            def q_bank(b):
                return ps[:, b, 0:256]

            def q_stat(k):
                return [p[:, k, :] for p in cqT]

            def q_need(k):
                return done["cq", k]

            def k_stat(k):
                return [p[:, k, :] for p in ckT]

            def k_need(k):
                return done["ck", k]

            for g in range(4):
                pump_until(lambda: g < 2 or 4 * g - 5 in values_done)

                def v_ev(n, o, t, g=g):
                    t = fn(ACT.Copy, V[:, g % 2, n, :], o, t, v_read[g % 2])
                    v_tok.setdefault(g, []).append(t)
                    return t

                chunk_a(lambda k, t: [p[:, k, 256 * t[0] + 128 * t[1]:256 * t[0] + 128 * (t[1] + 1)] for p in ckT],
                        keys, 4, k_need, [v_ev])
                if g % 2 == 0:
                    pump_until(lambda: g == 0 or 4 * g - 1 in scores_done)
                    qr_read = [pe.last]
                    for half in range(2):
                        jobs, gens = [], []
                        for i in (2 * half, 2 * half + 1):
                            def ev(o, t, i=i):
                                gen = turned(o, t, [p[:, i, :] for p in qr], qr_read)
                                gens.append((i, gen))
                                return next(gen)
                            jobs.append((q_stat, q_bank, q_need, ev))
                        b_half(jobs)
                        for i, gen in gens:
                            qr_tok[2 * g + i] = next(gen)
                            qk_done.add(("r", 2 * g + i))
                for j in range(4):
                    h = 4 * g + j
                    pump_until(lambda: h < 2 or h - 2 in scores_done)
                    launch("head", attention(h))

                    def part_ev(dst, h=h):
                        def ev(o, t):
                            t = split(dst[0][:, :], dst[1][:, :], o, t, scores_read[h % 2])
                            qk_tok.setdefault(h, []).append(t)
                            return t
                        return ev
                    b_half([(q_stat, q_bank, q_need, part_ev(qn[h % 2])),
                            (k_stat, lambda b: ps[:, b, :], k_need, part_ev(kn[h % 2]))])
                    qk_done.add(h)
                    pump()

            def need_o(k):
                pump_until(lambda: k in o_tok)
                if k == 15 and len(scratch.free) == 2:
                    scratch.free += [(2, p_free[1]), (3, p_free[1])]
                return o_tok[k]

            Y = W["Y2"]
            M = MOD[1]
            GBs = [GB1, W["GB0"]]
            gb_read, sq, yg = {0: [dve.last], 1: [dve.last, pe.last]}, {}, {}

            def out_chunk(c):
                gb, b = {}, c % 2

                def hook(_):
                    launch("gate", row_broadcast(GBs[b][:, :], M[:, 2, 4 * c:4 * c + 4, 0], gb_read[b],
                                                 mod_ready[3, 4 + c // 2], gb, "g"))

                def ev(n, o, t):
                    pump_until(lambda: "g" in gb)
                    e, efree = scratch.take()
                    t = sums(o, (n, c), E[e][:, 0:512], t, efree)
                    scratch.put(e, t)
                    sq[n, c] = t
                    t = tt(dve, Y[:, n, 512 * c:512 * (c + 1)], o, GBs[b][:, :], ALU.mult, t, gb["g"])
                    gb_read[b] = [t]
                    yg[n, c] = t
                    return t
                return ev, hook

            def o_stat(k, t):
                return [p[:, 0, k, 128 * t[1]:128 * (t[1] + 1)] for p in (Hh, Hl)]

            (ev0, hook0), (ev1, hook1) = out_chunk(0), out_chunk(1)
            chunk_a(o_stat, lat, NKT, need_o, [ev0, ev1], {(0, 2): hook0, (1, 2): hook1})
            for i in range(2):
                reload = load(sp, X[:, i, :], out[128 * i:128 * (i + 1), :], reload_sem, dve.last, spill)
            for c in (2, 3):
                ev, hook = out_chunk(c)
                chunk_a(o_stat, lat, NKT, need_o, [ev], {(0, 2): hook})
            for i in range(2):
                r = inv_rms([i], 4, D, 8 + i, [sq[i, c] for c in range(4)])
                t = stt(dve, X[:, i, :], Y[:, i, :], ST[:, 8 + i:9 + i], X[:, i, :], ALU.mult, ALU.add, r, yg[i, 3], reload)
                o_done = load(sp, out[128 * i:128 * (i + 1), :], X[:, i, :], spill_sem, t)
            sp.do(lambda e: None, [o_done])

        x_sums = []
        for i in range(2):
            for c in range(4):
                n, free = scratch.take()
                x_sums.append(sums(X[:, i, 512 * c:512 * (c + 1)], (i, c), E[n][:, 0:512], x_tok, free))
                scratch.put(n, x_sums[-1])
        x_tok = x_sums
        if upto is None or upto > 0:
            x_tok = layer1(0, x_tok)
        if upto is None or upto > 1:
            x_tok = layer1(1, x_tok)
        if upto is None or upto > 2:
            prep, context, sp3 = layer2(x_tok)
        if upto is None:
            layer3(prep, context, sp3)
        if upto is not None:
            sp.do(lambda e: None, st["loaded"][-NR:] + ([sp3] if upto > 2 else []))
        for q in (pe, act, dve, pool, sp):
            q.number()
        block = ctx.enter_context(nc.Block())

        @block.sync
        def _(e):
            sp.play(e)

        @block.scalar
        def _(e):
            act.play(e)

        @block.tensor
        def _(e):
            pe.play(e)

        @block.vector
        def _(e):
            dve.play(e)

        @block.gpsimd
        def _(e):
            pool.play(e)


def kernel(**inputs):
    import concourse.bacc as _bacc
    from concourse.bass_utils import run_bass_kernel_spmd as _run

    arrays = lay_out({n: np.asarray(a) for n, a in inputs.items()})
    nc = _bacc.Bacc("TRN2", target_bir_lowering=False, num_devices=1)
    io = {n: nc.dram_tensor("in_" + n, a.shape, mybir.dt.from_np(a.dtype), kind="ExternalInput").ap()
          for n, a in arrays.items()}
    out = nc.dram_tensor("out_x", (256, 2048), F, kind="ExternalOutput").ap()
    program(nc, io, out)
    r = _run(nc, [{"in_" + n: a for n, a in arrays.items()}], core_ids=[0])
    return r.results[0]["out_x"].reshape(1, 256, 2048)
```

```python
import concourse.bass as bass
from concourse import mybir
from contextlib import ExitStack
import numpy as np

F = mybir.dt.float32
R = mybir.dt.float32r
ACT = mybir.ActivationFunctionType
ALU = mybir.AluOpType
AX = mybir.AxisListType

D = 2048
NKT = 16
EPS = 1e-6
MASKED = -1.0e30
MLA_SCALE = (128 + 64) ** -0.5
WINDOWS = (2, 4, 8, 16)
PIECES = ["f_x", "f_g", "na_q", "na_k", "na_v", "na_g", "r_q", "r_k", "r_v", "r_g",
          "cv_a", "cv_b", "cv_g"]
ORDER = ["cv_a", "cv_b", "na_v", "na_q", "na_k", "na_g", "r_v", "r_q", "r_k", "r_g",
         "f_x", "cv_g", "f_g"]
EARLY_PIECES = ["cv_a", "cv_b", "na_v", "r_v", "f_x", "na_g"]
OUT_ORDER = ["na", "ret", "cv", "fft"]
CONCAT = ["fft", "na", "ret", "cv"]

CONST_COLS = {}


def _const_columns():
    at = 0
    for name, n in [("ident", 128), ("sel", 4), ("eps", 1), ("cc", 256), ("dist_f", 384), ("dist_b", 384),
                    ("hsel", 2), ("cosr", 64), ("sinr", 128), ("mask", 64), ("edge", 64)]:
        CONST_COLS[name] = (at, at + n)
        at += n
    return at


NCONST = _const_columns()


def constants():
    k = np.zeros((128, NCONST), np.float64)

    def put(name, a):
        lo, hi = CONST_COLS[name]
        k[:, lo:hi] = np.asarray(a).reshape(128, hi - lo)

    p = np.arange(128)
    put("ident", np.eye(128))
    ang = 2 * np.pi * ((p[:, None] * p[None, :]) % 128) / 128
    norm = 1.0 / np.sqrt(256 * 128)
    put("cc", np.concatenate([np.cos(ang) * norm, -np.sin(ang) * norm], axis=1))
    m = np.arange(384)[None, :] - 128 - p[:, None]
    put("dist_f", np.maximum(m, 0))
    put("dist_b", np.maximum(-m, 0))
    sel = np.zeros((128, 4))
    for i, rows in enumerate([(0, 64), (1, 65), (32, 96), (33, 97)]):
        sel[list(rows), i] = 1
    put("sel", sel)
    put("hsel", np.stack([p < 64, p >= 64], axis=1))
    inv = 10000.0 ** (-np.arange(32, dtype=np.float32) / np.float32(32))
    tok = np.arange(2)[None, :, None] * 128 + p[:, None, None]
    a = (tok.astype(np.float32) * inv.astype(np.float32)[None, None, :]).astype(np.float64)
    put("cosr", np.cos(a))
    put("sinr", np.stack([-np.sin(a), np.sin(a)], axis=2))
    col = p % 64
    start = np.clip(col - 8, 0, 48)
    rel = np.arange(64)[None, :] - start[:, None]
    put("mask", np.where((rel >= 0) & (rel < 16), 0.0, MASKED))
    put("eps", np.full((128, 1), EPS))
    edge = np.ones((4, 2, 8))
    for g, w in enumerate(WINDOWS):
        left, right = w // 2, w - 1 - w // 2
        for side, t0 in enumerate((0, 248)):
            for i in range(8):
                t = t0 + i
                cnt = min(t + right + 1, 256) - max(t - left, 0)
                edge[g, side, i] = w / cnt
    put("edge", np.broadcast_to(edge.reshape(1, 64), (128, 64)))
    return k.astype(np.float32)


def dft_tokens():
    n = np.arange(256)
    ang = 2 * np.pi * ((n[:, None] * n[None, :]) % 256) / 256
    t = np.concatenate([np.cos(ang)[:, :129], np.sin(ang)[:, 1:128]], axis=1)
    return np.ascontiguousarray(t.reshape(2, 128, 256).transpose(1, 0, 2)).reshape(128, 512).astype(np.float32)


def rope_tables():
    d = np.arange(128) % 64
    n = np.arange(256)
    freqs = (10000.0 ** (-np.arange(16, dtype=np.float32) / np.float32(16))).astype(np.float32)
    pos = np.where((d < 32)[:, None], (n // 64)[None, :], (n % 64)[None, :]).astype(np.float32)
    ang = (pos * freqs[d % 16][:, None]).astype(np.float32).astype(np.float64)
    sign = np.where(d % 32 < 16, -1.0, 1.0)[:, None]
    swap = np.zeros((128, 128))
    i = np.arange(128)
    swap[i ^ 16, i] = 1
    return np.concatenate([np.cos(ang), np.sin(ang) * sign, swap], axis=1).astype(np.float32)


def pack_a(w):
    k, n = w.shape
    t = w.reshape(k // 512, 4, 128, n // 512, 512).transpose(3, 0, 2, 1, 4)
    return np.ascontiguousarray(t).reshape(n // 512, k // 512, 128, 2048)


def pack_b(w):
    k, n = w.shape
    t = w.reshape(16, 128, n // 128, 128).transpose(2, 1, 0, 3)
    return np.ascontiguousarray(t).reshape(n // 128, 128, 2048)


def pack_b4(w):
    t = w.reshape(4, 128, w.shape[1] // 512, 4, 128).transpose(2, 1, 3, 0, 4)
    return np.ascontiguousarray(t).reshape(w.shape[1] // 512, 128, 2048)


def pack_ada(w):
    t = w.reshape(8, 2, 128, 3, 4, 512)
    mod = t[:, :, :, 0:2].transpose(4, 0, 2, 1, 3, 5)
    gate = w.reshape(16, 128, 3, 2048)[:, :, 2]
    return np.concatenate([mod.reshape(32, 128, 2048), gate])


def pack_ada_bias(b):
    t = b.reshape(3, 4, 512)
    blocks = [t[i, j] for j in range(4) for i in range(2)] + list(t[2])
    return np.stack([np.stack([v, v]) for v in blocks])


def cols(v):
    return np.asarray(v).reshape(-1, 128).T


PARAM_COLS = {}


def _param_columns():
    at = 0
    for name, n in [("norm_g", 32), ("conv", 272), ("logit", 32), ("pre", 32),
                    ("b_grp", 16), ("p_scale", 16), ("q_norm", 4), ("kv_norm", 4), ("c", 48)]:
        PARAM_COLS[name] = (at, at + n)
        at += n
    return at


NPARAM = _param_columns()


def lay_out(i):
    o = {}
    o["x_in"] = i["x"][0]
    o["ctx_in"] = i["ctx_2"][0]
    out_rows = [CONCAT.index(n) for n in OUT_ORDER]
    o["w_ada"] = np.stack([pack_ada(w) for w in i["w_ada"]] + [pack_ada(w) for w in i["ada_w_2"]])
    o["b_ada"] = np.stack([pack_ada_bias(b) for b in i["b_ada"]] + [pack_ada_bias(b) for b in i["ada_b_2"]])
    o["w_in"] = np.stack([pack_a(w) for w in i["w_in"]])
    o["w_fft"] = np.stack([pack_a(w) for w in i["w_fft"]])
    o["w_pw"] = np.stack([pack_a(w) for w in i["conv_w_pw"]])
    o["w_out"] = np.stack([pack_a(w.reshape(4, 512, 2048)[out_rows].reshape(2048, 2048)) for w in i["w_out"]])
    conv = np.concatenate([i["conv_w"], i["conv_b"][:, None], i["conv_ln_g"][:, None], i["conv_ln_b"][:, None]], axis=1)
    conv = conv.reshape(2, 34, 4, 128).transpose(3, 0, 2, 1).reshape(128, 272)
    logit = np.stack([i["ret_logit_fwd"], i["ret_logit_bwd"]], axis=1).reshape(1, 32)
    c = np.stack([cols(i["c"][0]), cols(i["c_2"][0]), cols(i["c_ctx_2"])], axis=2).reshape(128, 48)
    parts = {"norm_g": cols(i["norm_g"]), "conv": conv, "logit": np.broadcast_to(logit, (128, 32)),
             "pre": cols(i["pre_norm_2"]),
             "b_grp": cols(i["pool_b_grp_2"]), "p_scale": cols(i["pool_scale_2"]),
             "q_norm": cols(i["mla_q_norm_2"]), "kv_norm": cols(i["mla_kv_norm_2"]), "c": c}
    o["rows"] = np.stack([i["final_g"], i["post_norm_2"][0], i["post_norm_2"][1]]).reshape(3, 4, 512)
    o["params"] = np.concatenate([parts[n] for n in PARAM_COLS], axis=1)
    t = np.pad(i["na_rel_bias"], ((0, 0), (0, 0), (0, 0), (48, 48)))
    half, cc = np.arange(128)[:, None, None] // 64, np.arange(128)[:, None, None] % 64
    m, c2 = np.arange(6)[None, :, None], np.arange(64)[None, None, :]
    o["na_bias"] = np.ascontiguousarray(t[:, :, m + 5 - half, c2 - cc + 63]).reshape(2, 8, 128, 384)
    o["pool_in"] = pack_b(i["pool_w_in_2"][0])
    o["pool_grp"] = np.concatenate([pack_b4(w) for w in i["pool_w_grp_2"][0]])
    o["pool_out"] = pack_a(i["pool_w_out_2"][0])
    w = i["mla_w_in_2"][0]
    o["mla_in"] = pack_a(np.concatenate([w[:, :1024], w[:, 1088:]], axis=1))
    o["mla_kr"] = pack_b(np.concatenate([w[:, 1024:1088]] * 2, axis=1))
    uq = i["mla_w_uq_2"][0].reshape(512, 16, 192)
    ukv = i["mla_w_ukv_2"][0].reshape(512, 16, 256)
    qk = np.stack([uq[:, :, :128], ukv[:, :, :128]], axis=2).reshape(4, 128, 8, 2, 2, 128)
    o["mla_qk"] = np.ascontiguousarray(qk.transpose(2, 1, 3, 4, 0, 5)).reshape(8, 128, 2048)
    o["mla_rope"] = pack_b4(np.ascontiguousarray(uq[:, :, 128:]).reshape(512, 1024))
    o["mla_v"] = pack_a(np.ascontiguousarray(ukv[:, :, 128:]).reshape(512, 2048))
    o["mla_out"] = pack_a(i["mla_w_out_2"][0])
    o["const"] = constants()
    o["dft"] = dft_tokens()
    o["rope"] = rope_tables()
    return {n: np.ascontiguousarray(a) for n, a in o.items()}


class Token:

    def __init__(self, sem, value=None, due=0.0):
        self.sem, self.value, self.hit, self.due = sem, value, False, due


def flat(after):
    for t in after:
        if t is None:
            continue
        if isinstance(t, (list, tuple)):
            yield from flat(t)
        else:
            yield t


class Queue:

    def __init__(self, sem):
        self.sem, self.ops, self.last, self.t = sem, [], None, 0.0

    def do(self, fn, after=(), cost=0.1):
        after = list(flat(after))
        for t in after:
            t.hit = True
            self.t = max(self.t, t.due + 0.06)
        self.t += cost
        tok = Token(self.sem, None, self.t)
        self.ops.append((fn, after, tok))
        self.last = tok
        return tok

    def number(self):
        n = 0
        for _, _, tok in self.ops:
            if tok.value is None and tok.hit:
                n += 1
                tok.value = n

    def play(self, e):
        seen = {}
        for fn, after, tok in self.ops:
            need = {}
            for t in after:
                need[t.sem.name] = max(need.get(t.sem.name, (0, t.sem)), (t.value, t.sem), key=lambda p: p[0])
            for name, (v, sem) in need.items():
                if seen.get(name, 0) < v:
                    e.wait_ge(sem, v)
                    seen[name] = v
            ins = fn(e)
            if tok.hit and tok.sem is self.sem:
                ins.then_inc(self.sem, 1)


class Slots:

    def __init__(self, places):
        self.free = [(p, []) for p in places]

    def take(self):
        return self.free.pop(0)

    def put(self, place, toks):
        self.free.append((place, list(flat([toks]))))


def bcast(ap, *dims):
    return bass.AP(tensor=ap.tensor, offset=ap.offset, ap=[list(ap.ap[0])] + [list(d) for d in dims])


def three(ap, a):
    return ap.rearrange("p (a b) -> p a b", a=a)


def weave(main, ada, over, bend=1.0):
    res, k = [], 0
    for n, u in enumerate(main):
        res.append(u)
        want = len(ada) if n + 1 >= over else int(len(ada) * ((n + 1) / over) ** bend)
        res += ada[k:want]
        k = max(k, want)
    return res


def program(nc, io, out):
    ctx = ExitStack()
    with ctx:
        def sb(name, shape, dt, c=ctx):
            return c.enter_context(nc.sbuf_tensor("s_" + name, shape, dt))

        def sem(name):
            return ctx.enter_context(nc.semaphore("m_" + name))

        NR, NH = 4, 3
        KC = sb("const", [128, NCONST], F)
        PR = sb("params", [128, NPARAM], F)
        raw = [sb(f"raw{i}", [128, 2048], F) for i in range(NR)]
        hi_s = [sb(f"hi{i}", [128, 1024], R) for i in range(NH)]
        lo_s = [sb(f"lo{i}", [128, 1024], R) for i in range(NH)]
        E = [sb(f"E{i}", [128, 544], F) for i in range(4)]
        OG = [sb(f"og{i}", [128, 2, 256], F) for i in range(2)]
        GB1 = sb("gb1", [128, 512], F)
        CS = sb("cs", [128, 16, 3], F)
        MOD = [sb(f"mod{i}", [128, 2, 16, 2], F) for i in range(2)]
        ROWS = sb("rows", [128, 512], F)
        BR = sb("br", [128, 512], F)
        SS = sb("ss", [128, 6, 6], F)
        ST = sb("stat", [128, 16], F)
        LG = sb("lg", [128, 6, 32], F)
        RN = sb("rn", [128, 2, 16], F)
        MX = sb("mx", [128, 2, 4], F)
        BN = sb("bn", [128, 2, 16], F)

        def overlay(*variants):
            made, size = {}, 0
            for n_var, names in enumerate(variants):
                c, n = ExitStack(), 0
                for name, shape, dt in names:
                    made[name] = sb(name or f"gap{n_var}_{variants[0][0][0]}_{n}", shape, dt, c)
                    n += 4 * int(np.prod(shape[1:]))
                c.close()
                size = max(size, n)
            return made, size

        W, size = overlay(
            [("W1", [128, 2, 2048], F), ("G", [128, 2, 2, 512], F), ("qT", [128, 4, 256], F),
             ("kT", [128, 4, 256], F), ("dec", [128, 2, 384], F), ("nb", [128, 2, 384], F),
             ("dft", [128, 2, 256], F), ("", [128, 512], F)],
            [("YB", [128, 8192], F), ("CT", [128, 2048], F), ("GB0", [128, 512], F)],
            [("cqT_h", [128, 4, 256], R), ("cqT_l", [128, 4, 256], R), ("ckT_h", [128, 4, 512], R),
             ("ckT_l", [128, 4, 512], R), ("cq", [128, 2, 512], F), ("ckv", [128, 4, 512], F),
             ("kr_h", [128, 512], R), ("kr_l", [128, 512], R), ("rope", [128, 640], F)],
            [("Y2", [128, 2, 2048], F), ("", [128, 2048], F)] +
            [(f"{n}{i}", [128, k], R) for i in range(2)
             for n, k in (("qn_h", 256), ("qn_l", 256), ("kn_h", 512), ("kn_l", 512))])
        sb("room_w", [128, size // 4], F)
        XR, size = overlay([("X", [128, 2, 2048], F)], [("PH", [128, 4, 512], R), ("PL", [128, 4, 512], R)])
        sb("room_x", [128, size // 4], F)
        HU, _ = overlay(
            [("", [128, 4096], F), ("S0", [128, 2, 2, 512], F), ("uT", [128, 4, 286], F), ("", [128, 5000], F),
             ("S1", [128, 2, 2, 512], F)],
            [("", [128, 6144], F), ("PQ", [128, 4, 512], F), ("", [128, 6144], F), ("acc", [128, 4, 256], F),
             ("FX", [128, 2, 512], F)],
            [("", [128, 4096], F), ("V", [128, 2, 4, 512], F), ("", [128, 4096], F), ("qr_h", [128, 4, 256], R),
             ("qr_l", [128, 4, 256], R), ("Pm", [128, 2, 512], F), ("PT", [128, 4, 256], F)])
        Hh = sb("Hh", [128, 2, 16, 256], R)
        Hl = sb("Hl", [128, 2, 16, 256], R)
        ps = ctx.enter_context(nc.psum_tensor("ps", [128, 8, 512], F))

        pe, act, dve, pool, sp = (Queue(sem(n)) for n in ("pe", "act", "dve", "pool", "sp"))
        ring_sems = [sem(f"ring{i}") for i in range(NR)]
        loaded, bus, table = {}, [0.0], [None]

        def K(name, lo=0, hi=None):
            a, b = CONST_COLS[name]
            return KC[:, a + lo:(b if hi is None else a + hi)]

        def P(name, lo=0, hi=None):
            a, b = PARAM_COLS[name]
            return PR[:, a + lo:(b if hi is None else a + hi)]

        def size(ap):
            return int(np.prod(ap.shape[1:]))

        def load(q, dst, src, s, *after):
            loaded[s.name] = loaded.get(s.name, 0) + 16
            last = q.last
            t = q.do(lambda e: e.dma_start(dst, src).then_inc(s, 16), after, 0.05)
            q.last = last
            bus[0] = max(bus[0], t.due) + 128 * 4 * size(dst) / 360e3
            return Token(s, loaded[s.name], bus[0] + 2.0)

        def mm(o, l, r, first, last, *after):
            passes = 1 if l.dtype == R else 4
            return pe.do(lambda e: e.matmul(o, l, r, start=first, stop=last, skip_group_check=True), after,
                         max(0.02, passes * size(r) * 0.00042 * (0.27 if size(l) < 4 else 1)))

        def mm3(o, l, r, first, last, *after):
            mm(o, l[0], r[0], first, False, *after)
            mm(o, l[0], r[1], False, False)
            return mm(o, l[1], r[0], False, last)

        def tr(o, i, *after):
            ident = K("ident")
            return pe.do(lambda e: e.transpose(o, i, ident), after, 0.055)

        def vcost(q, o, rate=0.00104):
            return 0.1 + 0.0023 * size(o) if q is pool else 0.065 + rate * size(o)

        def tt(q, o, a, b, op, *after):
            return q.do(lambda e: e.tensor_tensor(o, a, b, op), after, vcost(q, o))

        def ts(q, o, a, s1, s2, op0, op1, *after):
            if op1 is None:
                return q.do(lambda e: e.tensor_scalar(o, a, s1, None, op0), after, vcost(q, o, 0.0007))
            return q.do(lambda e: e.tensor_scalar(o, a, s1, s2, op0, op1), after, vcost(q, o, 0.0007))

        def stt(q, o, a, s1, b, op0, op1, *after):
            return q.do(lambda e: e.scalar_tensor_tensor(out=o, in0=a, scalar=s1, in1=b, op0=op0, op1=op1), after,
                        vcost(q, o))

        def cp(q, o, a, *after):
            if q is act:
                return q.do(lambda e: e.activation(o, a, ACT.Copy), after, 0.1 + 0.00084 * size(o))
            return q.do(lambda e: e.tensor_copy(o, a), after, vcost(q, o))

        def fn(f, o, a, *after, **kw):
            cost = 0.1 + 0.00084 * size(o)
            if f not in (ACT.Copy, ACT.Square, ACT.Identity, table[0]):
                cost += 1.3
                table[0] = f
            return act.do(lambda e: e.activation(o, a, f, **kw), after, cost)

        def fill(q, o, v, *after):
            return q.do(lambda e: e.memset(o, v), after)

        def recip(o, a, *after):
            return dve.do(lambda e: e.reciprocal(o, a), after)

        def split(h, l, v, *after):
            t = cp(act, h, v, *after)
            return tt(dve, l, v, h, ALU.subtract, t)

        main = Slots([0, 1, 2, 3])
        side = Slots([4, 5, 6])
        scratch = Slots([0, 1, 2, 3])
        og = Slots([0, 1])

        def pair(name, l=None):
            v = io[name] if l is None else io[name][l]
            order = [(c, i) for i in range(4) for c in range(2)] + [(c, i) for c in (2, 3) for i in range(4)]
            return [("w", v[c, i]) for c, i in order]

        def w_units(l):
            if l < 2:
                early = EARLY_PIECES if l == 0 else []
                u = [("w", io["w_in"][l, PIECES.index(p), i]) for i in range(4) for p in early]
                u += [("w", io["w_in"][l, PIECES.index(p), i]) for p in ORDER if p not in early for i in range(4)]
                return u + [("w", io["w_pw"][l, 0, 0]), ("w", io["w_fft"][l, 0, 0])] + pair("w_out", l)
            if l == 2:
                u = []
                for g in range(4):
                    u += [("w", io["pool_in"][4 * g + i]) for i in range(4)]
                    u += [("w", io["pool_in"][16 + 4 * g + i]) for i in range(4)]
                    u += [("w", io["pool_grp"][g])]
                return u + [("w", io["pool_out"][c, i]) for c in (0, 1, 2, 3, 3) for i in range(4)]
            chunk = [[("w", io["mla_in"][c, i]) for i in range(4)] for c in range(6)]
            u = chunk[0] + chunk[2] + chunk[3] + chunk[1] + [("w", io["mla_kr"][0])] + chunk[4] + chunk[5]
            for g in range(4):
                u += [("w", io["mla_v"][g, 0])]
                if g % 2 == 0:
                    u += [("w", io["mla_rope"][g // 2])]
                u += [("w", io["mla_qk"][2 * g + i]) for i in range(2)]
            return u + pair("mla_out")

        def a_units(l, jobs):
            return [("ada", io["w_ada"][l, 8 * j + u], l, j, u) for j in jobs for u in range(8 if j < 4 else 16)]

        NEP, FIRST = len(EARLY_PIECES), (3, 4, 5, 6, 7, 8, 8)
        first, m0 = [a_units(0, [j]) for j in range(4)], w_units(0)
        units = first[0]
        for j in range(1, 4):
            units += first[j][:FIRST[0]]
            for i in range(NEP):
                units += [m0[NEP * (j - 1) + i]] + first[j][FIRST[i]:FIRST[i + 1]]
        units += weave(m0[3 * NEP:], a_units(0, (4,)) + a_units(1, range(4)), 68 - 3 * NEP) + a_units(1, (4,))[:5]
        units += weave(w_units(1), a_units(1, (4,))[5:] + a_units(2, range(4)), 54)
        units += a_units(2, (4,))[:2]
        units += weave(w_units(2), a_units(2, (4,))[2:] + a_units(3, range(4)), 46, 1.1)
        units += a_units(3, (4,))[:3]
        units += weave(w_units(3), a_units(3, (4,))[3:], 14)

        st = dict(consumed_upto=0, dma=0, pos=0, half=0, split=0, loaded=[], raw_free=[[] for _ in range(NR)])
        halves = [(n, h) for n, u in enumerate(units) if u[0] == "w" for h in range(2)]
        hl = Slots(range(NH))
        ready = {}

        def more_loads():
            while st["dma"] < len(units) and st["dma"] - NR < st["consumed_upto"]:
                n = st["dma"]
                st["loaded"].append(load(sp, raw[n % NR][:, :], units[n][1], ring_sems[n % NR], st["raw_free"][n % NR]))
                st["dma"] += 1

        done_units = set()

        def unit_read(n, tok):
            st["raw_free"][n % NR] = [tok]
            done_units.add(n)
            while st["consumed_upto"] in done_units:
                st["consumed_upto"] += 1
            more_loads()

        def more_splits(needed=None):
            while st["split"] < len(halves) and hl.free:
                n, h = halves[st["split"]]
                if n >= st["dma"]:
                    return
                if st["split"] != needed and max(t.due for t in flat([st["loaded"][n], hl.free[0][1]])) > \
                        max(pe.t, dve.t) + EARLY:
                    return
                i, free = hl.take()
                v = raw[n % NR][:, 1024 * h:1024 * (h + 1)]
                t = split(hi_s[i][:, :], lo_s[i][:, :], v, st["loaded"][n], free)
                ready[st["split"]] = (i, t)
                st["split"] += 1
                if h == 1:
                    unit_read(n, t)

        sides = []

        SLACK, CALM, AHEAD, EARLY = 4.5, 1.0, 4, -0.5

        def is_due(s):
            w = s["wait"]
            if isinstance(w, int):
                s["wait"] = w - 1
                return w <= 0
            if dve.t > pe.t + SLACK or act.t > pe.t + SLACK:
                return False
            if w == "dve":
                return dve.t <= pe.t + CALM
            if not side.free:
                return False
            return all(t.due <= pe.t + 0.1 for t in flat([w, side.free[0][1]]))

        def need_time(s):
            return max([pe.t] + [t.due for t in flat([s["wait"]])]) if s["wait"] != "dve" else dve.t

        def step(s):
            try:
                s["wait"] = next(s["gen"])
                s["wait"] = 0 if s["wait"] is None else s["wait"]
            except StopIteration:
                sides.remove(s)

        def pump(budget=3.3):
            more_splits()
            begin, went = pe.t, True
            while went and pe.t < begin + budget:
                went = False
                for s in [s for s in sides if not s["last"]]:
                    if is_due(s):
                        step(s)
                        went = went or not isinstance(s["wait"], int)
                for s in [s for s in sides if s["last"]][:1]:
                    if is_due(s):
                        step(s)

        def lend(n):
            a, b = (side, main) if n > 0 else (main, side)
            for bank in (4, 5)[:abs(n)]:
                at = [f for f in a.free if f[0] == bank]
                assert at
                a.free.remove(at[0])
                b.free.insert(0, at[0])

        def launch(name, gen, front=False, start=False, last=False):
            s = dict(name=name, gen=gen, wait=0, last=last)
            if front:
                sides.insert(0, s)
            else:
                sides.append(s)
            if start:
                step(s)

        def finish(name):
            for s in list(sides):
                if s["name"] == name:
                    for _ in s["gen"]:
                        pass
                    sides.remove(s)

        def work_off_ada():
            while units[st["pos"]][0] == "ada":
                ada_unit(st["pos"])
                st["pos"] += 1
                pump()

        def pump_until(there):
            for _ in range(2000):
                if there():
                    return
                waiting = []
                for s in list(sides):
                    if isinstance(s["wait"], int):
                        if is_due(s):
                            step(s)
                    else:
                        waiting.append(s)
                if there() or not waiting:
                    continue
                now = [s for s in waiting if is_due(s)]
                step(now[0] if now else min(waiting, key=need_time))
            raise AssertionError("no side job leads there: " + str([s["name"] for s in sides]))

        def prepared(h, k, can=lambda k: True):
            for j in range(k, min(k + AHEAD, NKT - 1) + 1, 2):
                if j == k or can(j):
                    pump_until(lambda: j in h)
            return h[k]

        def next_half():
            work_off_ada()
            k = st["half"]
            more_splits(k)
            st["half"] += 1
            if k % 2 == 1:
                st["pos"] += 1
            i, t = ready.pop(k)
            return (hi_s[i], lo_s[i]), t, i

        def give_back(i, tok):
            hl.put(i, tok)
            more_splits()

        def room(n):
            while len(scratch.free) < n:
                yield 1

        ada = dict(bank=[], rows=[], br=[])
        mod_ready, mod_read = {}, {0: [], 1: []}
        br_sem, gates_sem = sem("br"), sem("gates")
        gates = nc.dram_tensor("gates", (4, 4, 2, 512), F, kind="Internal").ap()

        def load_rows(src, s, *after):
            for i, row in enumerate(src):
                t = load(sp, BR[32 * i:32 * i + 2, :], row, s, *after)
            return t

        def ada_unit(n):
            _, _, l, j, u = units[n]
            (c0, m), gate = (0, 1) if l < 2 else (1, 2), j == 4
            for s in range(4):
                o, k = ps[32 * s:32 * s + m, 7, :], u if gate else 2 * u + s // 2
                last = mm(o, CS[:, k, c0:c0 + m], raw[n % NR][:, 512 * s:512 * (s + 1)],
                          u == 0, u == (15 if gate else 7), st["loaded"][n], cs_ready,
                          ada["bank"] if u == 0 else None)
            unit_read(n, last)
            if u == (12 if gate else 4):
                ada["br"] = load_rows([io["b_ada"][l, 2 * j + i] for i in range(4 if gate else 2)], br_sem, ada["bank"])
            if u == (15 if gate else 7):
                ada["bank"] = [tt(dve, ROWS[:, :], ps[:, 7, :], BR[:, :], ALU.add, last, ada["br"], ada["rows"])]
                ada["rows"] = None
                if gate:
                    gate_rows(l, m)
                else:
                    launch("ada", ada_cols(l, j, ada["bank"]), front=True)

        def gate_rows(l, m):
            t = ada["bank"]
            if l > 1:
                post = load_rows([bass.AP(tensor=io["rows"].tensor, offset=io["rows"][l - 1, i].offset,
                                          ap=[[0, 2], [1, 512]]) for i in range(4)], br_sem, t)
                t = ada["bank"] = [tt(dve, ROWS[:, :], ROWS[:, :], BR[:, :], ALU.mult, post, t)]
            for i in range(4):
                mod_ready[l, 4] = load(sp, gates[l, i, 0:m], ROWS[32 * i:32 * i + m, :], gates_sem, t)
            ada["rows"] = [mod_ready[l, 4]]
            ada["bank"] = [fill(dve, BR[64:128, :], 0.0, t)]

        def spread(dst, row, s, *after):
            return load(sp, dst, bass.AP(tensor=row.tensor, offset=row.offset, ap=[[0, 128], [1, 512]]), s, *after)

        def ada_cols(l, j, rows):
            yield rows
            b, free = side.take()
            for i in range(4):
                t = mm(ps[:, b, 4 * i:4 * i + 4], ROWS[:, 128 * i:128 * (i + 1)], K("sel"), True, True,
                       rows if i == 0 else None, free if i == 0 else None)
            ada["rows"] = [t]
            M, old = MOD[l % 2], mod_read[l % 2]
            v = ps[:, b, 0:16].rearrange("p (i c) -> p i c", i=4)
            nc_ = 1 if l < 2 else 2
            g = P("norm_g" if l < 2 else "pre", 16 * (l % 2) + 4 * j, 16 * (l % 2) + 4 * j + 4)
            cp(dve, M[:, 0, 4 * j:4 * j + 4, 0:nc_], v[:, :, 0:nc_], t, old)
            for c in range(nc_):
                t = stt(dve, M[:, 1, 4 * j:4 * j + 4, c], v[:, :, 2 + c], 1.0, g, ALU.add, ALU.mult)
            side.put(b, t)
            mod_ready[l, j] = t

        def chunk_a(stat, tiles, nk, need, evacs, hooks={}):
            banks = [[main.take() for _ in tiles] for _ in evacs]
            for u in range(nk // 4):
                for c, evac in enumerate(evacs):
                    for h in (2 * u, 2 * u + 1):
                        w, w_tok, slot = next_half()
                        last = []
                        for kt in (2 * h, 2 * h + 1):
                            for n, t in enumerate(tiles):
                                b, free = banks[c][n]
                                o = 512 * (kt % 2)
                                last.append(mm3(ps[:, b, :], stat(kt, t), [p[:, o:o + 512] for p in w], kt == 0,
                                                kt == nk - 1, w_tok, need(kt), free if kt == 0 else None))
                        give_back(slot, last[-1])
                        if (c, h) in hooks:
                            hooks[c, h](last[-1])
                        if h == nk // 2 - 1:
                            for n, t in enumerate(tiles):
                                main.put(banks[c][n][0], evac(n, ps[:, banks[c][n][0], :], last[n - len(tiles)]))
                        pump()

        def early_chunks(stat, need, evacs):
            banks = {}
            for q in range(4):
                for c, (held, evac) in enumerate(evacs):
                    if q == 0 or not held:
                        banks[c] = [main.take() for _ in range(2)]
                    for h in (2 * q, 2 * q + 1):
                        w, w_tok, slot = next_half()
                        last = []
                        for kt in (2 * h, 2 * h + 1):
                            for i in range(2):
                                b, free = banks[c][i]
                                o = 512 * (kt % 2)
                                first = kt == (0 if held else 4 * q)
                                last.append(mm3(ps[:, b, :], stat(kt, i), [p[:, o:o + 512] for p in w], first,
                                                kt == (15 if held else 4 * q + 3), w_tok, need(kt),
                                                free if first else None))
                        give_back(slot, last[-1])
                        if h % 2 and (q == 3 or not held):
                            for i in range(2):
                                b = banks[c][i][0]
                                main.put(b, evac(q, i, ps[:, b, :], last[2 + i]))
                        pump()

        def b_tile(rhs, shape, need, evac):
            b, free = main.take()
            for part in range(2):
                w, w_tok, slot = next_half()
                for j in range(8):
                    kt = 8 * part + j
                    last = mm3(shape(b), [p[:, 128 * j:128 * (j + 1)] for p in w], rhs(kt), kt == 0, kt == 15,
                               w_tok, need(kt), free if kt == 0 else None)
                give_back(slot, last)
                if part == 0:
                    pump()
            main.put(b, evac(shape(b), last))
            pump()

        def b_half(jobs):
            w, w_tok, slot = next_half()
            todo = []
            for m, (rhs, shape, need, evac) in enumerate(jobs):
                b, free = main.take()
                for kt in range(4):
                    c = 128 * (4 * m + kt)
                    last = mm3(shape(b), [p[:, c:c + 128] for p in w], rhs(kt), kt == 0, kt == 3,
                               w_tok, need(kt), free if kt == 0 else None)
                todo.append((b, evac, shape(b), last))
            give_back(slot, last)
            for b, evac, o, t in todo:
                main.put(b, evac(o, t))

        def sums(src, i, junk, *after):
            return fn(ACT.Square, junk, src, *after, accum_out=SS[:, i[0], i[1]:i[1] + 1])

        def inv_rms(tiles, parts, n, col, *after):
            k = len(tiles)
            t0, o = tiles[0], ST[:, col:col + k]
            if parts > 1:
                t = dve.do(lambda e: e.tensor_reduce(o, SS[:, t0:t0 + k, 0:parts], AX.X, ALU.add), after)
            else:
                t = cp(dve, o, SS[:, t0:t0 + k, 0], after)
            t = fn(ACT.Sqrt, o, o, t, bias=K("eps"), scale=1.0 / n)
            return recip(o, o, t)

        def inv_rms_steps(tiles, col, after):
            k, t0 = len(tiles), tiles[0]
            o = ST[:, col:col + k]
            yield after
            t = dve.do(lambda e: e.tensor_reduce(o, SS[:, t0:t0 + k, 0:4], AX.X, ALU.add), list(flat([after])))
            yield t
            t = fn(ACT.Sqrt, o, o, t, bias=K("eps"), scale=1.0 / D)
            yield t
            return recip(o, o, t)

        def feature_major(src, dst, mul, add, when, got):
            for k in range(0, NKT, 2):
                while when(k) is None:
                    yield 1
                yield when(k)
                b, free = side.take()
                for j in range(2):
                    for i in range(2):
                        c = 128 * (k + j)
                        t = tr(ps[:, b, 256 * j + 128 * i:256 * j + 128 * (i + 1)], src(i)[:, c:c + 128], when(k), free)
                n, nfree = og.take()
                for j in range(2):
                    e = fn(ACT.Identity, OG[n][:, j, :], ps[:, b, 256 * j:256 * (j + 1)], t, nfree,
                           scale=mul(k + j), bias=add(k + j))
                side.put(b, e)
                h, l = dst(k)
                t = cp(dve, h, OG[n][:, :, :], e)
                t = tt(dve, l, OG[n][:, :, :], h, ALU.subtract, t)
                og.put(n, t)
                got(k, t)
                got(k + 1, t)

        X = XR["X"]
        start_sem = sem("start")
        c_lo, c_hi = PARAM_COLS["c"]
        c_tok = load(sp, PR[:, c_lo:c_hi], io["params"][:, c_lo:c_hi], sem("c"))
        more_loads()
        cs_ready = fn(ACT.Silu, CS[:, :, :], P("c").rearrange("p (k c) -> p k c", k=16), c_tok)
        x_sem = sem("x")
        for t2 in range(2):
            x_tok = load(act, X[:, t2, :], io["x_in"][128 * t2:128 * (t2 + 1), :], x_sem)
        load(act, PR[:, 0:c_lo], io["params"][:, 0:c_lo], start_sem)
        early, table_sem, tables = CONST_COLS["cc"][0], sem("table"), []
        params = load(act, KC[:, 0:early], io["const"][:, 0:early], start_sem)
        t0 = fill(dve, ps[:, 7, :], 0.0)
        fill(dve, BR[:, :], 0.0)
        for i in range(4):
            t = fill(dve, E[i][:, :], 0.0)
        ada["bank"] = [t0, t]

        x = P("logit")
        a_, e_, s_, s2, p_, m_ = (LG[:, i, :] for i in range(6))
        t = ts(dve, a_, x, -1.0, None, ALU.mult, None, params)
        t = tt(dve, a_, a_, x, ALU.max, t)
        te = fn(ACT.Exp, e_, a_, t, scale=-1.0)
        t = ts(dve, s_, e_, 2.0, None, ALU.add, None, te)
        t = recip(s_, s_, t)
        t = tt(dve, s_, s_, e_, ALU.mult, t)
        t = tt(dve, s2, s_, s_, ALU.mult, t)
        t = ts(dve, p_, s2, 1.0 / 19, None, ALU.mult, None, t)
        for k in range(8, 0, -1):
            t = stt(dve, p_, p_, 1.0 / (2 * k + 1), s2, ALU.add, ALU.mult, t)
        t = stt(dve, p_, p_, 1.0, s_, ALU.add, ALU.mult, t)
        tm = ts(dve, m_, x, -1.0, 0.0, ALU.mult, ALU.max)
        t = stt(dve, p_, p_, 2.0, m_, ALU.mult, ALU.add, t, tm)
        lg_ready = ts(dve, LG[:, 0, :], p_, -1.0, None, ALU.mult, None, t)

        def lgam(l, back, h):
            c = 16 * l + 8 * back + h
            return LG[:, 0, c:c + 1]

        YB, CT = W["YB"], W["CT"]
        W1, G, qT, kT, dec, nb, dft = (W[n] for n in ("W1", "G", "qT", "kT", "dec", "nb", "dft"))
        uT, PQ, acc, FX = HU["uT"], HU["PQ"], HU["acc"], HU["FX"]
        TQ, TK = three(W1[:, 0, 0:1024], 2), three(W1[:, 0, 1024:2048], 2)
        V0, V1 = three(W1[:, 1, 0:1024], 2), three(W1[:, 1, 1024:2048], 2)
        G0, G1 = G[:, 0], G[:, 1]
        dec_slots, nb_slots = Slots([0, 1]), Slots([0, 1])
        gb_sems, fg_sems = [sem("gb0"), sem("gb1")], [sem("fg0"), sem("fg1")]
        dft_sem, nb_sems = sem("dft"), [sem("nb0"), sem("nb1")]
        places = {n: [] for n in ("TQ", "TK", "V0", "V1", "G0", "G1", "qk", "uT", "PQ", "acc", "FX", "dft",
                                  "H0", "H1", "rn0", "rn1", "rn2", "X")}

        def own(*names):
            toks = [places[n] for n in names]
            assert None not in toks, names
            for n in names:
                places[n] = None
            return toks

        def give(name, *toks):
            places[name] = list(flat(toks))

        def own_when(*names):
            pump_until(lambda: not (any(places[n] is None for n in names)))
            return own(*names)

        def keep(dst, name, f=ACT.Copy):
            done, free = [], []

            def ev(i, o, t):
                if i == 0:
                    free[:] = own_when(name)
                done.append(fn(f, dst[:, i, :], o, t, free))
                return done[-1]
            return ev, done

        def rotate(dst, name):
            done, free = [], []

            def ev(i, o, t):
                if i == 0:
                    free[:] = own_when(name)
                pump_until(lambda: scratch.free)
                s, sfree = scratch.take()
                o4 = o.rearrange("p (h x d) -> p h x d", h=8, x=2)
                s4 = E[s][:, 0:512].rearrange("p (h x d) -> p h x d", h=8, x=2)
                d4 = dst[:, i, :].rearrange("p (h x d) -> p h x d", h=8, x=2)
                a = tt(dve, d4, o4, bcast(K("cosr", 32 * i), (0, 8), (0, 2), (1, 32)), ALU.mult, t, free,
                       tables)
                for x in range(2):
                    sin = bcast(K("sinr", 64 * i + 32 * x), (0, 8), (1, 32))
                    e = tt(dve, s4[:, :, x, :], o4[:, :, 1 - x, :], sin, ALU.mult, sfree)
                r = tt(dve, dst[:, i, :], dst[:, i, :], E[s][:, 0:512], ALU.add, a, e)
                scratch.put(s, r)
                done.append(r)
                return e
            return ev, done

        def pair_transposed(q_tok, k_tok):
            while places["qk"] is None:
                yield 1
            free, n, got = own("qk"), 0, []
            for src, dst, tok, name in ((TQ, qT, q_tok, "TQ"), (TK, kT, k_tok, "TK")):
                for i in range(2):
                    b, bfree = side.take()
                    for pr in range(4):
                        tp = tr(ps[:, b, 128 * pr:128 * (pr + 1)], src[:, i, 128 * pr:128 * (pr + 1)], tok, bfree)
                    got.append(cp((act, dve)[n % 2], dst[:, :, 128 * i:128 * (i + 1)], three(ps[:, b, :], 4), tp, free))
                    n += 1
                    side.put(b, got[-1])
                    yield (tok if i == 0 else k_tok) if dst is qT else got
                give(name, tp)
            return got

        def gate_transposed(gate, rn, *after):
            yield from room(1)
            s, free = scratch.take()
            v = three(E[s][:, 0:256], 2)
            for i in range(2):
                t = tt(dve, three(v[:, i], 2), three(gate[:, i], 2), bcast(rn(i), (1, 2), (0, 64)), ALU.mult, after, free)
            yield t
            b, free = side.take()
            for i in range(2):
                tp = tr(ps[:, b, 128 * i:128 * (i + 1)], v[:, i], t, free)
            scratch.put(s, tp)
            return b, tp, t

        def token_to_parts(src, src_tok, free, s_out, k0, o_tok):
            yield src_tok
            for b2 in range(2):
                b, bfree = side.take()
                for j in range(2):
                    for i in range(2):
                        c = 128 * (2 * b2 + j)
                        tp = tr(ps[:, b, 256 * j + 128 * i:256 * j + 128 * (i + 1)], src[:, i, c:c + 128],
                                src_tok, bfree)
                k = k0 + 2 * b2
                h, l = (p[:, s_out, k:k + 2, :] for p in (Hh, Hl))
                t = split(h, l, three(ps[:, b, :], 2), tp, free)
                side.put(b, t)
                o_tok[k] = o_tok[k + 1] = t
                yield src_tok
            return tp

        def layer1(l, x_ready):
            M = MOD[l % 2]
            hT, oT = 0, 1
            h_tok, o_tok, made = {}, {}, {}
            t = inv_rms([0, 1], 4, D, 0, x_ready)
            free = own("TQ", "TK", "V0", "V1")
            xn = [ts(dve, W1[:, i, :], X[:, i, :], ST[:, i:i + 1], None, ALU.mult, None, t, free) for i in range(2)]
            hfree = own("H0")
            launch("prep", feature_major(
                lambda i: W1[:, i, :], lambda k: (Hh[:, hT, k:k + 2, :], Hl[:, hT, k:k + 2, :]),
                lambda k: M[:, 1, k, 0:1], lambda k: M[:, 0, k, 0:1],
                lambda k: [xn, hfree, mod_ready[l, k // 4]] if (l, k // 4) in mod_ready else None,
                h_tok.__setitem__), front=True)

            def need_h(k):
                return prepared(h_tok, k, lambda j: (l, j // 4) in mod_ready)

            def stat(s):
                return lambda k, i: [p[:, s, k, 128 * i:128 * (i + 1)] for p in (Hh, Hl)]

            def piece(ev, hooks={}):
                chunk_a(stat(hT), [0, 1], NKT, need_h, [ev], hooks)

            def cw(ct, k):
                return P("conv", 136 * l + 34 * ct + k, 136 * l + 34 * ct + k + 1)

            for n in ("TQ", "V0", "V1"):
                give(n, xn)
            ev_a, a_tok = keep(TQ, "TQ")
            u_tok = []

            def ev_b(i, o, t):
                t = fn(ACT.Sigmoid, TK[:, i, :], o, t)
                u_tok.append(tt(dve, TQ[:, i, :], TQ[:, i, :], TK[:, i, :], ALU.mult, t, a_tok[i]))
                if i == 1:
                    launch("conv", conv(), last=True)
                return t

            def conv():
                yield u_tok
                free_u, free_a = own("uT", "PQ"), own("acc")
                t = fill(pool, uT[:, :, 0:15], 0.0, free_u)
                t = [t, fill(pool, uT[:, :, 271:286], 0.0)]
                for i in range(2):
                    b, free = side.take()
                    for ct in range(4):
                        tp = tr(ps[:, b, 128 * ct:128 * (ct + 1)], TQ[:, i, 128 * ct:128 * (ct + 1)], u_tok, free)
                    e = cp(dve, uT[:, :, 15 + 128 * i:15 + 128 * (i + 1)], three(ps[:, b, :], 4), tp, free_u)
                    side.put(b, e)
                    t.append(e)
                give("TQ", tp)
                give("TK", u_tok)
                last = [None] * 4
                for k in range(31):
                    for ct in range(4):
                        u, a = uT[:, ct, k:k + 256], acc[:, ct, :]
                        if k == 0:
                            last[ct] = ts(dve, a, u, cw(ct, 0), cw(ct, 31), ALU.mult, ALU.add, t, free_a)
                        else:
                            last[ct] = stt(dve, a, u, cw(ct, k), a, ALU.mult, ALU.add, last[ct])
                    yield "dve" if k < 30 else last
                yn = bcast(uT[:, 0, :], (512, 2), (1, 512))
                y_tok = []
                for i in range(2):
                    b, free = side.take()
                    for ct in range(4):
                        tp = tr(ps[:, b, 128 * ct:128 * (ct + 1)], acc[:, ct, 128 * i:128 * (i + 1)], last, free)
                    S, A, V, o = BN[:, i, 0:6], BN[:, i, 6:8], BN[:, i, 8:9], ps[:, b, :]
                    t = dve.do(lambda e, S=S, o=o: e.bn_stats(S, o), [tp])
                    t = dve.do(lambda e, S=S, A=A: e.bn_aggr(A, S), [t])
                    t = fn(ACT.Sqrt, V, BN[:, i, 7:8], t, bias=K("eps"))
                    t = recip(V, V, t)
                    t = ts(dve, yn[:, i, :], o, BN[:, i, 6:7], V, ALU.subtract, ALU.mult, t, last)
                    side.put(b, t)
                    y_tok.append(t)
                yield y_tok
                for b2 in range(2):
                    b, free = side.take()
                    for j in range(2):
                        c = 128 * (2 * b2 + j)
                        for i in range(2):
                            tp = tr(ps[:, b, 256 * j + 128 * i:256 * j + 128 * (i + 1)], yn[:, i, c:c + 128], y_tok, free)
                    for j in range(2):
                        ct = 2 * b2 + j
                        t = fn(ACT.Silu, acc[:, ct, :], ps[:, b, 256 * j:256 * (j + 1)], tp,
                               bias=cw(ct, 33), scale=cw(ct, 32))
                    side.put(b, t)
                    yield y_tok
                give("uT", tp)
                give("PQ", tp)
                made["s"] = t

            ev_v, nv = keep(V0, "V0")
            rv, fx, ng = [], [], []
            if l == 0:
                def summed(store, dst, done, name=None, gate=False):
                    part = {}

                    def ev(q, i, o, t):
                        if q == 0:
                            t = cp(act, store[:, i, :], o, t)
                        elif q < 3:
                            t = tt(dve, store[:, i, :], o, store[:, i, :], ALU.add, t, part[i])
                        else:
                            if i == 0:
                                part["own"] = own(name) if name else []
                            t = tt(dve, dst[:, i, :], o, store[:, i, :], ALU.add, t, part[i], part["own"])
                            done.append(fn(ACT.Silu, dst[:, i, :], dst[:, i, :], t) if gate else t)
                        part[i] = t
                        return t
                    return False, ev

                S0, S1 = HU["S0"], HU["S1"]

                def other_tables():
                    while not h_tok:
                        yield 1
                    tables.append(load(sp, KC[:, early:], io["const"][:, early:], table_sem))
                launch("tables", other_tables())
                lend(2)
                early_chunks(stat(hT), need_h, [
                    summed(S0[:, 0], TQ, a_tok, "TQ"), (True, lambda q, i, o, t: ev_b(i, o, t)),
                    summed(S0[:, 1], V0, nv, "V0"), summed(S1[:, 0], V1, rv, "V1"),
                    summed(FX, FX, fx, "FX"), summed(S1[:, 1], G0, ng, "G0", True)])
                lend(-2)
                give("H1", dve.last)
            else:
                piece(ev_a)
                piece(ev_b)
                piece(ev_v)

            ev, nq = keep(TQ, "TQ")
            piece(ev)
            ev, nk = keep(TK, "TK")
            piece(ev)
            if l == 1:
                ev, ng = keep(G0, "G0", ACT.Silu)
                piece(ev)

            def neighbours():
                qk = yield from pair_transposed(nq, nk)
                hfree = places["H1"]
                biases, mx_read = {}, {0: [], 1: []}

                def bias(h):
                    d, free = nb_slots.take()
                    t = load(sp, nb[:, d, :], io["na_bias"][l, h], nb_sems[d], free)
                    v = nb[:, d, :].rearrange("p (m c) -> p m c", m=6)
                    biases[h] = (d, tt(pool, v, v, bcast(K("mask"), (0, 6), (1, 64)), ALU.add, t, tables))

                bias(0)
                bias(1)
                for pr in range(4):
                    rn = f"rn{1 + pr % 2}"
                    rfree, c0, exps, held = own(rn), 8 * (pr % 2), [], []
                    yield from room(2)
                    banks = [side.take(), side.take()]
                    for i in range(2):
                        for hh, (b, free) in enumerate(banks):
                            o = 64 * hh
                            t = mm(ps[:, b, 256 * (1 - i):256 * (2 - i)], qT[o:o + 64, pr, 128 * i:128 * (i + 1)],
                                   kT[o:o + 64, pr, :], True, True, qk, free)
                    for hh, (b, _) in enumerate(banks):
                        h = 2 * pr + hh
                        s, sfree = scratch.take()
                        d, d_tok = biases.pop(h)
                        pm, mx = three(E[s][:, 0:512], 2), MX[:, hh, 0:2]
                        m = stt(dve, pm, three(ps[:, b, :], 2), 0.125, bcast(nb[:, d, :], (128, 2), (1, 256)),
                                ALU.mult, ALU.add, t, d_tok, sfree)
                        side.put(b, m)
                        nb_slots.put(d, m)
                        if h < 6:
                            bias(h + 2)
                        m = dve.do(lambda e, mx=mx, pm=pm: e.tensor_reduce(mx, pm, AX.X, ALU.max, negate=True),
                                   [m] + mx_read[hh], 0.6)
                        for x in range(2):
                            c = c0 + 2 * (1 - x) + hh
                            m2 = fn(ACT.Exp, pm[:, x, :], pm[:, x, :], m, rfree, bias=mx[:, x:x + 1],
                                    accum_out=RN[:, 1, c:c + 1])
                        mx_read[hh] = [m2]
                        exps.append(m2)
                        held.append((s, pm, m2))
                    yield exps
                    parts = []
                    for hh, (s, pm, m2) in enumerate(held):
                        b, free = side.take()
                        for kt in range(2):
                            for i in range(2):
                                tp = tr(ps[:, b, 256 * kt + 128 * i:256 * kt + 128 * (i + 1)],
                                        pm[:, 1 - i, 128 * kt:128 * (kt + 1)], m2, free)
                        scratch.put(s, tp)
                        s, sfree = scratch.take()
                        t = cp((act, dve)[hh], E[s][:, 0:512], ps[:, b, :], tp, sfree)
                        side.put(b, t)
                        parts.append((s, t))
                    yield [t for _, t in parts]
                    ob, obfree = side.take()
                    for kt in range(2):
                        for hh, (s, t) in enumerate(parts):
                            o, h = 64 * hh, 2 * pr + hh
                            tp = mm(ps[o:o + 64, ob, 0:256], V0[:, kt, 64 * h:64 * (h + 1)],
                                    E[s][:, 256 * kt:256 * (kt + 1)], kt == 0, kt == 1, t, nv, obfree)
                    for s, _ in parts:
                        scratch.put(s, tp)
                    o_done = tp
                    r = RN[:, 1, c0:c0 + 4]
                    t = recip(r, r, exps)
                    b, tp, g = yield from gate_transposed(
                        G0[:, :, 128 * pr:128 * (pr + 1)], lambda i: RN[:, 1, c0 + 2 * i:c0 + 2 * i + 2], t, ng)
                    give(rn, g)
                    n, free = og.take()
                    t = cp(act, OG[n][:, 1, :], ps[:, b, 0:256], tp, free)
                    side.put(b, t)
                    t = tt(dve, OG[n][:, 0, :], ps[:, ob, 0:256], OG[n][:, 1, :], ALU.mult, t, o_done)
                    side.put(ob, t)
                    t = split(Hh[:, oT, pr, :], Hl[:, oT, pr, :], OG[n][:, 0, :], t, hfree)
                    og.put(n, t)
                    o_tok[pr] = t
                    yield t
                give("qk", pe.last)
                give("V0", o_done)
                give("G0", g)

            launch("na", neighbours())

            if l == 1:
                ev, rv = keep(V1, "V1")
                piece(ev)
            ev, rq = rotate(TQ, "TQ")
            piece(ev)
            ev, rk = rotate(TK, "TK")
            piece(ev)
            ev, rg = keep(G1, "G1", ACT.Silu)
            piece(ev)

            def retention():
                qk = yield from pair_transposed(rq, rk)
                ofree, rfree = own("TK", "rn0")
                oraw = bcast(TK[:, 0, :], (256, 4), (1, 256))
                oraw_tok, ss_tok, decs = [], [], {}

                def decay(h):
                    d, free = dec_slots.take()
                    c = dec[:, d, :]
                    t = ts(pool, c, K("dist_b"), lgam(l, 1, h), None, ALU.mult, None, lg_ready, free, tables)
                    t = stt(dve, c, K("dist_f"), lgam(l, 0, h), c, ALU.mult, ALU.add, t)
                    decs[h] = (d, fn(ACT.Exp, c, c, t))

                decay(0)
                decay(1)
                for pr in range(4):
                    yield from room(2)
                    banks, parts = [side.take(), side.take()], []
                    for jt in range(2):
                        for hh, (b, free) in enumerate(banks):
                            o = 64 * hh
                            tq = mm(ps[:, b, 256 * (1 - jt):256 * (2 - jt)], kT[o:o + 64, pr, 128 * jt:128 * (jt + 1)],
                                    qT[o:o + 64, pr, :], True, True, qk, free)
                    for hh, (b, _) in enumerate(banks):
                        h = 2 * pr + hh
                        s, sfree = scratch.take()
                        d, d_tok = decs.pop(h)
                        t = stt(dve, three(E[s][:, 0:512], 2), three(ps[:, b, :], 2), 0.125,
                                bcast(dec[:, d, :], (128, 2), (1, 256)), ALU.mult, ALU.mult, tq, d_tok, sfree)
                        side.put(b, t)
                        dec_slots.put(d, t)
                        if h < 6:
                            decay(h + 2)
                        parts.append((s, t))
                    yield [t for _, t in parts]
                    ob, obfree = side.take()
                    for jt in range(2):
                        for hh, (s, t) in enumerate(parts):
                            o, h = 64 * hh, 2 * pr + hh
                            tp = mm(ps[o:o + 64, ob, 0:256], V1[:, jt, 64 * h:64 * (h + 1)],
                                    E[s][:, 256 * (1 - jt):256 * (2 - jt)], jt == 0, jt == 1, t, rv, obfree)
                    for s, _ in parts:
                        scratch.put(s, tp)
                    oraw_tok.append(cp(act, oraw[:, pr, :], ps[:, ob, 0:256], tp, ofree))
                    s, sfree = scratch.take()
                    t = fn(ACT.Square, E[s][:, 0:256], ps[:, ob, 0:256], sfree)
                    side.put(ob, t)
                    yield t
                    b, free = side.take()
                    for i in range(2):
                        tp = mm(ps[:, b, 2 * i:2 * i + 2], E[s][:, 128 * i:128 * (i + 1)], K("hsel"), True, True, t, free,
                                tables)
                    scratch.put(s, tp)
                    ss_tok.append(cp(dve, bcast(RN[:, 0, 2 * pr:2 * pr + 1], (8, 2), (1, 2)), three(ps[:, b, 0:4], 2),
                                     tp, rfree))
                    side.put(b, ss_tok[-1])
                give("qk", tp)
                give("V1", tp)
                t = fn(ACT.Sqrt, RN[:, 0, :], RN[:, 0, :], ss_tok, bias=K("eps"), scale=1.0 / 64)
                rn_tok = recip(RN[:, 0, :], RN[:, 0, :], t)
                ofree = places["H1"]
                for pr in range(4):
                    b, tp, g = yield from gate_transposed(
                        G1[:, :, 128 * pr:128 * (pr + 1)], lambda i: RN[:, 0, 8 * i + 2 * pr:8 * i + 2 * pr + 2],
                        rn_tok, rg)
                    n, free = og.take()
                    t = tt(dve, OG[n][:, 0, :], ps[:, b, 0:256], oraw[:, pr, :], ALU.mult, tp, oraw_tok, free)
                    side.put(b, t)
                    fx = t
                    t = split(Hh[:, oT, 4 + pr, :], Hl[:, oT, 4 + pr, :], OG[n][:, 0, :], t, ofree)
                    og.put(n, t)
                    o_tok[4 + pr] = t
                give("G1", g)
                give("TK", fx)
                give("rn0", g)

            launch("ret", retention())

            dft_tok = load(sp, dft[:, :, :], three(io["dft"], 2), dft_sem, places["dft"])
            if l == 1:
                ev, fx = keep(FX, "FX")
                piece(ev)

            def fourier():
                while places["PQ"] is None:
                    yield 1
                free, pq = own("PQ"), []
                for g2 in range(2):
                    b, bfree = side.take()
                    for g in (2 * g2, 2 * g2 + 1):
                        for i in range(2):
                            tp = mm(ps[:, b, 256 * (g % 2):256 * (g % 2 + 1)], FX[:, i, 128 * g:128 * (g + 1)],
                                    dft[:, i, :], i == 0, i == 1, fx, dft_tok, bfree)
                    pq.append(cp((act, dve)[g2], PQ[:, 2 * g2:2 * g2 + 2, 0:256], three(ps[:, b, :], 2), tp, free))
                    side.put(b, pq[-1])
                    yield pq[-1] if g2 == 1 else fx
                give("dft", tp)
                yf = bcast(FX[:, 0, :], (256, 4), (1, 256))
                for g2 in range(2):
                    b, bfree = side.take()
                    for g in (2 * g2, 2 * g2 + 1):
                        o = 256 * (g % 2)
                        mm(ps[:, b, o:o + 129], K("cc", 0, 128), PQ[:, g, 0:129], True, True, pq, bfree, tables)
                        tq = mm(ps[:, b, o + 129:o + 256], K("cc", 128, 256), PQ[:, g, 129:256], True, True)
                    y, v = yf[:, 2 * g2:2 * g2 + 2, :], three(ps[:, b, :], 2)
                    down = bass.AP(tensor=y.tensor, offset=y.offset + 255, ap=[list(y.ap[0]), [256, 2], [-1, 127]])
                    t = cp(act, y[:, :, 0:129], v[:, :, 0:129], tq, tp)
                    t = tt(dve, down, y[:, :, 1:128], v[:, :, 129:256], ALU.subtract, t)
                    t = tt(dve, y[:, :, 1:128], y[:, :, 1:128], v[:, :, 129:256], ALU.add, t)
                    side.put(b, t)
                    made["f", g2] = t
                    yield pq
                made["pq"] = tq
                made["y"] = t

            launch("fft", fourier())
            ev, cg = keep(G0, "G0", ACT.Silu)
            piece(ev)
            ev, fg = keep(V0, "V0", ACT.Silu)

            def parts_of(src, k0, name):
                def hook(tok):
                    pump_until(lambda: not (name not in made))
                    for j in (0, 2):
                        made[name, "parts", j] = split(Hh[:, hT, k0 + j:k0 + j + 2, :], Hl[:, hT, k0 + j:k0 + j + 2, :],
                                                       src[:, j:j + 2, :], made[name], tok)
                return hook

            yf = bcast(FX[:, 0, :], (256, 4), (1, 256))
            piece(ev, {(0, 1): parts_of(acc, 0, "s"), (0, 3): parts_of(yf, 4, "y")})

            def gated_chunk(k0, name, dst, gate, gate_tok, free):
                o_done = []

                def ev(i, o, t):
                    o_done.append(tt(dve, dst[:, i, :], o, gate[:, i, :], ALU.mult, t, gate_tok, free))
                    return o_done[-1]
                chunk_a(lambda k, i: [p[:, hT, k0 + k, 128 * i:128 * (i + 1)] for p in (Hh, Hl)], [0, 1], 4,
                        lambda k: made[name, "parts", k // 2 * 2], [ev])
                return o_done

            o_cv = gated_chunk(0, "s", TQ, G0, cg, own_when("TQ"))
            give("G0", o_cv)
            hfree = places["H1"]

            def cv_out():
                tp = yield from token_to_parts(TQ, o_cv, [hfree, made["pq"]], oT, 8, o_tok)
                give("TQ", tp)

            launch("cvo", cv_out())
            o_ff = gated_chunk(4, "y", TK, V0, fg, own_when("TK"))
            give("V0", o_ff)
            give("H0", pe.last)

            def ff_out():
                tp = yield from token_to_parts(TK, o_ff, hfree, oT, 12, o_tok)
                give("TK", tp)
                made["ffo"] = tp

            launch("ffo", ff_out())
            if l == 1:
                launch("ctx", context_prep())

            def need_o(k):
                pump_until(lambda: not (k not in o_tok))
                return o_tok[k]

            GBs = [GB1, W["GB0"]]
            gb_read, ct_free = {0: [dve.last], 1: places["dft"]}, [dve.last]
            fg_read = {0: [], 1: []}
            x_tok = []

            def out_chunk(c):
                gb, b, late = {}, c % 2, c == 3

                def hook(_):
                    gb["g"] = spread(GBs[b][:, :], gates[l, c, 0], gb_sems[b], gb_read[b], mod_ready[l, 4])
                    if l == 1:
                        gb["f"] = spread(CT[:, 512 * b:512 * (b + 1)], io["rows"][0, c], fg_sems[b], fg_read[b],
                                         ct_free)

                def ev(i, o, t):
                    pump_until(lambda: scratch.free)
                    s, free = scratch.take()
                    xs = X[:, i, 512 * c:512 * (c + 1)]
                    t = tt(dve, E[s][:, 0:512], o, GBs[b][:, :], ALU.mult, t, gb["g"], free)
                    gb_read[b] = [t]
                    a = tt(dve if late else pool, xs, xs, E[s][:, 0:512], ALU.add, t)
                    made_x, a_f = a, None
                    if l == 1:
                        xf = YB[:, 4096 + 2048 * i + 512 * c:4096 + 2048 * i + 512 * (c + 1)]
                        a = tt(dve if late else pool, xf, xs, CT[:, 512 * b:512 * (b + 1)], ALU.mult, a, gb["f"], t)
                        fg_read[b], a_f = [a], a

                    def squares():
                        yield [made_x, a_f]
                        x_tok.append(sums(xs, (i, c), E[s][:, 0:512], made_x, a_f))
                        if l == 1:
                            x_tok.append(sums(xf, (4 + i, c), E[s][:, 0:512], a_f, x_tok[-1]))
                        scratch.put(s, x_tok[-1])
                    launch("squares", squares(), start=True)
                    if late:
                        finish("squares")
                    return t
                return ev, hook

            (ev0, hook0), (ev1, hook1) = out_chunk(0), out_chunk(1)
            chunk_a(stat(oT), [0, 1], NKT, need_o, [ev0, ev1], {(0, 4): hook0, (1, 4): hook1})
            for c in (2, 3):
                ev, hook = out_chunk(c)
                chunk_a(stat(oT), [0, 1], NKT, need_o, [ev], {(0, 2): hook})
            give("dft", gb_read[1])
            mod_read[l % 2] = [dve.last, pool.last]
            for n in ("conv", "ret", "na", "fft", "cvo", "ffo"):
                assert all(s["name"] != n for s in sides), n
            give("H1", pe.last)
            for n in ("uT", "acc", "FX", "PQ"):
                give(n, pe.last)
            return x_tok

        h2 = {0: {}, 1: {}}
        ctx_sem, spill_sem, reload_sem, ct_sem = sem("ctx"), sem("spill"), sem("reload"), sem("ct")

        def context_prep():
            names = ("TQ", "TK", "V0", "V1")
            while any(places[n] is None for n in names) or places["H0"] is None or (2, 0) not in mod_ready:
                yield 1
            free, hfree = own(*names), own("H0")
            for i in range(2):
                t = load(sp, W1[:, i, :], io["ctx_in"][128 * i:128 * (i + 1), :], ctx_sem, free)
            yield t
            sq = []
            for i in range(2):
                for c in range(4):
                    n, nfree = scratch.take()
                    sq.append(sums(W1[:, i, 512 * c:512 * (c + 1)], (2 + i, c), E[n][:, 0:512], t, nfree))
                    scratch.put(n, sq[-1])
                yield "dve"
            t = inv_rms([2, 3], 4, D, 2, sq)
            xn = [ts(dve, W1[:, i, :], W1[:, i, :], ST[:, 2 + i:3 + i], None, ALU.mult, None, t) for i in range(2)]
            yield xn
            M = MOD[0]
            yield from feature_major(
                lambda i: W1[:, i, :], lambda k: (Hh[:, 0, k:k + 2, :], Hl[:, 0, k:k + 2, :]),
                lambda k: M[:, 1, k, 1:2], lambda k: M[:, 0, k, 1:2],
                lambda k: [xn, hfree, mod_ready[2, k // 4]] if (2, k // 4) in mod_ready else None, h2[0].__setitem__)
            made = pe.last
            for n in names:
                give(n, made)

        def latent_prep(s, src, src_tok, l, k_after):
            M = MOD[l % 2]
            c = 1 - s
            return feature_major(
                src, lambda k: (Hh[:, s, k:k + 2, :], Hl[:, s, k:k + 2, :]),
                lambda k: M[:, 1, k, c:c + 1], lambda k: M[:, 0, k, c:c + 1],
                lambda k: [src_tok, k_after, mod_ready[l, k // 4]], h2[s].__setitem__)

        def layer2(x_tok):
            finish("ctx")
            r = inv_rms([0, 1], 4, D, 0, x_tok)
            S2 = ST[:, 4:6]
            t = dve.do(lambda e: e.tensor_reduce(S2, SS[:, 4:6, 0:4], AX.X, ALU.add), x_tok)
            t = tt(dve, S2, S2, ST[:, 0:2], ALU.mult, t, r)
            t = tt(dve, S2, S2, ST[:, 0:2], ALU.mult, t)
            t = fn(ACT.Sqrt, S2, S2, t, bias=K("eps"), scale=1.0 / D)
            t = recip(S2, S2, t)
            t = tt(dve, S2, S2, ST[:, 0:2], ALU.mult, t)
            xn = [ts(dve, YB[:, 2048 * i:2048 * (i + 1)], YB[:, 4096 + 2048 * i:6144 + 2048 * i], ST[:, 4 + i:5 + i],
                     None, ALU.mult, None, t, places["TQ"]) for i in range(2)]
            xs = [fn(ACT.Copy, X[:, i, :], YB[:, 4096 + 2048 * i:6144 + 2048 * i], r, scale=ST[:, i:i + 1])
                  for i in range(2)]
            for i in range(2):
                spill = load(act, out[128 * i:128 * (i + 1), :], X[:, i, :], spill_sem, xs[i])
            launch("prep", latent_prep(1, lambda i: YB[:, 2048 * i:2048 * (i + 1)], xn, 2, places["H1"]), front=True)

            def need_h(k):
                prepared(h2[1], k)
                return [h2[0][k], h2[1][k]]

            PH, PL = XR["PH"], XR["PL"]
            for _ in range(4):
                scratch.take()
            z = [fill(dve, E[i][:, :], 0.0, act.last, pe.last) for i in range(2)]
            U = [three(E[i][:, :], 2) for i in range(4)]
            u_free = [[z[0]], [z[1]]]
            pt, y_tok, yt_tok = {}, {}, {}
            grp_read = [xn, xs]
            Yk = YB[:, :].rearrange("p (k s n) -> p k s n", k=16, s=2)

            def pooled(g, i):
                w, slot = WINDOWS[g], i % 2

                def ev(o, t):
                    A, B, u = U[2], U[3], U[slot]
                    t = cp(act, u[:, :, 8:264], o, t, u_free[slot])
                    ev_tok = t
                    a, b = 8 - 7, 8 + 263
                    if w == 2:
                        a, b = 8, 264
                    t = tt(dve, A[:, :, a:b], u[:, :, a - 1:b - 1], u[:, :, a:b], ALU.add, t, scr_free)
                    cur, other, shift, width = A, B, 1, 2
                    while width < w:
                        width *= 2
                        shift = width // 4
                        a, b = (8, 264) if width == w else (a + shift, b - shift)
                        t = tt(dve, other[:, :, a:b], cur[:, :, a - shift:b - shift], cur[:, :, a + shift:b + shift],
                               ALU.add, t)
                        cur, other = other, cur
                    ed = bcast(cur[:, 0, 8:9], (272, 2), (248, 2), (1, 8))
                    t = tt(dve, ed, ed, bcast(K("edge", 16 * g), (0, 2), (8, 2), (1, 8)), ALU.mult, t)
                    n, nfree = og.take()
                    t = stt(dve, OG[n][:, :, :], cur[:, :, 8:264], 1.0 / w, u[:, :, 8:264], ALU.mult, ALU.subtract,
                            t, nfree)
                    u_free[slot] = [t]
                    scr_free[:] = [t]
                    t = split(three(PH[:, i, :], 2), three(PL[:, i, :], 2), OG[n][:, :, :], t, list(grp_read), spill)
                    og.put(n, t)
                    pt[i] = t
                    return ev_tok
                return ev

            scr_free = []

            def gate_ev(k):
                def ev(o, t):
                    t = fn(ACT.Silu, Yk[:, k], o, t, xn_read)
                    y_tok[k] = ts(pool, Yk[:, k], Yk[:, k], P("p_scale", k, k + 1), None, ALU.mult, None, t)
                    return t
                return ev

            def grp_ev(k):
                def ev(o, t):
                    yt_tok[k] = stt(dve, Yk[:, k], o, P("b_grp", k, k + 1), Yk[:, k], ALU.add, ALU.mult, t, y_tok[k])
                    return yt_tok[k]
                return ev

            def bank(b):
                return three(ps[:, b, :], 2)

            def rhs(k):
                return [p[:, :, k, :] for p in (Hh, Hl)]

            def first_tiles():
                got, banks = {}, [main.take(), main.take()]

                def work(c, part, s):
                    if (c, part) not in got:
                        got[c, part] = next_half()
                    w, w_tok, slot = got[c, part]
                    b, free = banks[c]
                    for j in range(8):
                        kt = 8 * part + j
                        h = prepared(h2[1], kt) if s else h2[0][kt]
                        t = mm3(ps[:, b, 256 * s:256 * (s + 1)], [p[:, 128 * j:128 * (j + 1)] for p in w],
                                [p[:, s, kt, :] for p in (Hh, Hl)], kt == 0, kt == 15, w_tok, h,
                                free if kt == 0 else None)
                    if s:
                        give_back(slot, t)
                    pump()
                    return t

                for c, part, s in ((0, 0, 0), (0, 1, 0), (1, 0, 0), (0, 0, 1), (1, 1, 0), (0, 1, 1), (1, 0, 1), (1, 1, 1)):
                    t = work(c, part, s)
                    if (part, s) == (1, 1):
                        main.put(banks[c][0], pooled(0, c)(bank(banks[c][0]), t))

            first_tiles()
            xn_read = [pe.last]
            for g in range(4):
                for i in range(2 if g == 0 else 0, 4):
                    b_tile(rhs, bank, need_h, pooled(g, i))
                for i in range(4):
                    b_tile(rhs, bank, need_h, gate_ev(4 * g + i))
                h_read = pe.last
                for half in range(2):
                    jobs = []
                    for i in (2 * half, 2 * half + 1):
                        jobs.append((lambda k: [three(PH[:, k, :], 2), three(PL[:, k, :], 2)], bank,
                                     lambda k: pt[k], grp_ev(4 * g + i)))
                    b_half(jobs)
                    if g == 3 and half == 0:
                        early = y_parts(range(12), yt_tok, h_read, Yk)
                    pump()
                grp_read[:] = [pe.last]
            rest = y_parts(range(12, 16), yt_tok, h_read, Yk)
            parts = {**early, **rest}
            for i in range(4):
                scratch.put(i, [dve.last, act.last])

            lend(2)
            Y = YB[:, :].rearrange("p (t n) -> p t n", t=4)
            M = MOD[0]
            tiles = [(1, 0), (1, 1), (0, 0), (0, 1)]
            for i in range(2):
                reload = load(sp, X[:, i, :], out[128 * i:128 * (i + 1), :], reload_sem, grp_read, spill)
            ct0 = load(sp, CT[:, :], io["ctx_in"][0:128, :], ct_sem, pe.last)
            GB2 = [W["GB0"], GB1]
            gb_read = {0: [pe.last], 1: [dve.last]}
            sq, yg = {}, {}
            def out_stat(k, t):
                return [p[:, t[0], k, 128 * t[1]:128 * (t[1] + 1)] for p in (Hh, Hl)]

            for c in range(4):
                gb = {}

                def make_gate(_, s, c=c, gb=gb):
                    gb[s] = spread(GB2[s][:, :], gates[2, c, 1 - s], gb_sems[1 - s], gb_read[s], mod_ready[2, 4])

                def ev(n, o, t, c=c, gb=gb, among=tiles):
                    s, i = among[n]
                    j = 2 * s + i
                    e, efree = scratch.take()
                    t = sums(o, (j, c), E[e][:, 0:512], t, efree)
                    scratch.put(e, t)
                    sq[j, c] = t
                    t = tt(dve, Y[:, j, 512 * c:512 * (c + 1)], o, GB2[s][:, :], ALU.mult, t, gb[s])
                    gb_read[s] = [t]
                    yg[j, c] = t
                    return t

                hooks = {(0, 3): lambda _: make_gate(_, 1), (0, 4): lambda _: make_gate(_, 0)}
                if c < 3:
                    chunk_a(out_stat, tiles, NKT, lambda k: parts[k], [ev], hooks)
                else:
                    chunk_a(out_stat, tiles[:2], NKT, lambda k: parts[k], [ev], hooks)
                    y_read, xs = pe.last, {}
            lend(-2)

            def latent_end():
                r = yield from inv_rms_steps([2, 3], 10, [sq[2 + i, c] for c in range(4) for i in range(2)])
                q = []
                for i in range(2):
                    for c in range(4):
                        v = slice(512 * c, 512 * (c + 1))
                        t = stt(dve, X[:, i, v], Y[:, 2 + i, v], ST[:, 10 + i:11 + i], X[:, i, v], ALU.mult, ALU.add,
                                r, yg[2 + i, 3], reload)
                        e, efree = scratch.take()
                        q.append(sums(X[:, i, v], (2 + i, c), E[e][:, 0:512], t, efree))
                        scratch.put(e, q[-1])
                        if c == 1:
                            yield 0
                    xs[i] = load(act, out[128 * i:128 * (i + 1), :], X[:, i, :], spill_sem, t, reload)
                r = yield from inv_rms_steps([2, 3], 14, q)
                xn = [ts(dve, Y[:, 2 + i, :], X[:, i, :], ST[:, 14 + i:15 + i], None, ALU.mult, None, r)
                      for i in range(2)]
                yield from latent_prep(1, lambda i: Y[:, 2 + i, :], xn, 3, y_read)

            h2[1].clear()
            launch("prep", latent_end(), front=True)
            chunk_a(out_stat, tiles[2:], NKT, lambda k: parts[k], [lambda n, o, t: ev(n, o, t, among=tiles[2:])])
            mod_read[0] = [dve.last, pool.last]
            h2[0].clear()
            ctx_read = pe.last

            def context():
                yield "dve"
                ct_tok, xn = ct0, []
                for i in range(2):
                    r, q = (yield from inv_rms_steps([i], 8 + i, [sq[i, c] for c in range(4)])), []
                    for c in range(4):
                        v = slice(512 * c, 512 * (c + 1))
                        t = stt(dve, CT[:, v], Y[:, i, v], ST[:, 8 + i:9 + i], CT[:, v], ALU.mult, ALU.add,
                                r, yg[i, 3], ct_tok)
                        e, efree = scratch.take()
                        q.append(sums(CT[:, v], (i, c), E[e][:, 0:512], t, efree))
                        scratch.put(e, q[-1])
                        yield "dve"
                    r = yield from inv_rms_steps([i], 12 + i, q)
                    t = ts(dve, Y[:, i, :], CT[:, :], ST[:, 12 + i:13 + i], None, ALU.mult, None, r)
                    xn.append(t)
                    if i == 0:
                        ct_tok = load(act, CT[:, :], io["ctx_in"][128:256, :], ct_sem, t, q)
                    yield ct_tok if i == 0 else xn
                yield from latent_prep(0, lambda i: Y[:, i, :], xn, 3, ctx_read)

            return context, xs

        def y_parts(ks, yt_tok, h_read, Yk):
            return {k: split(Hh[:, :, k, :], Hl[:, :, k, :], Yk[:, k], yt_tok[k], h_read) for k in ks}

        def layer3(context, xs):
            cqT, ckT = [W["cqT_h"], W["cqT_l"]], [W["ckT_h"], W["ckT_l"]]
            kr = [W["kr_h"], W["kr_l"]]
            cq, ckv, RT = W["cq"], W["ckv"], W["rope"]
            V, Pm, PT = HU["V"], HU["Pm"], HU["PT"]
            qr = [HU["qr_h"], HU["qr_l"]]
            rope_sem = sem("rope")
            rope_tok = load(sp, RT[:, :], io["rope"], rope_sem, pe.last, dve.last)

            def need_lat(k):
                prepared(h2[1], k)
                return h2[1][k]

            def need_ctx(k):
                prepared(h2[0], k)
                return h2[0][k]

            launch("ctx", context())

            def stat(k, t):
                return [p[:, t[0], k, 128 * t[1]:128 * (t[1] + 1)] for p in (Hh, Hl)]

            def low_rank(dst, sq, done, row):
                def ev(n, o, t):
                    done.append(fn(ACT.Copy, dst[:, n, :], o, t))
                    e, efree = scratch.take()
                    t = sums(o, (n, row), E[e][:, 0:512], t, efree)
                    scratch.put(e, t)
                    sq.append(t)
                    return t
                return ev

            cq_tok, cq_sq, ck_tok, ck_sq = [], [], [], []
            lat = [(1, 0), (1, 1)]
            keys = [(0, 0), (0, 1), (1, 0), (1, 1)]
            chunk_a(stat, lat, NKT, need_lat, [low_rank(cq, cq_sq, cq_tok, 4)])

            def normed(name, src, tok, sq, tiles, col, mul, dst, width, row):
                o = ST[:, col:col + tiles]
                t = cp(dve, o, SS[:, 0:tiles, row], sq)
                t = fn(ACT.Sqrt, o, o, t, bias=K("eps"), scale=1.0 / 512)
                t = recip(o, o, t)
                nt = [ts(dve, src[:, i, :], src[:, i, :], ST[:, col + i:col + i + 1], None, ALU.mult, None, t, tok)
                      for i in range(tiles)]
                yield nt
                per = 512 // width
                for b2 in range(4 // per):
                    b, free = side.take()
                    for j in range(per):
                        k = per * b2 + j
                        for i in range(tiles):
                            tp = tr(ps[:, b, width * j + 128 * i:width * j + 128 * (i + 1)],
                                    src[:, i, 128 * k:128 * (k + 1)], nt, free)
                    n, nfree = og.take()
                    flat_og = OG[n][:, :, :].rearrange("p a b -> p (a b)")
                    for j in range(per):
                        k = per * b2 + j
                        e = fn(ACT.Copy, flat_og[:, width * j:width * (j + 1)], ps[:, b, width * j:width * (j + 1)],
                               tp, nfree, scale=mul(k))
                    side.put(b, e)
                    k = per * b2
                    v = flat_og if per == 1 else OG[n][:, :, :]
                    h, l = (p[:, k, :] if per == 1 else p[:, k:k + 2, :] for p in dst)
                    t = cp(dve, h, v, e, pe.last)
                    t = tt(dve, l, v, h, ALU.subtract, t)
                    og.put(n, t)
                    for j in range(per):
                        done[name, k + j] = t
                    yield nt

            done = {}
            GX = X
            g_tok = {}

            def gate_chunk(c):
                def ev(n, o, t):
                    t = fn(ACT.Silu, GX[:, n, 512 * c:512 * (c + 1)], o, t, xs[0], xs[1])
                    g_tok[c, n] = t
                    return t
                chunk_a(stat, lat, NKT, need_lat, [ev])

            gate_chunk(0)
            gate_chunk(1)
            pump_until(lambda: 15 in h2[0])
            launch("cq", normed("cq", cq, cq_tok, cq_sq, 2, 0, lambda k: P("q_norm", k, k + 1), cqT, 256, 4))
            chunk_a(stat, keys, NKT, lambda k: [need_ctx(k), need_lat(k)], [low_rank(ckv, ck_sq, ck_tok, 5)])
            launch("ckv", normed("ck", ckv, ck_tok, ck_sq, 4, 4, lambda k: P("kv_norm", k, k + 1), ckT, 512, 5))

            def turned(o, t, dst, free):
                s, sfree = scratch.take()
                v = E[s]
                t = cp(act, v[:, 0:256], o, t, sfree)
                bank_free = t
                yield bank_free
                b, bfree = side.take()
                tp = mm(ps[:, b, 0:256], RT[:, 512:640], v[:, 0:256], True, True, t, bfree, rope_tok)
                a = tt(dve, v[:, 256:512], ps[:, b, 0:256], RT[:, 256:512], ALU.mult, tp)
                side.put(b, a)
                c = tt(dve, v[:, 0:256], v[:, 0:256], RT[:, 0:256], ALU.mult, a)
                c = tt(dve, v[:, 0:256], v[:, 0:256], v[:, 256:512], ALU.add, c)
                t = split(dst[0], dst[1], v[:, 0:256], c, free)
                scratch.put(s, t)
                yield t

            kr_tok = {}

            def kr_ev(o, t):
                t1 = split(kr[0][:, 0:256], kr[1][:, 0:256], o[:, 0, :], t)
                kr_tok[0] = t1
                g = turned(o[:, 1, :], t1, [p[:, 256:512] for p in kr], None)
                t2 = next(g)

                def rest():
                    yield t2
                    kr_tok[1] = next(g)
                launch("kr", rest())
                return [t1, t2]

            b_tile(lambda k: [p[:, :, k, :] for p in (Hh, Hl)], lambda b: three(ps[:, b, :], 2),
                   lambda k: [h2[0][k], h2[1][k]], kr_ev)
            gate_chunk(2)
            gate_chunk(3)
            for n in ("cq", "ckv", "kr"):
                finish(n)
            h_read = pe.last

            qn = [[W[f"qn_h{i}"], W[f"qn_l{i}"]] for i in range(2)]
            kn = [[W[f"kn_h{i}"], W[f"kn_l{i}"]] for i in range(2)]
            scores_read = {i: [pe.last, dve.last, act.last] for i in range(2)}
            v_read = {0: [h_read], 1: [h_read]}
            qr_tok, v_tok, qk_tok, o_tok = {}, {}, {}, {}
            def attention(h):
                while p_free[h % 2] is None or not og.free or any(k not in qk_done for k in [h, ("r", h // 2)]):
                    yield 1
                r, o, pr = h % 2, 64 * (h % 2), h // 2 % 4
                P_, pfree, (n, nfree) = PP[r], p_free[r], og.take()
                p_free[r] = None
                yield qk_tok[h], qr_tok[h // 2]
                exps = []
                for i in range(2):
                    b, free = side.take()
                    q, k = [p[:, 128 * i:128 * (i + 1)] for p in qn[r]], [p[:, :] for p in kn[r]]
                    mm3(ps[:, b, :], q, k, True, False, qk_tok[h], free)
                    q, k = [p[o:o + 64, pr, 128 * i:128 * (i + 1)] for p in qr], [p[o:o + 64, :] for p in kr]
                    last = mm3(ps[:, b, :], q, k, False, True, qr_tok[h // 2], list(kr_tok.values()))
                    mx, o_, mn = MX[:, r, 2 * i:2 * i + 1], ps[:, b, :], MX[:, r, 2 * i + 1:2 * i + 2]
                    t = dve.do(lambda e, mx=mx, o_=o_: e.tensor_reduce(mx, o_, AX.X, ALU.max), [last, mx_free[r]], 0.6)
                    t = ts(dve, mn, mx, -MLA_SCALE, None, ALU.mult, None, t)
                    t = fn(ACT.Exp, P_[i], o_, t, pfree, rn_free[r], bias=mn, scale=MLA_SCALE,
                           accum_out=RN[:, r, i:i + 1])
                    side.put(b, t)
                    exps.append(t)
                scores_done.add(h)
                mx_free[r], scores_read[r] = exps[-1], [last]
                rn = recip(RN[:, r, 0:2], RN[:, r, 0:2], exps)
                for i in range(2):
                    g = ts(dve, OG[n][:, 0, 128 * i:128 * (i + 1)], GX[:, i, 128 * h:128 * (h + 1)],
                           RN[:, r, i:i + 1], None, ALU.mult, None, rn, g_tok[h // 4, i], nfree)
                rn_free[r] = [g]
                yield exps
                while places["PT"] is None:
                    yield 1
                pt_free, cps = own("PT"), []
                for i in range(2):
                    b, free = side.take()
                    for kt in range(4):
                        tp = tr(ps[:, b, 128 * kt:128 * (kt + 1)], P_[i][:, 128 * kt:128 * (kt + 1)], exps, free)
                    cps.append(cp((act, dve)[i], PT[:, :, 128 * i:128 * (i + 1)], three(ps[:, b, :], 4), tp, pt_free))
                    side.put(b, cps[-1])
                p_free[r] = [tp]
                b, free = side.take()
                for i in range(2):
                    tp = tr(ps[:, b, 128 * i:128 * (i + 1)], OG[n][:, 0, 128 * i:128 * (i + 1)], g, free)
                g = cp(act, OG[n][:, 1, :], ps[:, b, 0:256], tp)
                side.put(b, g)
                yield cps, v_tok[h // 4]
                b, free = side.take()
                for kt in range(4):
                    tp = mm(ps[:, b, 0:256], V[:, h // 4 % 2, kt, 128 * (h % 4):128 * (h % 4 + 1)], PT[:, kt, :],
                            kt == 0, kt == 3, cps, v_tok[h // 4], free)
                give("PT", tp)
                v_read[h // 4 % 2] = [tp]
                values_done.add(h)
                t = tt(dve, OG[n][:, 0, :], ps[:, b, 0:256], OG[n][:, 1, :], ALU.mult, tp, g)
                side.put(b, t)
                t = split(Hh[:, 0, h, :], Hl[:, 0, h, :], OG[n][:, 0, :], t, h_read)
                og.put(n, t)
                o_tok[h] = t

            mx_free, rn_free = {0: None, 1: None}, {0: None, 1: None}
            scores_done, values_done, qk_done = set(), set(), set()
            e2, e3 = [p for p in scratch.free if p[0] >= 2]
            scratch.free = [p for p in scratch.free if p[0] < 2]
            PP = [[Pm[:, 0, :], Pm[:, 1, :]], [E[2][:, 0:512], E[3][:, 0:512]]]
            p_free = [[h_read], [e2[1], e3[1]]]
            places["PT"] = [h_read]
            assert (3, 4) in mod_ready
            side.put(7, ada["bank"])

            def q_bank(b):
                return ps[:, b, 0:256]

            def q_stat(k):
                return [p[:, k, :] for p in cqT]

            def q_need(k):
                return done["cq", k]

            def k_stat(k):
                return [p[:, k, :] for p in ckT]

            def k_need(k):
                return done["ck", k]

            for g in range(4):
                pump_until(lambda: g < 2 or 4 * g - 5 in values_done)

                def v_ev(n, o, t, g=g):
                    t = fn(ACT.Copy, V[:, g % 2, n, :], o, t, v_read[g % 2])
                    v_tok.setdefault(g, []).append(t)
                    return t

                chunk_a(lambda k, t: [p[:, k, 256 * t[0] + 128 * t[1]:256 * t[0] + 128 * (t[1] + 1)] for p in ckT],
                        keys, 4, k_need, [v_ev])
                if g % 2 == 0:
                    pump_until(lambda: g == 0 or 4 * g - 1 in scores_done)
                    qr_read = [pe.last]
                    for half in range(2):
                        jobs = []
                        for i in (2 * half, 2 * half + 1):
                            def ev(o, t, i=i, g=g):
                                pump_until(lambda: scratch.free)
                                gen = turned(o, t, [p[:, i, :] for p in qr], qr_read)
                                copied = next(gen)

                                def rest():
                                    yield copied
                                    qr_tok[2 * g + i] = next(gen)
                                    qk_done.add(("r", 2 * g + i))
                                launch("rope", rest(), front=True)
                                return copied
                            jobs.append((q_stat, q_bank, q_need, ev))
                        b_half(jobs)
                for j in range(4):
                    h = 4 * g + j
                    pump_until(lambda: h < 2 or h - 2 in scores_done)
                    launch("head", attention(h))

                    def part_ev(dst, h=h):
                        def ev(o, t):
                            t = split(dst[0][:, :], dst[1][:, :], o, t, scores_read[h % 2])
                            qk_tok.setdefault(h, []).append(t)
                            return t
                        return ev
                    b_half([(q_stat, q_bank, q_need, part_ev(qn[h % 2])),
                            (k_stat, lambda b: ps[:, b, :], k_need, part_ev(kn[h % 2]))])
                    qk_done.add(h)
                    pump()

            def need_o(k):
                pump_until(lambda: k in o_tok)
                if k == 15 and len(scratch.free) == 2:
                    scratch.free += [(2, p_free[1]), (3, p_free[1])]
                return o_tok[k]

            Y = W["Y2"]
            M = MOD[1]
            GBs = [GB1, W["GB0"]]
            gb_read, sq, yg = {0: [dve.last], 1: [dve.last, pe.last]}, {}, {}

            def out_chunk(c):
                gb, b = {}, c % 2

                def hook(_):
                    gb["g"] = spread(GBs[b][:, :], gates[3, c, 0], gb_sems[b], gb_read[b], mod_ready[3, 4])

                def ev(n, o, t):
                    e, efree = scratch.take()
                    t = sums(o, (n, c), E[e][:, 0:512], t, efree)
                    scratch.put(e, t)
                    sq[n, c] = t
                    t = tt(dve, Y[:, n, 512 * c:512 * (c + 1)], o, GBs[b][:, :], ALU.mult, t, gb["g"])
                    gb_read[b] = [t]
                    yg[n, c] = t
                    return t
                return ev, hook

            def o_stat(k, t):
                return [p[:, 0, k, 128 * t[1]:128 * (t[1] + 1)] for p in (Hh, Hl)]

            (ev0, hook0), (ev1, hook1) = out_chunk(0), out_chunk(1)
            chunk_a(o_stat, lat, NKT, need_o, [ev0, ev1], {(0, 2): hook0, (1, 2): hook1})
            for i in range(2):
                reload = load(sp, X[:, i, :], out[128 * i:128 * (i + 1), :], reload_sem, dve.last, xs[0], xs[1])
            for c in (2, 3):
                ev, hook = out_chunk(c)
                chunk_a(o_stat, lat, NKT, need_o, [ev], {(0, 2): hook})
            for i in range(2):
                r = inv_rms([i], 4, D, 8 + i, [sq[i, c] for c in range(4)])
                t = stt(dve, X[:, i, :], Y[:, i, :], ST[:, 8 + i:9 + i], X[:, i, :], ALU.mult, ALU.add, r, yg[i, 3], reload)
                o_done = load(sp, out[128 * i:128 * (i + 1), :], X[:, i, :], spill_sem, t)
            sp.do(lambda e: None, [o_done])

        x_sums = []
        for i in range(2):
            for c in range(4):
                n, free = scratch.take()
                x_sums.append(sums(X[:, i, 512 * c:512 * (c + 1)], (i, c), E[n][:, 0:512], x_tok, free))
                scratch.put(n, x_sums[-1])
        x_tok = x_sums
        x_tok = layer1(0, x_tok)
        x_tok = layer1(1, x_tok)
        context, xs = layer2(x_tok)
        layer3(context, xs)
        for q in (pe, act, dve, pool, sp):
            q.number()
        block = ctx.enter_context(nc.Block())

        @block.sync
        def _(e):
            sp.play(e)

        @block.scalar
        def _(e):
            act.play(e)

        @block.tensor
        def _(e):
            pe.play(e)

        @block.vector
        def _(e):
            dve.play(e)

        @block.gpsimd
        def _(e):
            pool.play(e)


def kernel(**inputs):
    import concourse.bacc as _bacc
    from concourse.bass_utils import run_bass_kernel_spmd as _run

    arrays = lay_out({n: np.asarray(a) for n, a in inputs.items()})
    nc = _bacc.Bacc("TRN2", target_bir_lowering=False, num_devices=1)
    io = {n: nc.dram_tensor("in_" + n, a.shape, mybir.dt.from_np(a.dtype), kind="ExternalInput").ap()
          for n, a in arrays.items()}
    out = nc.dram_tensor("out_x", (256, 2048), F, kind="ExternalOutput").ap()
    program(nc, io, out)
    r = _run(nc, [{"in_" + n: a for n, a in arrays.items()}], core_ids=[0])
    return r.results[0]["out_x"].reshape(1, 256, 2048)
```
